# Optimizing a Trainium2 kernel written in Bass

```python
import jax, jax.numpy as jnp
from jax import lax
import numpy as np

D_MODEL = 1024
BATCH = 1
SEQ = 1024
DEPTH = 1

CHUNK = 64
EPS = 1e-6

A_HEADS = 8
A_WIDTH = D_MODEL // 2
A_HEAD_DIM = A_WIDTH // A_HEADS
A_LEFT_CHUNKS = 8
A_BAND = (A_LEFT_CHUNKS + 1) * CHUNK
REL_CLIP = 2 * CHUNK

B_HEADS = 4
B_V_WIDTH = D_MODEL // 2
B_QK_WIDTH = B_V_WIDTH // 2
B_KEY_DIM = B_QK_WIDTH // B_HEADS
B_VAL_DIM = B_V_WIDTH // B_HEADS
B_GATE_RANK = 16
B_GATE_TEMP = 16.0

N_BRANCH = 2
IN_SPLIT = (A_WIDTH, A_WIDTH, A_WIDTH,
            B_QK_WIDTH, B_QK_WIDTH, B_V_WIDTH,
            B_V_WIDTH, B_GATE_RANK,
            N_BRANCH * D_MODEL)
IN_COLS = sum(IN_SPLIT)
SPLIT_POINTS = tuple(sum(IN_SPLIT[:i + 1]) for i in range(len(IN_SPLIT) - 1))

N_GROUPS = 4
EXPERTS_PER_GROUP = 8
N_EXPERTS = N_GROUPS * EXPERTS_PER_GROUP
TOP_K = 2
D_EXPERT = D_MODEL // 4

kernel_name = "hybrid_chunkattn_gla_hiermoe"

def rms_norm(x, gain):
    xf = x.astype(jnp.float32)
    y = xf * lax.rsqrt(jnp.mean(xf * xf, axis=-1, keepdims=True) + EPS)
    return (y * gain.astype(jnp.float32)).astype(x.dtype)

def chunk_band_attention(q, k, v, q_gain, k_gain, rel_bias):
    b_, s_, h_, dh = q.shape
    nc = s_ // CHUNK
    pad = A_LEFT_CHUNKS * CHUNK
    q = rms_norm(q, q_gain) * (dh ** -0.5)
    k = rms_norm(k, k_gain)
    k_pad = jnp.pad(k, ((0, 0), (pad, 0), (0, 0), (0, 0)))
    v_pad = jnp.pad(v, ((0, 0), (pad, 0), (0, 0), (0, 0)))
    q_pos = jnp.arange(CHUNK)[:, None] + pad
    k_pos = jnp.arange(A_BAND)[None, :]
    rel = jnp.clip(q_pos - k_pos, -REL_CLIP, REL_CLIP) + REL_CLIP
    bias = jnp.transpose(rel_bias[rel], (2, 0, 1)).astype(jnp.float32)
    q_chunks = jnp.transpose(q.reshape(b_, nc, CHUNK, h_, dh), (1, 0, 2, 3, 4))

    def one_chunk(args):
        c, q_c = args
        start = c * CHUNK
        k_band = lax.dynamic_slice_in_dim(k_pad, start, A_BAND, axis=1)
        v_band = lax.dynamic_slice_in_dim(v_pad, start, A_BAND, axis=1)
        s = jnp.einsum('bqhd,bkhd->bhqk', q_c, k_band).astype(jnp.float32) + bias
        valid = (start + jnp.arange(A_BAND)) >= pad
        s = jnp.where(valid[None, None, None, :], s, -jnp.inf)
        p = jax.nn.softmax(s, axis=-1).astype(v.dtype)
        return jnp.einsum('bhqk,bkhd->bqhd', p, v_band)

    out = lax.map(one_chunk, (jnp.arange(nc), q_chunks))
    return jnp.transpose(out, (1, 0, 2, 3, 4)).reshape(b_, s_, h_ * dh)

def gla_chunked(q, k, v, log_a):
    b_, s_, h_, dk = q.shape
    dv = v.shape[-1]
    nc = s_ // CHUNK
    out_dtype = v.dtype

    def to_chunks(t):
        t = t.astype(jnp.float32).reshape(b_, nc, CHUNK, h_, t.shape[-1])
        return jnp.transpose(t, (1, 0, 3, 2, 4))

    qc = to_chunks(q) * (dk ** -0.5)
    kc, vc, gc = to_chunks(k), to_chunks(v), to_chunks(log_a)
    causal = jnp.tril(jnp.ones((CHUNK, CHUNK), dtype=bool))

    def step(state, inp):
        q_c, k_c, v_c, g_c = inp
        b = jnp.cumsum(g_c, axis=2)
        o_inter = jnp.einsum('bhck,bhkv->bhcv', q_c * jnp.exp(b), state)
        diff = b[:, :, :, None, :] - b[:, :, None, :, :]
        decay = jnp.exp(jnp.where(causal[:, :, None], diff, -jnp.inf))
        attn = jnp.einsum('bhik,bhjk,bhijk->bhij', q_c, k_c, decay)
        o_intra = jnp.einsum('bhij,bhjv->bhiv', attn, v_c)
        b_last = b[:, :, -1:, :]
        new_state = (jnp.exp(b_last[:, :, 0, :])[..., None] * state
                     + jnp.einsum('bhck,bhcv->bhkv', k_c * jnp.exp(b_last - b), v_c))
        return new_state, o_inter + o_intra

    state0 = jnp.zeros((b_, h_, dk, dv), jnp.float32)
    _, o = lax.scan(step, state0, (qc, kc, vc, gc))
    o = jnp.transpose(o, (1, 0, 3, 2, 4)).reshape(b_, s_, h_, dv)
    return o.astype(out_dtype)

def hier_moe(h, w_group, b_group, w_router, b_router, w_gate, w_up, w_down):
    shape = h.shape
    hf = h.reshape(-1, shape[-1])
    t_ = hf.shape[0]
    g_prob = jax.nn.softmax((hf @ w_group).astype(jnp.float32) + b_group, axis=-1)
    g_top, g_idx = lax.top_k(g_prob, 1)
    e_logits = ((hf @ w_router).astype(jnp.float32) + b_router).reshape(t_, N_GROUPS, EXPERTS_PER_GROUP)
    e_in_group = jnp.take_along_axis(e_logits, g_idx[:, :, None], axis=1)[:, 0]
    e_top, e_idx = lax.top_k(e_in_group, TOP_K)
    e_w = jax.nn.softmax(e_top, axis=-1) * g_top
    expert_id = g_idx * EXPERTS_PER_GROUP + e_idx
    gates = jnp.sum(jax.nn.one_hot(expert_id, N_EXPERTS, dtype=jnp.float32) * e_w[..., None], axis=1)
    gates = gates.astype(h.dtype)
    y = jnp.zeros_like(hf)
    for e in range(N_EXPERTS):
        a = jax.nn.silu(hf @ w_gate[e]) * (hf @ w_up[e])
        y = y + gates[:, e:e + 1] * (a @ w_down[e])
    return y.reshape(shape)

def setup_inputs(seed: int = 0) -> dict:
    key = jax.random.key(seed)
    ks = jax.random.split(key, 20)
    f32 = jnp.float32

    def nrm(k, shape, scale):
        return jax.random.normal(k, shape, f32) * scale

    return {
        "x": nrm(ks[0], (BATCH, SEQ, D_MODEL), 1.0),
        "norm_mix_gain": 1.0 + nrm(ks[1], (DEPTH, D_MODEL), 0.02),
        "w_in": nrm(ks[2], (DEPTH, D_MODEL, IN_COLS), D_MODEL ** -0.5),
        "a_q_gain": 1.0 + nrm(ks[3], (DEPTH, A_HEADS, A_HEAD_DIM), 0.02),
        "a_k_gain": 1.0 + nrm(ks[4], (DEPTH, A_HEADS, A_HEAD_DIM), 0.02),
        "rel_bias": nrm(ks[5], (2 * REL_CLIP + 1, A_HEADS), 0.2),
        "b_gate_up": nrm(ks[6], (DEPTH, B_GATE_RANK, B_QK_WIDTH), B_GATE_RANK ** -0.5),
        "b_gate_bias": nrm(ks[7], (DEPTH, B_QK_WIDTH), 0.1),
        "b_out_gain": 1.0 + nrm(ks[8], (DEPTH, B_HEADS, B_VAL_DIM), 0.02),
        "proj_a": nrm(ks[9], (DEPTH, A_WIDTH, D_MODEL), A_WIDTH ** -0.5),
        "proj_b": nrm(ks[10], (DEPTH, B_V_WIDTH, D_MODEL), B_V_WIDTH ** -0.5),
        "w_out": nrm(ks[11], (DEPTH, D_MODEL, D_MODEL), D_MODEL ** -0.5),
        "norm_ffn_gain": 1.0 + nrm(ks[12], (DEPTH, D_MODEL), 0.02),
        "w_group": nrm(ks[13], (DEPTH, D_MODEL, N_GROUPS), D_MODEL ** -0.5),
        "b_group": nrm(ks[14], (DEPTH, N_GROUPS), 0.01),
        "w_router": nrm(ks[15], (DEPTH, D_MODEL, N_EXPERTS), D_MODEL ** -0.5),
        "b_router": nrm(ks[16], (DEPTH, N_EXPERTS), 0.01),
        "w_gate": nrm(ks[17], (DEPTH, N_EXPERTS, D_MODEL, D_EXPERT), D_MODEL ** -0.5),
        "w_up": nrm(ks[18], (DEPTH, N_EXPERTS, D_MODEL, D_EXPERT), D_MODEL ** -0.5),
        "w_down": nrm(ks[19], (DEPTH, N_EXPERTS, D_EXPERT, D_MODEL), D_EXPERT ** -0.5),
    }

def reference(x, norm_mix_gain, w_in, a_q_gain, a_k_gain, rel_bias, b_gate_up, b_gate_bias,
              b_out_gain, proj_a, proj_b, w_out, norm_ffn_gain, w_group, b_group, w_router,
              b_router, w_gate, w_up, w_down):
    b_, s_, _ = x.shape
    for l in range(DEPTH):
        h = rms_norm(x, norm_mix_gain[l])
        u = h @ w_in[l]
        a_q, a_k, a_v, b_q, b_k, b_v, b_r, b_lr, gate_cols = jnp.split(u, SPLIT_POINTS, axis=-1)

        y_a = chunk_band_attention(a_q.reshape(b_, s_, A_HEADS, A_HEAD_DIM),
                                   a_k.reshape(b_, s_, A_HEADS, A_HEAD_DIM),
                                   a_v.reshape(b_, s_, A_HEADS, A_HEAD_DIM),
                                   a_q_gain[l], a_k_gain[l], rel_bias)

        log_a = jax.nn.log_sigmoid((b_lr @ b_gate_up[l]).astype(jnp.float32)
                                   + b_gate_bias[l].astype(jnp.float32)) / B_GATE_TEMP
        o_b = gla_chunked(b_q.reshape(b_, s_, B_HEADS, B_KEY_DIM),
                          b_k.reshape(b_, s_, B_HEADS, B_KEY_DIM),
                          b_v.reshape(b_, s_, B_HEADS, B_VAL_DIM),
                          log_a.reshape(b_, s_, B_HEADS, B_KEY_DIM))
        y_b = rms_norm(o_b, b_out_gain[l]).reshape(b_, s_, B_V_WIDTH) * jax.nn.silu(b_r)

        g_a, g_b = jnp.split(jax.nn.sigmoid(gate_cols), N_BRANCH, axis=-1)
        merged = g_a * (y_a @ proj_a[l]) + g_b * (y_b @ proj_b[l])
        x = x + merged @ w_out[l]

        h = rms_norm(x, norm_ffn_gain[l])
        x = x + hier_moe(h, w_group[l], b_group[l], w_router[l], b_router[l],
                         w_gate[l], w_up[l], w_down[l])
    return x


_drawn_inputs = setup_inputs


def setup_inputs(seed=0):
    import zlib

    import numpy as np

    out = dict(_drawn_inputs(seed))
    spreads = {}
    factors = {'a_q_gain': 8.0,
     'a_k_gain': 7.702,
     'rel_bias': 3.043,
     'b_out_gain': 3.476,
     'b_group': 11.924,
     'b_router': 3.285}
    for name, (base, spread) in spreads.items():
        noise = np.random.default_rng([zlib.crc32(name.encode()), seed]).standard_normal(out[name].shape)
        drawn = base * np.exp(spread * noise) if base else spread * noise
        out[name] = __import__('jax').numpy.asarray(drawn.astype(out[name].dtype))
    for name, factor in factors.items():
        out[name] = (out[name] * factor).astype(out[name].dtype)
    return out
```

```python
from contextlib import ExitStack

import concourse.bass as bass
from concourse import mybir

ALU = mybir.AluOpType
ACT = mybir.ActivationFunctionType
AX = mybir.AxisListType
F32 = mybir.dt.float32
I32 = mybir.dt.int32
U32 = mybir.dt.uint32

P = 128
D = 1024
SEQ = 1024
T = SEQ // P
KD = D // P
EPS = 1e-6
CHUNK = 64
LEFT = 8
HALF = 512
A_W, A_H, A_D = 512, 8, 64
A_PAIRS = A_H // 2
BAND_T = LEFT * CHUNK // P + 1
BANDW = BAND_T * P
B_V, B_QK, B_H, B_DK, B_DV, RANK = 512, 256, 4, 64, 128, 16
B_PAIRS = B_H // 2
GATE_TEMP = 16.0
LEVELS = 8
NG, EPG, NE = 4, 8, 32
DE = 256
MAX_OVER = 2 * SEQ // P
TILES = NE + MAX_OVER
NEG = -1e30


class Chain:

    def __init__(self, eng, sem, before=0):
        self.eng, self.sem, self.before, self.n = eng, sem, before, 0

    def __call__(self, ins):
        self.n += 1
        ins.then_inc(self.sem, 1)
        self.eng.wait_ge(self.sem, self.before + self.n)


def layer_kernel(nc, x, g1, wv, wqk, wlr, wd, wout, qg, kg, bog, gup, gbias, relx, g2p, wr, br,
                 w_gate, w_up, w_down, out, h2_dram, y_dram):
    x_t = x.rearrange("(t p) d -> t p d", p=P)
    out_t = out.rearrange("(t p) d -> t p d", p=P)
    h2_t = h2_dram.rearrange("(t p) d -> t p d", p=P)
    y_t = y_dram.rearrange("(t p) d -> t p d", p=P)
    wg_e = w_gate.rearrange("e (p k) f -> e p k f", p=P)
    wu_e = w_up.rearrange("e (p k) f -> e p k f", p=P)
    wn_e = w_down.rearrange("e (p c) n -> e p (c n)", p=P)

    with ExitStack() as top:
        def sem(name):
            return top.enter_context(nc.semaphore(name))

        def sb(name, shape, dt=F32, ctx=top):
            return ctx.enter_context(nc.sbuf_tensor(name, shape, dt))

        ps = top.enter_context(nc.psum_tensor("ps", [P, 8, HALF], F32))
        ticks = sem("ticks")

        def apart(eng):
            eng.sem_inc(ticks, 1)

        ident = sb("ident", [P, P])
        ones = sb("ones", [P, P])
        head_mean = sb("head_mean", [P, P])
        tri16 = sb("tri16", [P, P])
        before = sb("before", [P, P])
        load_small = sem("load_small")
        g1_sb = sb("g1_sb", [P, KD])
        qg_sb = sb("qg_sb", [P, A_PAIRS])
        kg_sb = sb("kg_sb", [P, A_PAIRS])
        bog_sb = sb("bog_sb", [P, B_H])
        lgt = sb("lgt", [P, T, NG + NE])
        eps_sb = sb("eps_sb", [P, 1])
        c_pool = sem("c_pool")
        c_dve = sem("c_dve")
        w_v_in = sem("w_v_in")

        yaT = sb("yaT", [P, A_W // P, SEQ])
        ybT = sb("ybT", [P, B_V // P, SEQ])
        hT = sb("hT", [P, KD, SEQ])

        mid = ExitStack()
        va = sb("va", [P, T, A_W], ctx=mid)
        vb = sb("vb", [P, T, B_V], ctx=mid)
        rs = sb("rs", [P, T, B_V], ctx=mid)

        with ExitStack() as st:
            wv_sb = sb("wv_sb", [P, KD, 3 * HALF], ctx=st)
            xin = [sb(f"xin{u}", [P, D], ctx=st) for u in range(2)]
            hn = [sb(f"hn{u}", [P, D], ctx=st) for u in range(2)]
            hst = [sb(f"hst{u}", [P, KD, P], ctx=st) for u in range(2)]
            junk = sb("junk_a", [P, D], ctx=st)
            msq = sb("msq", [P, 2], ctx=st)
            rstd = sb("rstd", [P, 2], ctx=st)
            sg = [sb(f"sg{u}", [P, HALF], ctx=st) for u in range(2)]
            x_in = [sem(f"x_in{u}") for u in range(2)]
            msq_ready = sem("msq_ready")
            rms_ready = sem("rms_ready")
            rstd_ready = sem("rstd_ready")
            hn_ready = sem("hn_ready")
            hT_psum = sem("hT_psum")
            hst_ready = sem("hst_ready")
            hT_copied = sem("hT_copied")
            v_psum = sem("v_psum")
            va_done = sem("va_done")
            vb_done = sem("vb_done")
            rs_done = sem("rs_done")
            sg_ready = sem("sg_ready")
            psT = [ps[:, 0:2, :].rearrange("p b c -> p (b c)"), ps[:, 2:4, :].rearrange("p b c -> p (b c)")]

            with nc.Block() as block:
                @block.sync
                def _(sp):
                    for dst, src in ((g1_sb, g1), (qg_sb, qg), (kg_sb, kg), (bog_sb, bog)):
                        sp.dma_start(dst[:], src).then_inc(load_small, 16)
                    with sp.Fori(0, T // 2) as i:
                        for u in range(2):
                            sp.wait_ge(hn_ready, i * 2 + u + 1)
                            sp.dma_start(xin[u][:], x_t[i * 2 + u]).then_inc(x_in[u], 16)

                @block.scalar
                def _(act):
                    act.dma_start(wv_sb[:], wv).then_inc(w_v_in, 16)
                    act.sem_inc(va_done, 1)
                    act.sem_inc(vb_done, 1)
                    act.wait_ge(c_pool, 10)
                    with act.Fori(0, T // 2) as i:
                        for u in range(2):
                            act.wait_ge(x_in[u], i * 16 + 16)
                            act.wait_ge(hn_ready, i * 2 + u + 1)
                            nc.scalar.activation(junk[:], xin[u][:], ACT.Square, scale=D ** -0.5,
                                                 accum_out=msq[:, u:u + 1]).then_inc(msq_ready, 1)
                            act.wait_ge(msq_ready, i * 2 + u + 1)
                            nc.scalar.activation(msq[:, u:u + 1], msq[:, u:u + 1], ACT.Sqrt,
                                                 bias=eps_sb[:]).then_inc(rms_ready, 1)
                        for u in range(2):
                            t = i * 2 + u
                            act.wait_ge(v_psum, t * 3 + 1)
                            nc.scalar.copy(va[:, t, :], ps[:, 4, :]).then_inc(va_done, 1)
                            act.wait_ge(v_psum, t * 3 + 2)
                            nc.scalar.copy(vb[:, t, :], ps[:, 5, :]).then_inc(vb_done, 1)
                            act.wait_ge(v_psum, t * 3 + 3)
                            nc.scalar.activation(sg[u][:], ps[:, 6, :], ACT.Sigmoid).then_inc(sg_ready, 1)

                @block.gpsimd
                def _(pool):
                    pool.sem_inc(hT_copied, 2)
                    link = Chain(pool, c_pool)
                    link(nc.gpsimd.memset(ident[:], 0.0))
                    link(nc.gpsimd.affine_select(out=ident[:], in_=ident[:], compare_op=ALU.not_equal, fill=1.0,
                                                 base=0, pattern=[[-1, P]], channel_multiplier=1))
                    link(nc.gpsimd.memset(ones[:], 1.0))
                    link(nc.gpsimd.memset(eps_sb[:], EPS))
                    link(nc.gpsimd.memset(head_mean[:], 0.0))
                    for h in range(2):
                        link(nc.gpsimd.memset(head_mean[h * A_D:(h + 1) * A_D, h * A_D:(h + 1) * A_D], 1.0 / A_D))
                    link(nc.gpsimd.memset(tri16[:], 1.0 / GATE_TEMP))
                    link(nc.gpsimd.affine_select(out=tri16[:], in_=tri16[:], compare_op=ALU.is_ge, fill=0.0,
                                                 base=0, pattern=[[1, P]], channel_multiplier=-1))
                    link(nc.gpsimd.affine_select(out=before[:], in_=ones[:], compare_op=ALU.is_gt, fill=0.0,
                                                 base=0, pattern=[[1, P]], channel_multiplier=-1))
                    with pool.Fori(0, T // 2) as i:
                        for u in range(2):
                            t = i * 2 + u
                            pool.wait_ge(hst_ready, t + 3)
                            nc.gpsimd.tensor_copy(hT[:, :, bass.ds(t * P, P)], hst[u][:]).then_inc(hT_copied, 1)

                @block.vector
                def _(dve):
                    dve.sem_inc(hn_ready, 2)
                    dve.sem_inc(hst_ready, 2)
                    dve.sem_inc(rs_done, 1)
                    dve.wait_ge(load_small, 64)
                    with dve.Fori(0, T // 2) as i:
                        for u in range(2):
                            t = i * 2 + u
                            dve.wait_ge(rms_ready, t + 1)
                            nc.vector.reciprocal(rstd[:, u:u + 1], msq[:, u:u + 1]).then_inc(rstd_ready, 1)
                            dve.wait_ge(rstd_ready, t + 1)
                            dve.wait_ge(hst_ready, t + 1)
                            nc.vector.tensor_scalar(hn[u][:], xin[u][:], rstd[:, u:u + 1], None,
                                                    ALU.mult).then_inc(hn_ready, 1)
                        for u in range(2):
                            t = i * 2 + u
                            dve.wait_ge(hT_psum, t + 1)
                            dve.wait_ge(hT_copied, t + 1)
                            nc.vector.tensor_tensor(hst[u][:], psT[u].rearrange("p (k c) -> p k c", k=KD),
                                                    g1_sb[:].unsqueeze(2).broadcast_to([P, KD, P]),
                                                    ALU.mult).then_inc(hst_ready, 1)
                        for u in range(2):
                            t = i * 2 + u
                            dve.wait_ge(sg_ready, t + 1)
                            nc.vector.tensor_tensor(rs[:, t, :], ps[:, 6, :], sg[u][:], ALU.mult).then_inc(rs_done, 1)

                @block.tensor
                def _(pe):
                    pe.wait_ge(c_pool, 10)
                    with pe.Fori(0, T // 2) as i:
                        for u in range(2):
                            t = i * 2 + u
                            pe.wait_ge(hn_ready, t + 3)
                            for k in range(KD):
                                mm = pe.transpose(psT[u][:, k * P:(k + 1) * P], hn[u][:, k * P:(k + 1) * P], ident[:])
                            mm.then_inc(hT_psum, 1)
                        for u in range(2):
                            t = i * 2 + u
                            pe.wait_ge(hst_ready, t + 3)
                            pe.wait_ge(w_v_in, 16)
                            for g, freed in enumerate((va_done, vb_done, rs_done)):
                                pe.wait_ge(freed, t + 1)
                                for k in range(KD):
                                    mm = pe.matmul(ps[:, 4 + g, :], hst[u][:, k, :],
                                                   wv_sb[:, k, g * HALF:(g + 1) * HALF],
                                                   start=(k == 0), stop=(k == KD - 1))
                                mm.then_inc(v_psum, 1)

        UN = 2 * T
        with ExitStack() as st:
            w_sb = sb("w_sb", [P, KD, 2 * P], ctx=st)
            qn = sb("qn", [P, SEQ], ctx=st)
            kn = sb("kn", [P, SEQ], ctx=st)
            sq = [sb(f"sq{u}", [P, SEQ], ctx=st) for u in range(2)]
            inv = sb("inv", [P, SEQ], ctx=st)
            bias = sb("bias", [P, 2, BANDW], ctx=st)
            ng = [sb(f"ng{u}", [P, BANDW], ctx=st) for u in range(2)]
            pr = [sb(f"pr{u}", [P, BANDW], ctx=st) for u in range(2)]
            prT = [sb(f"prT{u}", [P, BANDW], ctx=st) for u in range(2)]
            nmax = sb("nmax", [P, 2], ctx=st)
            rsum = sb("rsum", [P, 2], ctx=st)
            rinv = sb("rinv", [P, 2], ctx=st)
            ya = [sb(f"ya{u}", [P, P], ctx=st) for u in range(2)]
            zeros = sb("zeros", [P, D], ctx=st)
            zeros_ready = sem("zeros_ready")
            rows_cleared = sem("rows_cleared")
            w_in = sem("a_w_in")
            bias_in = sem("bias_in")
            qk_psum = sem("qk_psum")
            sq_ready = sem("sq_ready")
            ms_psum = sem("ms_psum")
            band_dve = sem("band_dve")
            rms_ready = sem("head_rms_ready")
            norm_done = sem("norm_done")
            score_psum = sem("score_psum")
            neg_ready = sem("neg_ready")
            prob_ready = sem("prob_ready")
            probT_psum = sem("probT_psum")
            probT_ready = sem("probT_ready")
            pv_psum = sem("pv_psum")
            ya_ready = sem("ya_ready")
            yaT_psum = sem("yaT_psum")
            yaT_done = sem("yaT_done")

            def keys(t):
                n = min(t + 1, BAND_T)
                return t + 1 - n, n

            q_ps = ps[:, 0:2, :].rearrange("p b c -> p (b c)")
            k_ps = ps[:, 2:4, :].rearrange("p b c -> p (b c)")
            s_ps = [q_ps, k_ps]
            tr_ps = ps[:, 4:6, :].rearrange("p b c -> p (b c)")
            ms_ps = [tr_ps, ps[:, 6:8, :].rearrange("p b c -> p (b c)")]

            with nc.Block() as block:
                @block.gpsimd
                def _(pool):
                    nc.gpsimd.memset(zeros[:], 0.0).then_inc(zeros_ready, 1)

                @block.sync
                def _(sp):
                    sp.wait_ge(zeros_ready, 1)
                    with sp.Fori(NE, TILES) as o:
                        sp.dma_start(y_t[o], zeros[:]).then_inc(rows_cleared, 16)
                    with sp.Fori(0, A_PAIRS) as p:
                        sp.wait_ge(qk_psum, p * 2 + 2)
                        sp.dma_start(w_sb[:], wqk[p]).then_inc(w_in, 16)
                        sp.wait_ge(neg_ready, p * UN + 2)
                        sp.dma_start(bias[:], relx[p]).then_inc(bias_in, 16)
                    sp.wait_ge(rows_cleared, 16 * MAX_OVER)

                @block.tensor
                def _(pe):
                    pe.sem_inc(qk_psum, 2)
                    pe.sem_inc(probT_psum, 2)
                    pe.sem_inc(pv_psum, 2)
                    pe.sem_inc(yaT_psum, 2)
                    with pe.Fori(0, A_PAIRS) as p:
                        n0 = p * UN
                        pe.wait_ge(w_in, p * 16 + 16)
                        pe.wait_ge(neg_ready, n0 + 2)
                        for b in range(2):
                            for half in range(2):
                                for k in range(KD):
                                    mm = pe.matmul(ps[:, 2 * b + half, :], w_sb[:, k, b * P:(b + 1) * P],
                                                   hT[:, k, half * HALF:(half + 1) * HALF],
                                                   start=(k == 0), stop=(k == KD - 1))
                            mm.then_inc(qk_psum, 1)
                        pe.wait_ge(probT_ready, n0 + 1)
                        pe.wait_ge(ya_ready, n0 + 2)
                        pe.wait_ge(yaT_done, p * T + 2)
                        for b in range(2):
                            pe.wait_ge(sq_ready, p * 2 + b + 1)
                            for half in range(2):
                                mm = pe.matmul(ms_ps[b][:, half * HALF:(half + 1) * HALF], head_mean[:],
                                               sq[b][:, half * HALF:(half + 1) * HALF], start=True, stop=True)
                            mm.then_inc(ms_psum, 1)
                        pe.wait_ge(norm_done, p * 2 + 2)
                        for s in range(UN + 4):
                            if s < UN:
                                t, h = s // 2, s % 2
                                k0, nk = keys(t)
                                hd = slice(h * A_D, (h + 1) * A_D)
                                pe.wait_ge(neg_ready, n0 + s + 1)
                                for c in range(0, nk * P, HALF):
                                    w = min(HALF, nk * P - c)
                                    mm = pe.matmul(s_ps[s % 2][:, c:c + w], qn[hd, t * P:(t + 1) * P],
                                                   kn[hd, k0 * P + c:k0 * P + c + w], start=True, stop=True)
                                mm.then_inc(score_psum, 1)
                            if 0 <= s - 1 < UN:
                                m = s - 1
                                k0, nk = keys(m // 2)
                                pe.wait_ge(prob_ready, n0 + m + 3)
                                pe.wait_ge(probT_ready, n0 + m + 1)
                                for j in range(nk):
                                    mm = pe.transpose(tr_ps[:, j * P:(j + 1) * P], pr[m % 2][:, j * P:(j + 1) * P],
                                                      ident[:])
                                mm.then_inc(probT_psum, 1)
                            if 0 <= s - 2 < UN:
                                m = s - 2
                                t, h = m // 2, m % 2
                                k0, nk = keys(t)
                                pe.wait_ge(probT_ready, n0 + m + 2)
                                pe.wait_ge(ya_ready, n0 + m + 2)
                                for j in range(nk):
                                    mm = pe.matmul(ps[:, 6, h * A_D:(h + 1) * A_D], prT[m % 2][:, j * P:(j + 1) * P],
                                                   va[:, k0 + j, bass.ds(p * P + h * A_D, A_D)],
                                                   start=(j == 0), stop=(j == nk - 1))
                                mm.then_inc(pv_psum, 1)
                            if s - 4 >= 0 and (s - 4) % 2 == 1:
                                t = (s - 4) // 2
                                pe.wait_ge(ya_ready, n0 + 2 * t + 4)
                                pe.wait_ge(yaT_done, p * T + t + 2)
                                pe.transpose(ps[:, 7, (t % 2) * P:(t % 2 + 1) * P], ya[t % 2][:],
                                             ident[:]).then_inc(yaT_psum, 1)

                @block.scalar
                def _(act):
                    act.sem_inc(prob_ready, 2)
                    act.sem_inc(probT_ready, 1)
                    act.sem_inc(yaT_done, 2)
                    with act.Fori(0, A_PAIRS) as p:
                        n0 = p * UN
                        for b in range(2):
                            act.wait_ge(qk_psum, p * 2 + b + 3)
                            nc.scalar.activation(sq[b][:], s_ps[b], ACT.Square).then_inc(sq_ready, 1)
                        for b in range(2):
                            act.wait_ge(ms_psum, p * 2 + b + 1)
                            nc.scalar.activation(sq[b][:], ms_ps[b], ACT.Sqrt, bias=eps_sb[:]).then_inc(rms_ready, 1)
                        for s in range(UN + 5):
                            if s < UN:
                                w = keys(s // 2)[1] * P
                                act.wait_ge(neg_ready, n0 + s + 3)
                                act.wait_ge(probT_psum, n0 + s + 1)
                                act.wait_ge(ya_ready, n0 + s + 1)
                                nc.scalar.activation(pr[s % 2][:, :w], ng[s % 2][:, :w], ACT.Exp,
                                                     bias=nmax[:, s % 2:s % 2 + 1], scale=-1.0,
                                                     accum_out=rsum[:, s % 2:s % 2 + 1]).then_inc(prob_ready, 1)
                            if 0 <= s - 1 < UN:
                                m = s - 1
                                w = keys(m // 2)[1] * P
                                act.wait_ge(probT_psum, n0 + m + 3)
                                act.wait_ge(pv_psum, n0 + m + 1)
                                nc.scalar.copy(prT[m % 2][:, :w], tr_ps[:, :w]).then_inc(probT_ready, 1)
                            if s - 5 >= 0 and (s - 5) % 2 == 1:
                                t = (s - 5) // 2
                                act.wait_ge(yaT_psum, p * T + t + 3)
                                nc.scalar.activation(yaT[:, p, t * P:(t + 1) * P],
                                                     ps[:, 7, (t % 2) * P:(t % 2 + 1) * P], ACT.Copy).then_inc(yaT_done, 1)

                @block.vector
                def _(dve):
                    dve.sem_inc(neg_ready, 2)
                    dve.sem_inc(ya_ready, 2)
                    link0 = Chain(dve, c_dve)
                    link0(nc.vector.tensor_scalar(qg_sb[:], qg_sb[:], A_D ** -0.5, None, ALU.mult))
                    with dve.Fori(0, A_PAIRS) as p:
                        n0 = p * UN
                        link = Chain(dve, band_dve, p * (4 + UN))
                        dve.wait_ge(bias_in, p * 16 + 16)
                        link(nc.vector.memset(bias[0:CHUNK, :, BANDW - CHUNK:BANDW], NEG))
                        link(nc.vector.memset(bias[CHUNK:P, :, 0:CHUNK], NEG))
                        for b, (gain, dst) in enumerate(((qg_sb, qn), (kg_sb, kn))):
                            dve.wait_ge(rms_ready, p * 2 + b + 1)
                            if b == 1:
                                dve.wait_ge(norm_done, p * 2 + 1)
                            link(nc.vector.reciprocal(inv[:], sq[b][:]))
                            nc.vector.scalar_tensor_tensor(out=dst[:], in0=s_ps[b], scalar=gain[:, bass.ds(p, 1)],
                                                           in1=inv[:], op0=ALU.mult,
                                                           op1=ALU.mult).then_inc(norm_done, 1)
                        for s in range(UN + 2):
                            if s < UN:
                                w = keys(s // 2)[1] * P
                                dve.wait_ge(score_psum, n0 + s + 1)
                                dve.wait_ge(prob_ready, n0 + s + 1)
                                apart(dve)
                                nc.vector.tensor_tensor_reduce(
                                    out=ng[s % 2][:, :w], in0=s_ps[s % 2][:, :w], in1=bias[:, s % 2, BANDW - w:BANDW],
                                    scale=-1.0, scalar=1e38, op0=ALU.add, op1=ALU.min,
                                    accum_out=nmax[:, s % 2:s % 2 + 1]).then_inc(neg_ready, 1)
                            if 0 <= s - 2:
                                m = s - 2
                                t, h = m // 2, m % 2
                                dve.wait_ge(pv_psum, n0 + m + 3)
                                link(nc.vector.reciprocal(rinv[:, h:h + 1], rsum[:, h:h + 1]))
                                dve.wait_ge(yaT_psum, p * T + t + 1)
                                nc.vector.tensor_scalar(ya[t % 2][:, h * A_D:(h + 1) * A_D],
                                                        ps[:, 6, h * A_D:(h + 1) * A_D], rinv[:, h:h + 1], None,
                                                        ALU.mult).then_inc(ya_ready, 1)

        with ExitStack() as st:
            gw_sb = sb("gw_sb", [P, KD, 2 * P], ctx=st)
            wlr_sb = sb("wlr_sb", [P, KD, RANK], ctx=st)
            gup_sb = sb("gup_sb", [RANK, B_QK], ctx=st)
            gbias_sb = sb("gbias_sb", [1, B_QK], ctx=st)
            lrT = sb("lrT", [RANK, SEQ], ctx=st)
            masks = sb("masks", [P, LEVELS, P], I32, ctx=st)
            ii = sb("ii", [P, P], I32, ctx=st)
            jj = sb("jj", [P, P], I32, ctx=st)
            vf = sb("vf", [P, P], ctx=st)
            tf = sb("tf", [P, P], ctx=st)
            bq = sb("bq", [P, SEQ], ctx=st)
            bk = sb("bk", [P, SEQ], ctx=st)
            gm = sb("gm", [P, SEQ], ctx=st)
            t1 = sb("t1", [P, SEQ], ctx=st)
            t2 = sb("t2", [P, SEQ], ctx=st)
            gl = sb("gl", [P, SEQ], ctx=st)
            cum = sb("cum", [P, SEQ], ctx=st)
            qe = sb("qe", [P, SEQ], ctx=st)
            kdT = sb("kdT", [P, T, P], ctx=st)
            df = [sb(f"df{u}", [P, SEQ], ctx=st) for u in range(2)]
            ef = [t1, t2]
            ql = [gm, sb("ql1", [P, SEQ], ctx=st)]
            kl = [gl, sb("kl1", [P, SEQ], ctx=st)]
            att = sb("att", [P, 2 * T, P], ctx=st)
            state = [sb(f"state{u}", [P, P], ctx=st) for u in range(2)]
            elast = sb("elast", [P, T], ctx=st)
            junk = sb("junk_g", [P, 2, P], ctx=st)
            oms = sb("oms", [P, 2, 2], ctx=st)
            ors = sb("ors", [P, 2, 2], ctx=st)
            yb = [sb(f"yb{u}", [P, 2 * P], ctx=st) for u in range(2)]
            g_w_in = sem("g_w_in")
            g_small = sem("g_small")
            g_consts = sem("g_consts")
            iota_ready = sem("iota_ready")
            lr_psum = sem("lr_psum")
            lr_ready = sem("lr_ready")
            g_qk_psum = sem("g_qk_psum")
            z_psum = sem("z_psum")
            g_qk_ready = sem("g_qk_ready")
            sp_act = sem("softplus_act")
            gla_dve = sem("gla_dve")
            decay_ready = sem("decay_ready")
            cum_psum = sem("cum_psum")
            cum_ready = sem("cum_ready")
            tail_diff = sem("tail_diff")
            head_exp = sem("head_exp")
            tail_exp = sem("tail_exp")
            kd_ready = sem("kd_ready")
            kd_psum = sem("kd_psum")
            kdT_ready = sem("kdT_ready")
            diff_ready = sem("diff_ready")
            exp_ready = sem("exp_ready")
            lev_ready = sem("lev_ready")
            lev_psum = sem("lev_psum")
            att_part = sem("att_part")
            o_psum = sem("o_psum")
            u_psum = sem("u_psum")
            st_ready = sem("st_ready")
            oms_ready = sem("oms_ready")
            orms_ready = sem("orms_ready")
            yb_ready = sem("yb_ready")
            ybT_psum = sem("ybT_psum")
            ybT_done = sem("ybT_done")
            two = lambda b: ps[:, b:b + 2, :].rearrange("p b c -> p (b c)")
            NL = LEVELS - 1

            with nc.Block() as block:
                @block.sync
                def _(sp):
                    sp.dma_start(wlr_sb[:], wlr).then_inc(g_small, 16)
                    sp.dma_start(gup_sb[:], gup).then_inc(g_small, 16)
                    sp.dma_start(gbias_sb[:], gbias).then_inc(g_small, 16)
                    with sp.Fori(0, B_PAIRS) as p:
                        sp.wait_ge(g_qk_psum, p * 2 + 2)
                        sp.dma_start(gw_sb[:], wqk[p + A_PAIRS]).then_inc(g_w_in, 16)

                @block.gpsimd
                def _(pool):
                    nc.gpsimd.iota(ii[:], pattern=[[1, P]], base=0, channel_multiplier=0).then_inc(iota_ready, 1)
                    nc.gpsimd.iota(jj[:], pattern=[[0, P]], base=0, channel_multiplier=1).then_inc(iota_ready, 1)

                @block.tensor
                def _(pe):
                    pe.sem_inc(g_qk_psum, 2)
                    pe.sem_inc(ybT_psum, 2)
                    pe.wait_ge(g_small, 48)
                    for half in range(2):
                        for k in range(KD):
                            mm = pe.matmul(ps[0:RANK, 6 + half, :], wlr_sb[:, k, :],
                                           hT[:, k, half * HALF:(half + 1) * HALF],
                                           start=(k == 0), stop=(k == KD - 1))
                    mm.then_inc(lr_psum, 1)
                    with pe.Fori(0, B_PAIRS) as p:
                        pe.wait_ge(g_w_in, p * 16 + 16)
                        pe.wait_ge(ybT_done, p * T + 2)
                        for b in range(2):
                            for half in range(2):
                                for k in range(KD):
                                    mm = pe.matmul(ps[:, 2 * b + half, :], gw_sb[:, k, b * P:(b + 1) * P],
                                                   hT[:, k, half * HALF:(half + 1) * HALF],
                                                   start=(k == 0), stop=(k == KD - 1))
                            mm.then_inc(g_qk_psum, 1)
                        pe.wait_ge(lr_ready, 1)
                        for t in range(T):
                            z = ps[:, 4 + t // 4, (t % 4) * P:(t % 4 + 1) * P]
                            pe.matmul(z, lrT[:, t * P:(t + 1) * P], gup_sb[:, bass.ds(p * P, P)],
                                      start=True, stop=False)
                            mm = pe.matmul(z, ones[0:1, :], gbias_sb[:, bass.ds(p * P, P)], start=False, stop=True)
                        mm.then_inc(z_psum, 1)
                        pe.wait_ge(decay_ready, p + 1)
                        for t in range(T):
                            mm = pe.matmul(ps[:, 6 + t // 4, (t % 4) * P:(t % 4 + 1) * P], gl[:, t * P:(t + 1) * P],
                                           tri16[:], start=True, stop=True)
                        mm.then_inc(cum_psum, 1)
                        pe.wait_ge(kd_ready, p + 1)
                        for t in range(T):
                            mm = pe.transpose(ps[:, 4 + t // 4, (t % 4) * P:(t % 4 + 1) * P],
                                              df[0][:, t * P:(t + 1) * P], ident[:])
                        mm.then_inc(kd_psum, 1)
                        for l in range(LEVELS):
                            pe.wait_ge(lev_ready, p * LEVELS + l + 1)
                            if l == 1:
                                pe.wait_ge(kdT_ready, p + 1)
                            if l >= 2:
                                pe.wait_ge(att_part, p * LEVELS + l - 1)
                            kk, qq = (bk, bq) if l == 0 else (kl[l % 2], ql[l % 2])
                            for n in range(2 * T):
                                t, h = n % T, n // T
                                hd = slice(h * B_DK, (h + 1) * B_DK)
                                mm = pe.matmul(ps[:, (l % 2) * 4 + n // 4, (n % 4) * P:(n % 4 + 1) * P],
                                               kk[hd, t * P:(t + 1) * P], qq[hd, t * P:(t + 1) * P],
                                               start=True, stop=True)
                            mm.then_inc(lev_psum, 1)
                        pe.wait_ge(att_part, p * LEVELS + LEVELS)
                        for t in range(T + 1):
                            if t < T:
                                pe.wait_ge(yb_ready, p * T + t + 1)
                                if t >= 1:
                                    pe.wait_ge(st_ready, p * T + t)
                                for h in range(2):
                                    hd = slice(h * B_DK, (h + 1) * B_DK)
                                    o = ps[:, (t % 2) * 2 + h, 0:P]
                                    mm = pe.matmul(o, att[:, h * T + t, :], vb[:, t, bass.ds(p * 2 * P + h * P, P)],
                                                   start=True, stop=(t == 0))
                                    if t >= 1:
                                        mm = pe.matmul(o, qe[hd, t * P:(t + 1) * P], state[(t - 1) % 2][hd, :],
                                                       start=False, stop=True)
                                mm.then_inc(o_psum, 1)
                                pe.matmul(ps[:, 4 + t % 2, 0:2 * P], kdT[:, t, :], vb[:, t, bass.ds(p * 2 * P, 2 * P)],
                                          start=True, stop=True).then_inc(u_psum, 1)
                            if t >= 1:
                                m = t - 1
                                pe.wait_ge(yb_ready, p * T + m + 3)
                                pe.wait_ge(ybT_done, p * T + m + 1)
                                for h in range(2):
                                    mm = pe.transpose(ps[:, 6 + m % 2, h * P:(h + 1) * P],
                                                      yb[m % 2][:, h * P:(h + 1) * P], ident[:])
                                mm.then_inc(ybT_psum, 1)

                @block.scalar
                def _(act):
                    act.sem_inc(g_qk_ready, 0 + 1)
                    act.wait_ge(lr_psum, 1)
                    nc.scalar.copy(lrT[:], ps[0:RANK, 6:8, :].rearrange("p b c -> p (b c)")).then_inc(lr_ready, 1)
                    with act.Fori(0, B_PAIRS) as p:
                        act.wait_ge(g_qk_psum, p * 2 + 3)
                        nc.scalar.activation(bq[:], two(0), ACT.Copy, scale=B_DK ** -0.5).then_inc(g_qk_ready, 1)
                        act.wait_ge(g_qk_psum, p * 2 + 4)
                        nc.scalar.activation(bk[:], two(2), ACT.Copy).then_inc(g_qk_ready, 1)
                        act.wait_ge(z_psum, p + 1)
                        link = Chain(act, sp_act, p * 3)
                        link(nc.scalar.activation(t1[:], two(4), ACT.Abs))
                        link(nc.scalar.activation(t2[:], t1[:], ACT.Exp, scale=-1.0))
                        link(nc.scalar.activation(gl[:], t2[:], ACT.Ln, bias=1.0))
                        act.wait_ge(cum_ready, p + 1)
                        nc.scalar.activation(qe[:], cum[:], ACT.Exp).then_inc(head_exp, 1)
                        act.wait_ge(tail_diff, p + 1)
                        nc.scalar.activation(t2[:], t1[:], ACT.Exp).then_inc(tail_exp, 1)
                        act.wait_ge(kd_psum, p + 1)
                        nc.scalar.copy(kdT[:].rearrange("p t c -> p (t c)"), two(4)).then_inc(kdT_ready, 1)
                        for l in range(1, LEVELS):
                            act.wait_ge(diff_ready, p * NL + l)
                            nc.scalar.activation(ef[l % 2][:], df[l % 2][:], ACT.Exp).then_inc(exp_ready, 1)
                        for t in range(T):
                            act.wait_ge(o_psum, p * T + t + 1)
                            act.wait_ge(yb_ready, p * T + t + 1)
                            for h in range(2):
                                nc.scalar.activation(junk[:, h, :], ps[:, (t % 2) * 2 + h, 0:P], ACT.Square,
                                                     scale=B_DV ** -0.5,
                                                     accum_out=oms[:, t % 2, h:h + 1]).then_inc(oms_ready, 1)
                            act.wait_ge(oms_ready, (p * T + t) * 2 + 2)
                            nc.scalar.activation(oms[:, t % 2, :], oms[:, t % 2, :], ACT.Sqrt,
                                                 bias=eps_sb[:]).then_inc(orms_ready, 1)

                @block.vector
                def _(dve):
                    dve.sem_inc(yb_ready, 2)
                    dve.sem_inc(ybT_done, 2)
                    link = Chain(dve, g_consts)
                    dve.wait_ge(iota_ready, 2)
                    link(nc.vector.tensor_tensor(masks[:, 0, :], ii[:], jj[:], ALU.bitwise_xor))
                    link(nc.vector.tensor_copy(vf[:], masks[:, 0, :]))
                    link(nc.vector.tensor_tensor(tf[:], ii[:], jj[:], ALU.is_ge))
                    link(nc.vector.scalar_tensor_tensor(out=vf[:], in0=vf[:], scalar=1.0, in1=tf[:],
                                                        op0=ALU.add, op1=ALU.mult))
                    link(nc.vector.tensor_scalar(masks[:, 0, :], vf[:], 1.0, None, ALU.is_equal))
                    for l in range(1, LEVELS):
                        c = 1 << (l - 1)
                        link(nc.vector.tensor_scalar(tf[:], vf[:], float(2 * c + 1), None, ALU.is_lt))
                        link(nc.vector.scalar_tensor_tensor(out=masks[:, l, :], in0=vf[:], scalar=float(c + 1),
                                                            in1=tf[:], op0=ALU.is_ge, op1=ALU.mult))
                    link(nc.vector.memset(att[:], 0.0))
                    link(nc.vector.memset(ql[1][:], 0.0))
                    link(nc.vector.memset(kl[1][:], 0.0))

                    def halves(a, c):
                        v = a[:].rearrange("p (n s c) -> p n s c", s=2, c=c)
                        return v[:, :, 0, :], v[:, :, 1, :]

                    with dve.Fori(0, B_PAIRS) as p:
                        link = Chain(dve, gla_dve, p * (3 + NL * 3 + 4 * T))
                        dve.wait_ge(sp_act, p * 3 + 1)
                        link(nc.vector.tensor_scalar(gm[:], two(4), 0.0, None, ALU.min))
                        dve.wait_ge(sp_act, p * 3 + 3)
                        nc.vector.tensor_tensor(gl[:], gm[:], gl[:], ALU.subtract).then_inc(decay_ready, 1)
                        dve.wait_ge(cum_psum, p + 1)
                        nc.vector.tensor_copy(cum[:], two(6)).then_inc(cum_ready, 1)
                        dve.wait_ge(cum_ready, p + 1)
                        c3 = cum[:].rearrange("p (t c) -> p t c", c=P)
                        nc.vector.tensor_tensor(t1[:].rearrange("p (t c) -> p t c", c=P),
                                                c3[:, :, P - 1:P].broadcast_to([P, T, P]), c3,
                                                ALU.subtract).then_inc(tail_diff, 1)
                        dve.wait_ge(head_exp, p + 1)
                        link(nc.vector.tensor_copy(elast[:], qe[:].rearrange("p (t c) -> p t c", c=P)[:, :, P - 1]))
                        dve.wait_ge(g_qk_ready, p * 2 + 3)
                        link(nc.vector.tensor_tensor(qe[:], qe[:], bq[:], ALU.mult))
                        dve.wait_ge(tail_exp, p + 1)
                        nc.vector.tensor_tensor(df[0][:], bk[:], t2[:], ALU.mult).then_inc(kd_ready, 1)
                        dve.wait_ge(kd_psum, p + 1)
                        dve.sem_inc(lev_ready, 1)

                        def diff(l):
                            c = 1 << (l - 1)
                            lo, hi = halves(cum, c)
                            dlo, dhi = halves(df[l % 2], c)
                            ref = lo[:, :, c - 1:c].broadcast_to([P, SEQ // (2 * c), c])
                            link(nc.vector.tensor_tensor(dlo, ref, lo, ALU.subtract))
                            nc.vector.tensor_tensor(dhi, hi, ref, ALU.subtract).then_inc(diff_ready, 1)

                        def take(l):
                            dve.wait_ge(lev_psum, p * LEVELS + l + 1)
                            apart(dve)
                            b = (l % 2) * 4
                            nc.vector.copy_predicated(
                                att[:], masks[:, l:l + 1, :].broadcast_to([P, 2 * T, P]),
                                ps[:, b:b + 4, :].rearrange("p b (n c) -> p (b n) c", c=P)).then_inc(att_part, 1)

                        diff(1)
                        for l in range(1, LEVELS):
                            if l + 1 < LEVELS:
                                diff(l + 1)
                            c = 1 << (l - 1)
                            dve.wait_ge(exp_ready, p * NL + l)
                            elo, ehi = halves(ef[l % 2], c)
                            link(nc.vector.tensor_tensor(halves(kl[l % 2], c)[0], halves(bk, c)[0], elo, ALU.mult))
                            link(nc.vector.tensor_tensor(halves(ql[l % 2], c)[1], halves(bq, c)[1], ehi, ALU.mult))
                            dve.sem_inc(lev_ready, 1)
                            take(l - 1)
                            dve.wait_ge(att_part, p * LEVELS + l)
                        take(LEVELS - 1)
                        for t in range(T + 1):
                            if t < T:
                                dve.wait_ge(u_psum, p * T + t + 1)
                                for h in range(2):
                                    hd = slice(h * B_DK, (h + 1) * B_DK)
                                    u = ps[hd, 4 + t % 2, h * P:(h + 1) * P]
                                    if t == 0:
                                        ins = nc.vector.tensor_copy(state[0][hd, :], u)
                                    else:
                                        ins = nc.vector.scalar_tensor_tensor(
                                            out=state[t % 2][hd, :], in0=state[(t - 1) % 2][hd, :],
                                            scalar=elast[hd, t:t + 1], in1=u, op0=ALU.mult, op1=ALU.add)
                                    if h == 0:
                                        link(ins)
                                ins.then_inc(st_ready, 1)
                                dve.wait_ge(st_ready, p * T + t + 1)
                                dve.wait_ge(orms_ready, p * T + t + 1)
                                link(nc.vector.reciprocal(ors[:, t % 2, :], oms[:, t % 2, :]))
                                dve.wait_ge(ybT_psum, p * T + t + 1)
                                for h in range(2):
                                    ins = nc.vector.scalar_tensor_tensor(
                                        out=yb[t % 2][:, h * P:(h + 1) * P], in0=ps[:, (t % 2) * 2 + h, 0:P],
                                        scalar=ors[:, t % 2, h:h + 1], in1=rs[:, t, bass.ds(p * 2 * P + h * P, P)],
                                        op0=ALU.mult, op1=ALU.mult)
                                    if h == 0:
                                        link(ins)
                                ins.then_inc(yb_ready, 1)
                            if t >= 1:
                                m = t - 1
                                dve.wait_ge(ybT_psum, p * T + m + 3)
                                for h in range(2):
                                    ins = nc.vector.tensor_scalar(
                                        ybT[:, p * 2 + h, m * P:(m + 1) * P], ps[:, 6 + m % 2, h * P:(h + 1) * P],
                                        bog_sb[:, bass.ds(p * 2 + h, 1)], None, ALU.mult)
                                    if h == 0:
                                        link(ins)
                                ins.then_inc(ybT_done, 1)
        mid.close()

        x2 = sb("x2", [P, T, D])
        mg = ExitStack()
        mT = sb("mT", [P, KD, SEQ], ctx=mg)
        with ExitStack() as st:
            GA, GB, PA, PB = 0, KD * P, 2 * KD * P, 2 * KD * P + (A_W // P) * P
            WD = PB + (B_V // P) * P
            wd_sb = [sb(f"wd{u}", [P, WD], ctx=st) for u in range(2)]
            gs = [sb(f"gs{u}", [P, 2, HALF], ctx=st) for u in range(2)]
            m1 = sb("m1", [P, HALF], ctx=st)
            m2 = sb("m2", [P, HALF], ctx=st)
            wd_in = [sem(f"wd_in{u}") for u in range(2)]
            d_psum = sem("d_psum")
            gs_ready = sem("gs_ready")
            m_dve = sem("m_dve")
            m_done = sem("m_done")
            with nc.Block() as block:
                @block.sync
                def _(sp):
                    with sp.Fori(0, KD // 2) as i:
                        for u in range(2):
                            sp.wait_ge(d_psum, (i * 2 + u) * 2 + 2)
                            sp.dma_start(wd_sb[u][:], wd[i * 2 + u]).then_inc(wd_in[u], 16)

                @block.tensor
                def _(pe):
                    pe.sem_inc(d_psum, 4)
                    with pe.Fori(0, KD // 2) as i:
                        for u in range(2):
                            pe.wait_ge(wd_in[u], i * 16 + 16)
                            for half in range(2):
                                pe.wait_ge(m_done, (i * 2 + u) * 2 + half + 1)
                                cols = slice(half * HALF, (half + 1) * HALF)
                                for b, (base, src, nk) in enumerate(((GA, hT, KD), (GB, hT, KD),
                                                                     (PA, yaT, A_W // P), (PB, ybT, B_V // P))):
                                    for k in range(nk):
                                        mm = pe.matmul(ps[:, half * 4 + b, :],
                                                       wd_sb[u][:, base + k * P:base + (k + 1) * P],
                                                       src[:, k, cols], start=(k == 0), stop=(k == nk - 1))
                                mm.then_inc(d_psum, 1)

                @block.scalar
                def _(act):
                    with act.Fori(0, KD // 2) as i:
                        for u in range(2):
                            for half in range(2):
                                n = (i * 2 + u) * 2 + half
                                act.wait_ge(d_psum, n + 5)
                                act.wait_ge(m_done, n + 1)
                                nc.scalar.activation(gs[half][:], ps[:, half * 4:half * 4 + 2, :],
                                                     ACT.Sigmoid).then_inc(gs_ready, 1)

                @block.vector
                def _(dve):
                    dve.sem_inc(m_done, 2)
                    with dve.Fori(0, KD // 2) as i:
                        for u in range(2):
                            for half in range(2):
                                n = (i * 2 + u) * 2 + half
                                link = Chain(dve, m_dve, n * 2)
                                dve.wait_ge(gs_ready, n + 1)
                                dve.wait_ge(m_done, n + 2)
                                link(nc.vector.tensor_tensor(m1[:], gs[half][:, 0, :], ps[:, half * 4 + 2, :], ALU.mult))
                                link(nc.vector.tensor_tensor(m2[:], gs[half][:, 1, :], ps[:, half * 4 + 3, :], ALU.mult))
                                nc.vector.tensor_tensor(mT[:, i * 2 + u, half * HALF:(half + 1) * HALF], m1[:], m2[:],
                                                        ALU.add).then_inc(m_done, 1)

        with ExitStack() as st:
            wo_sb = sb("wo_sb", [P, KD, D], ctx=st)
            xin = [sb(f"xin2{u}", [P, D], ctx=st) for u in range(2)]
            mst = [sb(f"mst{u}", [P, KD, P], ctx=st) for u in range(2)]
            h2 = [sb(f"h2{u}", [P, D], ctx=st) for u in range(2)]
            h2T = sb("h2T", [P, KD, P], ctx=st)
            junk = sb("junk_p", [P, D], ctx=st)
            g2_sb = sb("g2_sb", [P, D], ctx=st)
            wr_sb = sb("wr_sb", [P, KD, NG + NE], ctx=st)
            br_sb = sb("br_sb", [P, NG + NE], ctx=st)
            msq = sb("msq2", [P, 2], ctx=st)
            rstd = sb("rstd2", [P, 2], ctx=st)
            wo_in = sem("wo_in")
            r_small = sem("r_small")
            x_in = [sem(f"x2_in{u}") for u in range(2)]
            m_staged = sem("m_staged")
            o_psum2 = sem("out_psum")
            x2_ready = sem("x2_ready")
            msq_ready = sem("msq2_ready")
            rms_ready = sem("rms2_ready")
            rstd_ready = sem("rstd2_ready")
            h2_ready = sem("h2_ready")
            h2_stored = [sem(f"h2_stored{u}") for u in range(2)]
            h2T_psum = sem("h2T_psum")
            h2T_ready = sem("h2T_ready")
            lg_psum = sem("lg_psum")
            lg_ready = sem("lg_ready")
            with nc.Block() as block:
                @block.sync
                def _(sp):
                    sp.dma_start(wo_sb[:], wout).then_inc(wo_in, 16)
                    sp.dma_start(wr_sb[:], wr).then_inc(r_small, 16)
                    sp.dma_start(br_sb[:], br.partition_broadcast(P)).then_inc(r_small, 16)
                    sp.dma_start(g2_sb[:], g2p.partition_broadcast(P)).then_inc(r_small, 16)
                    with sp.Fori(0, T // 2) as i:
                        for u in range(2):
                            sp.wait_ge(x2_ready, i * 2 + u + 1)
                            sp.dma_start(xin[u][:], x_t[i * 2 + u]).then_inc(x_in[u], 16)

                @block.gpsimd
                def _(pool):
                    with pool.Fori(0, T // 2) as i:
                        for u in range(2):
                            t = i * 2 + u
                            pool.wait_ge(o_psum2, t + 1)
                            nc.gpsimd.tensor_copy(mst[u][:], mT[:, :, bass.ds(t * P, P)]).then_inc(m_staged, 1)

                @block.tensor
                def _(pe):
                    pe.sem_inc(o_psum2, 2)
                    pe.sem_inc(h2T_psum, 2)
                    pe.wait_ge(wo_in, 16)
                    with pe.Fori(0, T // 2) as i:
                        for u in range(2):
                            t = i * 2 + u
                            pe.wait_ge(m_staged, t + 1)
                            pe.wait_ge(x2_ready, t + 1)
                            for n in range(2):
                                for k in range(KD):
                                    mm = pe.matmul(ps[:, 2 * u + n, :], mst[u][:, k, :],
                                                   wo_sb[:, k, n * HALF:(n + 1) * HALF],
                                                   start=(k == 0), stop=(k == KD - 1))
                            mm.then_inc(o_psum2, 1)
                        pe.wait_ge(r_small, 48)
                        for u in range(2):
                            t = i * 2 + u
                            pe.wait_ge(h2_ready, t + 1)
                            pe.wait_ge(lg_ready, t + 1)
                            for k in range(KD):
                                mm = pe.transpose(ps[:, 4 + k // 4, (k % 4) * P:(k % 4 + 1) * P],
                                                  h2[u][:, k * P:(k + 1) * P], ident[:])
                            mm.then_inc(h2T_psum, 1)
                            pe.wait_ge(h2T_ready, t + 1)
                            for k in range(KD):
                                mm = pe.matmul(ps[:, 6, 0:NG + NE], h2T[:, k, :], wr_sb[:, k, :],
                                               start=(k == 0), stop=(k == KD - 1))
                            mm.then_inc(lg_psum, 1)

                @block.scalar
                def _(act):
                    with act.Fori(0, T // 2) as i:
                        for u in range(2):
                            t = i * 2 + u
                            act.wait_ge(x2_ready, t + 3)
                            nc.scalar.activation(junk[:], x2[:, t, :], ACT.Square, scale=D ** -0.5,
                                                 accum_out=msq[:, u:u + 1]).then_inc(msq_ready, 1)
                            act.wait_ge(msq_ready, t + 1)
                            nc.scalar.activation(msq[:, u:u + 1], msq[:, u:u + 1], ACT.Sqrt,
                                                 bias=eps_sb[:]).then_inc(rms_ready, 1)
                        for u in range(2):
                            t = i * 2 + u
                            act.wait_ge(h2_ready, t + 1)
                            act.dma_start(h2_t[t], h2[u][:]).then_inc(h2_stored[u], 16)
                            act.wait_ge(h2T_psum, t + 3)
                            nc.scalar.copy(h2T[:].rearrange("p k c -> p (k c)"), two(4)).then_inc(h2T_ready, 1)
                    for u in range(2):
                        act.wait_ge(h2_stored[u], 16 + 16 * (T // 2))

                @block.vector
                def _(dve):
                    dve.sem_inc(x2_ready, 2)
                    dve.sem_inc(lg_ready, 1)
                    for u in range(2):
                        dve.sem_inc(h2_stored[u], 16)
                    dve.wait_ge(r_small, 48)
                    with dve.Fori(0, T // 2) as i:
                        for u in range(2):
                            t = i * 2 + u
                            dve.wait_ge(o_psum2, t + 3)
                            dve.wait_ge(x_in[u], i * 16 + 16)
                            nc.vector.tensor_tensor(x2[:, t, :], two(2 * u), xin[u][:], ALU.add).then_inc(x2_ready, 1)
                        for u in range(2):
                            t = i * 2 + u
                            dve.wait_ge(rms_ready, t + 1)
                            nc.vector.reciprocal(rstd[:, u:u + 1], msq[:, u:u + 1]).then_inc(rstd_ready, 1)
                            dve.wait_ge(rstd_ready, t + 1)
                            dve.wait_ge(h2_stored[u], i * 16 + 16)
                            dve.wait_ge(h2T_psum, t + 1)
                            nc.vector.scalar_tensor_tensor(
                                out=h2[u][:].rearrange("q (k p) -> q k p", k=KD),
                                in0=x2[:, t, :].rearrange("q (p k) -> q k p", k=KD), scalar=rstd[:, u:u + 1],
                                in1=g2_sb[:].rearrange("q (k p) -> q k p", k=KD),
                                op0=ALU.mult, op1=ALU.mult).then_inc(h2_ready, 1)
                        for u in range(2):
                            t = i * 2 + u
                            dve.wait_ge(lg_psum, t + 1)
                            nc.vector.tensor_tensor(lgt[:, t, :], ps[:, 6, 0:NG + NE], br_sb[:],
                                                    ALU.add).then_inc(lg_ready, 1)
        mg.close()

        slot_id = sb("slot_id", [P, TILES], I32)
        row_id = sb("row_id", [P, 2, T], I32)
        e_w = sb("e_w", [P, 2, T])
        over_e = sb("over_e", [P, MAX_OVER], I32)
        n_over = sb("n_over", [P, 1], I32)
        with ExitStack() as st:
            def f(name, shape, dt=F32):
                return sb("r_" + name, shape, dt, ctx=st)
            iot = f("iot", [P, P], I32)
            io = f("io", [P, P])
            tok_i = f("tok_i", [P, T], I32)
            tok1 = f("tok1", [P, T])
            rv4, rv8 = f("rv4", [P, NG]), f("rv8", [P, EPG])
            thr = f("thr", [P, T - 1])
            gmax, gex, gsum, gtop = f("gmax", [P, T]), f("gex", [P, T, NG]), f("gsum", [P, T]), f("gtop", [P, T])
            cand4, goh = f("cand4", [P, T, NG]), f("goh", [P, T, NG])
            r1 = f("r1", [P, T])
            prod = f("prod", [P, T, NG, EPG])
            es = [f("es0", [P, T, EPG]), f("es1", [P, T, EPG])]
            em = f("em", [P, 2, T])
            cand8 = f("cand8", [P, T, EPG])
            oh = [f("oh0", [P, T, EPG]), f("oh1", [P, T, EPG])]
            dif, ex, den = f("dif", [P, T]), f("ex", [P, T]), f("den", [P, T])
            M = [f("M0", [P, T, NE]), f("M1", [P, T, NE])]
            Ms, Mp = f("Ms", [P, T, NE]), f("Mp", [P, T, NE])
            tot, totT, novT = f("tot", [P, NE]), f("totT", [NE, 1]), f("novT", [NE, 1])
            cmp7 = f("cmp7", [NE, T - 1])
            novB = f("novB", [NE, P])
            incl = f("incl", [NE, 2, NE])
            off = f("off", [P, 2, NE])
            cmpo = f("cmpo", [P, MAX_OVER, NE])
            eid = f("eid", [P, MAX_OVER])
            pr32 = f("pr32", [P, T, NE])
            rank, ea, eb2 = f("rank", [P, 2, T]), f("ea", [P, 2, T]), f("eb", [P, 2, T])
            cmpr = f("cmpr", [P, 2, T, T - 1])
            mt, isov, tile_, slot = f("mt", [P, 2, T]), f("isov", [P, 2, T]), f("tile", [P, 2, T]), f("slot", [P, 2, T])
            pos = f("pos", [P, 2, T])
            R = f("R", [P, 2, T, P])
            O = f("O", [P, 2, T, TILES])
            lst, emp = f("lst", [P, TILES]), f("emp", [P, TILES])
            r_iota = sem("r_iota")
            r_dve = sem("r_dve")
            r_act = sem("r_act")
            r_psum = sem("r_psum")
            need_exp = sem("need_exp")
            need_tot = sem("need_tot")
            need_off = sem("need_off")
            need_slots = sem("need_slots")

            def last(a, n):
                return a.unsqueeze(len(a.shape)).broadcast_to(list(a.shape) + [n])

            with nc.Block() as block:
                @block.gpsimd
                def _(pool):
                    nc.gpsimd.iota(iot[:], pattern=[[1, P]], base=0, channel_multiplier=0).then_inc(r_iota, 1)
                    nc.gpsimd.iota(tok_i[:], pattern=[[P, T]], base=1, channel_multiplier=1).then_inc(r_iota, 1)

                @block.scalar
                def _(act):
                    act.wait_ge(need_exp, 1)
                    nc.scalar.activation(gex[:], cand4[:], ACT.Exp).then_inc(r_act, 1)
                    nc.scalar.activation(ex[:], dif[:], ACT.Exp).then_inc(r_act, 1)

                @block.tensor
                def _(pe):
                    pe.wait_ge(need_tot, 1)
                    rk = ps[:, 0, 0:T * NE]
                    pe.matmul(rk, before[:], Ms[:].rearrange("p t e -> p (t e)"), start=True, stop=False)
                    pe.matmul(rk, ones[:], Mp[:].rearrange("p t e -> p (t e)"), start=False, stop=True)
                    pe.matmul(ps[0:NE, 1, 0:1], tot[:], ones[:, 0:1], start=True, stop=True).then_inc(r_psum, 1)
                    pe.wait_ge(need_off, 1)
                    pe.matmul(ps[:, 2, 0:2 * NE], novB[:], incl[:].rearrange("p a e -> p (a e)"),
                              start=True, stop=True).then_inc(r_psum, 1)
                    pe.wait_ge(need_slots, 1)
                    for n in range(2 * T):
                        mm = pe.matmul(ps[:, 3, 0:TILES], R[:, n // T, n % T, :], O[:, n // T, n % T, :],
                                       start=(n == 0), stop=(n == 2 * T - 1))
                    mm.then_inc(r_psum, 1)

                @block.vector
                def _(dve):
                    link = Chain(dve, r_dve)
                    v = nc.vector
                    dve.wait_ge(r_iota, 2)
                    link(v.tensor_copy(io[:], iot[:]))
                    link(v.tensor_copy(tok1[:], tok_i[:]))
                    link(v.tensor_scalar(rv4[:], io[:, 0:NG], -1.0, float(NG), ALU.mult, ALU.add))
                    link(v.tensor_scalar(rv8[:], io[:, 0:EPG], -1.0, float(EPG), ALU.mult, ALU.add))
                    link(v.tensor_scalar(thr[:], io[:, 0:T - 1], 1.0, float(P), ALU.add, ALU.mult))
                    gl_ = lgt[:, :, 0:NG]
                    el_ = lgt[:, :, NG:].rearrange("p t (g e) -> p t g e", g=NG)
                    link(v.tensor_reduce(gmax[:], gl_, AX.X, ALU.max))
                    link(v.tensor_tensor(goh[:], gl_, last(gmax[:], NG), ALU.is_equal))
                    link(v.tensor_tensor(goh[:], goh[:], rv4[:].unsqueeze(1).broadcast_to([P, T, NG]), ALU.mult))
                    link(v.tensor_reduce(r1[:], goh[:], AX.X, ALU.max))
                    link(v.tensor_tensor(goh[:], goh[:], last(r1[:], NG), ALU.is_equal))
                    link(v.tensor_tensor(cand4[:], gl_, last(gmax[:], NG), ALU.subtract))
                    link(v.tensor_tensor(prod[:], el_, last(goh[:], EPG), ALU.mult))
                    link(v.tensor_reduce(es[0][:], prod[:].rearrange("p t g e -> p t e g"), AX.X, ALU.add))
                    for c in range(2):
                        link(v.tensor_reduce(em[:, c, :], es[c][:], AX.X, ALU.max))
                        link(v.tensor_tensor(cand8[:], es[c][:], last(em[:, c, :], EPG), ALU.is_equal))
                        link(v.tensor_tensor(cand8[:], cand8[:], rv8[:].unsqueeze(1).broadcast_to([P, T, EPG]),
                                             ALU.mult))
                        link(v.tensor_reduce(r1[:], cand8[:], AX.X, ALU.max))
                        link(v.tensor_tensor(oh[c][:], cand8[:], last(r1[:], EPG), ALU.is_equal))
                        if c == 0:
                            link(v.scalar_tensor_tensor(out=es[1][:], in0=oh[0][:], scalar=-3e38, in1=es[0][:],
                                                        op0=ALU.mult, op1=ALU.add))
                    v.tensor_tensor(dif[:], em[:, 1, :], em[:, 0, :], ALU.subtract).then_inc(need_exp, 1)
                    for c in range(2):
                        link(v.tensor_tensor(M[c][:].rearrange("p t (g e) -> p t g e", g=NG), last(goh[:], EPG),
                                             oh[c][:].unsqueeze(2).broadcast_to([P, T, NG, EPG]), ALU.mult))
                    link(v.tensor_tensor(Ms[:], M[0][:], M[1][:], ALU.add))
                    link(v.memset(Mp[:, 0, :], 0.0))
                    for t in range(1, T):
                        link(v.tensor_tensor(Mp[:, t, :], Mp[:, t - 1, :], Ms[:, t - 1, :], ALU.add))
                    v.tensor_tensor(tot[:], Mp[:, T - 1, :], Ms[:, T - 1, :], ALU.add).then_inc(need_tot, 1)
                    link(v.tensor_copy(incl[:, 0, :], before[0:NE, 0:NE]))
                    link(v.tensor_tensor(incl[:, 1, :], before[0:NE, 0:NE], ident[0:NE, 0:NE], ALU.add))
                    dve.wait_ge(r_act, 2)
                    link(v.tensor_reduce(gsum[:], gex[:], AX.X, ALU.add))
                    link(v.reciprocal(gtop[:], gsum[:]))
                    link(v.tensor_scalar(den[:], ex[:], 1.0, None, ALU.add))
                    link(v.reciprocal(den[:], den[:]))
                    link(v.tensor_tensor(e_w[:, 0, :], den[:], gtop[:], ALU.mult))
                    link(v.tensor_tensor(e_w[:, 1, :], e_w[:, 0, :], ex[:], ALU.mult))
                    dve.wait_ge(r_psum, 1)
                    link(v.tensor_copy(totT[:], ps[0:NE, 1, 0:1]))
                    link(v.tensor_scalar(cmp7[:], thr[0:NE, :], totT[:, 0:1], None, ALU.is_lt))
                    link(v.tensor_reduce(novT[:], cmp7[:], AX.X, ALU.add))
                    v.tensor_scalar(novB[:], ones[0:NE, :], novT[:, 0:1], None, ALU.mult).then_inc(need_off, 1)
                    rk = ps[:, 0, 0:T * NE].rearrange("p (t e) -> p t e", e=NE)
                    for c in range(2):
                        link(v.tensor_tensor(pr32[:], M[c][:], rk, ALU.mult))
                        link(v.tensor_reduce(rank[:, c, :], pr32[:], AX.X, ALU.add))
                        link(v.tensor_tensor(pr32[:], M[c][:], io[:, 0:NE].unsqueeze(1).broadcast_to([P, T, NE]),
                                             ALU.mult))
                        link(v.tensor_reduce(ea[:, c, :], pr32[:], AX.X, ALU.add))
                    dve.wait_ge(r_psum, 2)
                    link(v.tensor_copy(off[:].rearrange("p a e -> p (a e)"), ps[:, 2, 0:2 * NE]))
                    for c in range(2):
                        link(v.tensor_tensor(pr32[:], M[c][:], off[:, 0:1, :].broadcast_to([P, T, NE]), ALU.mult))
                        link(v.tensor_reduce(eb2[:, c, :], pr32[:], AX.X, ALU.add))
                    link(v.tensor_copy(n_over[:], off[:, 1, NE - 1:NE]))
                    link(v.tensor_tensor(cmpo[:], off[:, 1:2, :].broadcast_to([P, MAX_OVER, NE]),
                                         last(io[:, 0:MAX_OVER], NE), ALU.is_le))
                    link(v.tensor_reduce(eid[:], cmpo[:], AX.X, ALU.add))
                    link(v.tensor_scalar(over_e[:], eid[:], float(NE - 1), None, ALU.min))
                    link(v.tensor_tensor(cmpr[:], last(rank[:], T - 1),
                                         thr[:].unsqueeze(1).unsqueeze(1).broadcast_to([P, 2, T, T - 1]), ALU.is_ge))
                    link(v.tensor_reduce(mt[:], cmpr[:], AX.X, ALU.add))
                    link(v.tensor_scalar(isov[:], mt[:], 0.0, None, ALU.is_gt))
                    link(v.tensor_tensor(eb2[:], eb2[:], mt[:], ALU.add))
                    link(v.tensor_tensor(eb2[:], eb2[:], ea[:], ALU.subtract))
                    link(v.scalar_tensor_tensor(out=eb2[:], in0=eb2[:], scalar=float(NE - 1), in1=isov[:],
                                                op0=ALU.add, op1=ALU.mult))
                    link(v.tensor_tensor(tile_[:], ea[:], eb2[:], ALU.add))
                    link(v.scalar_tensor_tensor(out=slot[:], in0=mt[:], scalar=-float(P), in1=rank[:],
                                                op0=ALU.mult, op1=ALU.add))
                    link(v.scalar_tensor_tensor(out=pos[:], in0=tile_[:], scalar=float(P), in1=slot[:],
                                                op0=ALU.mult, op1=ALU.add))
                    link(v.tensor_copy(row_id[:], pos[:]))
                    for c in range(2):
                        for t in range(T):
                            link(v.tensor_scalar(R[:, c, t, :], io[:], slot[:, c, t:t + 1], None, ALU.is_equal))
                            link(v.tensor_scalar(O[:, c, t, :], io[:, 0:TILES], tile_[:, c, t:t + 1],
                                                 tok1[:, t:t + 1], ALU.is_equal, ALU.mult))
                    dve.sem_inc(need_slots, 1)
                    dve.wait_ge(r_psum, 3)
                    link(v.tensor_copy(lst[:], ps[:, 3, 0:TILES]))
                    link(v.tensor_scalar(emp[:], lst[:], 0.0, 8.0 * SEQ, ALU.is_equal, ALU.mult))
                    link(v.scalar_tensor_tensor(out=slot_id[:], in0=lst[:], scalar=-1.0, in1=emp[:],
                                                op0=ALU.add, op1=ALU.add))

        with ExitStack() as st:
            wgu = [sb(f"wgu{u}", [P, KD, 2, DE], ctx=st) for u in range(2)]
            wdn = [sb(f"wdn{u}", [P, 2, D], ctx=st) for u in range(2)]
            idx = [sb(f"idx{u}", [P, 1], I32, ctx=st) for u in range(2)]
            hg = [sb(f"hg{u}", [P, D], ctx=st) for u in range(2)]
            hgT = [sb(f"hgT{u}", [P, KD, P], ctx=st) for u in range(2)]
            sg = [sb(f"esg{u}", [P, DE], ctx=st) for u in range(2)]
            sil = sb("sil", [P, DE], ctx=st)
            av = [sb(f"av{u}", [P, 2, P], ctx=st) for u in range(2)]
            avT = [sb(f"avT{u}", [P, 2, P], ctx=st) for u in range(2)]
            ys = [sb(f"ys{u}", [P, D], ctx=st) for u in range(2)]
            wgu_in = [sem(f"wgu_in{u}") for u in range(2)]
            wdn_in = [sem(f"wdn_in{u}") for u in range(2)]
            hg_clear = sem("hg_clear")
            idx_ready = sem("idx_ready")
            hg_in = [sem(f"hg_in{u}") for u in range(2)]
            hgT_psum = sem("hgT_psum")
            hgT_ready = sem("hgT_ready")
            gu_psum = sem("gu_psum")
            esg_ready = sem("esg_ready")
            sil_ready = sem("sil_ready")
            av_ready = sem("av_ready")
            avT_psum = sem("avT_psum")
            avT_ready = sem("avT_ready")
            y_psum = sem("y_psum")
            ys_ready = sem("ys_ready")
            ys_stored = [sem(f"ys_stored{u}") for u in range(2)]
            o_w_in = sem("o_w_in")
            o_idx = sem("o_idx")
            o_hg_in = sem("o_hg_in")
            o_pe = sem("o_pe")
            o_act = sem("o_act")
            o_dve = sem("o_dve")
            o_stored = sem("o_stored")
            o_free = sem("o_free")

            def transposes(pe, src, pieces, dst):
                for k in range(pieces):
                    mm = pe.transpose(dst[:, k * P:(k + 1) * P], src[:, k * P:(k + 1) * P], ident[:])
                return mm

            def gate_up(pe, u, bank):
                for k in range(KD):
                    mm = pe.matmul(ps[:, bank, :], hgT[u][:, k, :], wgu[u][:, k, :, :].rearrange("p a f -> p (a f)"),
                                   start=(k == 0), stop=(k == KD - 1))
                return mm

            def down(pe, u):
                for n in range(2):
                    for c in range(2):
                        mm = pe.matmul(ps[:, 5 + n, :], avT[u][:, c, :], wdn[u][:, c, n * HALF:(n + 1) * HALF],
                                       start=(c == 0), stop=(c == 1))
                return mm

            def act_order(a):
                return a.rearrange("q (p c) -> q c p", c=2)

            av2 = [a[:].rearrange("p c f -> p (c f)") for a in av]
            avT2 = [a[:].rearrange("p c f -> p (c f)") for a in avT]
            with nc.Block() as block:
                @block.sync
                def _(sp):
                    with sp.Fori(0, NE // 2) as i:
                        for u in range(2):
                            e = i * 2 + u
                            sp.wait_ge(gu_psum, e + 1)
                            sp.dma_start(wgu[u][:, :, 0, :], wg_e[e]).then_inc(wgu_in[u], 16)
                            sp.dma_start(wgu[u][:, :, 1, :], wu_e[e]).then_inc(wgu_in[u], 16)
                            sp.wait_ge(y_psum, e + 1)
                            sp.dma_start(wdn[u][:].rearrange("p c n -> p (c n)"), wn_e[e]).then_inc(wdn_in[u], 16)
                    over = sp.value_load(n_over[0:1, 0:1], min_val=0, max_val=MAX_OVER)
                    sp.wait_ge(y_psum, NE + 2)
                    with sp.Fori(0, MAX_OVER) as o:
                        with sp.If(o < over):
                            sp.wait_ge(o_pe, o * 4 + 4)
                            apart(sp)
                            e = sp.value_load(over_e[0:1, bass.ds(o, 1)], min_val=0, max_val=NE - 1)
                            sp.dma_start(wgu[0][:, :, 0, :], wg_e[e]).then_inc(o_w_in, 16)
                            sp.dma_start(wgu[0][:, :, 1, :], wu_e[e]).then_inc(o_w_in, 16)
                            sp.dma_start(wdn[0][:].rearrange("p c n -> p (c n)"), wn_e[e]).then_inc(o_w_in, 16)
                            sp.nop()

                @block.gpsimd
                def _(pool):
                    for u in range(2):
                        nc.gpsimd.memset(hg[u][:], 0.0).then_inc(hg_clear, 1)
                    pool.wait_ge(hg_clear, 2)

                    def gather(t, u, n):
                        nc.gpsimd.tensor_copy(idx[u][:], slot_id[:, bass.ds(t, 1)]).then_inc(idx_ready, 1)
                        pool.wait_ge(idx_ready, n)
                        apart(pool)
                        nc.gpsimd.indirect_dma_start(
                            hg[u][:], None, h2_dram, bass.IndirectOffsetOnAxis(ap=idx[u][:, 0:1].bitcast(U32), axis=0),
                            bounds_check=SEQ - 1, oob_is_err=False).then_inc(hg_in[u], 16)

                    gather(0, 0, 1)
                    with pool.Fori(0, NE // 2) as i:
                        for u in range(2):
                            t = i * 2 + u
                            pool.wait_ge(hgT_psum, t + 2)
                            gather(t + 1, 1 - u, t + 2)
                    over = pool.value_load(n_over[0:1, 0:1], min_val=0, max_val=MAX_OVER)
                    pool.wait_ge(hgT_psum, NE + 3)
                    with pool.Fori(0, MAX_OVER) as o:
                        with pool.If(o < over):
                            pool.wait_ge(o_pe, o * 4 + 4)
                            nc.gpsimd.tensor_copy(idx[0][:], slot_id[:, bass.ds(o + NE, 1)]).then_inc(o_idx, 1)
                            pool.wait_ge(o_idx, o + 1)
                            apart(pool)
                            nc.gpsimd.indirect_dma_start(
                                hg[0][:], None, h2_dram,
                                bass.IndirectOffsetOnAxis(ap=idx[0][:, 0:1].bitcast(U32), axis=0),
                                bounds_check=SEQ - 1, oob_is_err=False).then_inc(o_hg_in, 16)
                            pool.wait_ge(o_dve, o * 5 + 5)
                            pool.dma_start(y_t[o + NE], ys[0][:]).then_inc(o_stored, 16)
                            pool.wait_ge(o_stored, o * 16 + 16)
                            pool.sem_inc(o_free, 1)

                @block.tensor
                def _(pe):
                    pe.sem_inc(hgT_psum, 2)
                    pe.sem_inc(gu_psum, 2)
                    pe.sem_inc(y_psum, 2)
                    pe.sem_inc(o_pe, 4)
                    pe.wait_ge(hg_in[0], 16)
                    transposes(pe, hg[0], KD, two(0)).then_inc(hgT_psum, 1)
                    with pe.Fori(0, NE // 2) as i:
                        for u in range(2):
                            t = i * 2 + u
                            pe.wait_ge(wgu_in[u], i * 32 + 32)
                            pe.wait_ge(hgT_ready, t + 2)
                            pe.wait_ge(av_ready, t + 1)
                            gate_up(pe, u, 2 + u).then_inc(gu_psum, 1)
                            pe.wait_ge(hg_in[1 - u], i * 16 + 16 + 16 * u)
                            transposes(pe, hg[1 - u], KD, two(0)).then_inc(hgT_psum, 1)
                            pe.wait_ge(av_ready, t + 3)
                            pe.wait_ge(avT_ready, t + 1)
                            transposes(pe, av2[u], 2, ps[:, 4 + 3 * u, 0:2 * P]).then_inc(avT_psum, 1)
                            pe.wait_ge(avT_ready, t + 3)
                            pe.wait_ge(wdn_in[u], i * 16 + 16)
                            pe.wait_ge(ys_ready, t + 1)
                            down(pe, u).then_inc(y_psum, 1)
                    over = pe.value_load(n_over[0:1, 0:1], min_val=0, max_val=MAX_OVER)
                    pe.wait_ge(ys_ready, NE + 1)
                    pe.wait_ge(hgT_ready, NE + 2)
                    with pe.Fori(0, MAX_OVER) as o:
                        with pe.If(o < over):
                            pe.wait_ge(o_hg_in, o * 16 + 16)
                            transposes(pe, hg[0], KD, two(0)).then_inc(o_pe, 1)
                            pe.wait_ge(o_w_in, o * 48 + 48)
                            pe.wait_ge(o_dve, o * 5 + 1)
                            gate_up(pe, 0, 2).then_inc(o_pe, 1)
                            pe.wait_ge(o_dve, o * 5 + 3)
                            transposes(pe, av2[0], 2, ps[:, 4, 0:2 * P]).then_inc(o_pe, 1)
                            pe.wait_ge(o_dve, o * 5 + 4)
                            down(pe, 0).then_inc(o_pe, 1)
                            pe.nop()

                @block.scalar
                def _(act):
                    act.sem_inc(hgT_ready, 1)
                    for u in range(2):
                        act.sem_inc(ys_stored[u], 16)
                    act.wait_ge(hgT_psum, 3)
                    nc.scalar.copy(hgT[0][:].rearrange("p k c -> p (k c)"), two(0)).then_inc(hgT_ready, 1)
                    with act.Fori(0, NE // 2) as i:
                        for u in range(2):
                            t = i * 2 + u
                            act.wait_ge(gu_psum, t + 3)
                            act.wait_ge(av_ready, t + 1)
                            nc.scalar.activation(sg[u][:], ps[:, 2 + u, 0:DE], ACT.Sigmoid).then_inc(esg_ready, 1)
                            act.wait_ge(hgT_psum, t + 4)
                            nc.scalar.copy(hgT[1 - u][:].rearrange("p k c -> p (k c)"), two(0)).then_inc(hgT_ready, 1)
                            act.wait_ge(ys_ready, t + 2)
                            act.dma_start(y_t[t], ys[u][:]).then_inc(ys_stored[u], 16)
                    for u in range(2):
                        act.wait_ge(ys_stored[u], 16 + 8 * NE)
                    over = act.value_load(n_over[0:1, 0:1], min_val=0, max_val=MAX_OVER)
                    with act.Fori(0, MAX_OVER) as o:
                        with act.If(o < over):
                            act.wait_ge(o_pe, o * 4 + 6)
                            nc.scalar.activation(sg[0][:], ps[:, 2, 0:DE], ACT.Sigmoid).then_inc(o_act, 1)
                            act.nop()

                @block.vector
                def _(dve):
                    dve.sem_inc(av_ready, 2)
                    dve.sem_inc(avT_ready, 2)
                    dve.sem_inc(ys_ready, 1)
                    dve.sem_inc(o_free, 1)
                    with dve.Fori(0, NE // 2) as i:
                        for u in range(2):
                            t = i * 2 + u
                            dve.wait_ge(esg_ready, t + 1)
                            nc.vector.tensor_tensor(sil[:], ps[:, 2 + u, 0:DE], sg[u][:],
                                                    ALU.mult).then_inc(sil_ready, 1)
                            dve.wait_ge(sil_ready, t + 1)
                            nc.vector.tensor_tensor(av[u][:], act_order(sil[:]), act_order(ps[:, 2 + u, DE:2 * DE]),
                                                    ALU.mult).then_inc(av_ready, 1)
                            dve.wait_ge(avT_psum, t + 1)
                            nc.vector.tensor_copy(avT2[u], ps[:, 4 + 3 * u, 0:2 * P]).then_inc(avT_ready, 1)
                            dve.wait_ge(y_psum, t + 3)
                            dve.wait_ge(ys_stored[u], i * 16 + 16)
                            nc.vector.tensor_copy(ys[u][:], two(5)).then_inc(ys_ready, 1)
                    over = dve.value_load(n_over[0:1, 0:1], min_val=0, max_val=MAX_OVER)
                    dve.wait_ge(ys_stored[0], 16 + 8 * NE)
                    with dve.Fori(0, MAX_OVER) as o:
                        with dve.If(o < over):
                            link = Chain(dve, o_dve, o * 5)
                            dve.wait_ge(o_pe, o * 4 + 5)
                            link(nc.vector.tensor_copy(hgT[0][:].rearrange("p k c -> p (k c)"), two(0)))
                            dve.wait_ge(o_act, o + 1)
                            link(nc.vector.tensor_tensor(sil[:], ps[:, 2, 0:DE], sg[0][:], ALU.mult))
                            link(nc.vector.tensor_tensor(av[0][:], act_order(sil[:]), act_order(ps[:, 2, DE:2 * DE]),
                                                         ALU.mult))
                            dve.wait_ge(o_pe, o * 4 + 7)
                            link(nc.vector.tensor_copy(avT2[0], ps[:, 4, 0:2 * P]))
                            dve.wait_ge(o_pe, o * 4 + 8)
                            dve.wait_ge(o_free, o + 1)
                            link(nc.vector.tensor_copy(ys[0][:], two(5)))
                            apart(dve)

        with ExitStack() as st:
            ya_ = [[sb(f"yg{c}{u}", [P, D], ctx=st) for u in range(2)] for c in range(2)]
            yg_in = [sem(f"yg_in{u}") for u in range(2)]
            first_added = sem("first_added")
            both_added = sem("both_added")
            out_stored = sem("out_stored")
            with nc.Block() as block:
                @block.gpsimd
                def _(pool):
                    for t in range(T):
                        if t >= 2:
                            pool.wait_ge(both_added, t - 1)
                        for c in range(2):
                            nc.gpsimd.indirect_dma_start(
                                ya_[c][t % 2][:], None, y_dram,
                                bass.IndirectOffsetOnAxis(ap=row_id[:, c, t:t + 1].bitcast(U32), axis=0),
                                bounds_check=TILES * P - 1, oob_is_err=False).then_inc(yg_in[t % 2], 16)

                @block.vector
                def _(dve):
                    for t in range(T):
                        dve.wait_ge(yg_in[t % 2], 32 * (t // 2 + 1))
                        nc.vector.scalar_tensor_tensor(out=x2[:, t, :], in0=ya_[0][t % 2][:],
                                                       scalar=e_w[:, 0, t:t + 1], in1=x2[:, t, :], op0=ALU.mult,
                                                       op1=ALU.add).then_inc(first_added, 1)
                        dve.wait_ge(first_added, t + 1)
                        nc.vector.scalar_tensor_tensor(out=x2[:, t, :], in0=ya_[1][t % 2][:],
                                                       scalar=e_w[:, 1, t:t + 1], in1=x2[:, t, :], op0=ALU.mult,
                                                       op1=ALU.add).then_inc(both_added, 1)

                @block.sync
                def _(sp):
                    for t in range(T):
                        sp.wait_ge(both_added, t + 1)
                        sp.dma_start(out_t[t], x2[:, t, :]).then_inc(out_stored, 16)
                    sp.wait_ge(out_stored, 16 * T)


def kernel(**inputs):
    import numpy as np
    import concourse.bacc as bacc
    from concourse import mybir as my
    from concourse.bass_utils import run_bass_kernel_spmd

    a = {k: np.asarray(v) for k, v in inputs.items()}
    w_in = a["w_in"][0]

    def rows(w):
        return w.reshape(-1, P, w.shape[1]).transpose(1, 0, 2)

    def cols(v):
        return v.reshape(-1, P).T

    o = [0, 512, 1024, 1536, 1792, 2048, 2560, 3072, 3088, 5136]
    part = [w_in[:, o[n]:o[n + 1]] for n in range(9)]
    aq, ak, av, bq, bk, bv, brr, lr, gates = part
    pairs = [(aq, ak, n) for n in range(A_PAIRS)] + [(bq, bk, n) for n in range(B_PAIRS)]
    blk = lambda w, n: w[:, n * P:(n + 1) * P]
    wqk = np.stack([rows(np.concatenate([blk(q, n), blk(k, n)], 1)) for q, k, n in pairs])
    flat = lambda w: rows(w).reshape(P, -1)
    wd = np.stack([np.concatenate([flat(blk(gates, n)), flat(blk(gates, KD + n)), flat(blk(a["proj_a"][0], n)),
                                   flat(blk(a["proj_b"][0], n))], 1) for n in range(KD)])
    rel = a["rel_bias"]
    at = np.clip(5 * P + np.arange(P)[:, None] - np.arange(BANDW)[None, :], 0, 2 * P)
    relx = rel[at].transpose(2, 0, 1).reshape(A_PAIRS, 2, P, BANDW).transpose(0, 2, 1, 3)
    turned = lambda w: w.reshape(P, KD, -1)
    arrays = {
        "x": a["x"][0], "g1": cols(a["norm_mix_gain"][0]), "wv": rows(np.concatenate([av, bv, brr], 1)),
        "wqk": wqk, "wlr": rows(lr), "wd": wd, "wout": rows(a["w_out"][0]),
        "qg": cols(a["a_q_gain"][0].reshape(-1)), "kg": cols(a["a_k_gain"][0].reshape(-1)),
        "bog": cols(a["b_out_gain"][0].reshape(-1)), "gup": a["b_gate_up"][0], "gbias": a["b_gate_bias"],
        "relx": relx, "g2p": a["norm_ffn_gain"][0].reshape(P, KD).T.reshape(-1),
        "wr": turned(np.concatenate([a["w_group"][0], a["w_router"][0]], 1)),
        "br": np.concatenate([a["b_group"][0], a["b_router"][0]]),
        "w_gate": a["w_gate"][0], "w_up": a["w_up"][0], "w_down": a["w_down"][0],
    }
    nc = bacc.Bacc("TRN2", target_bir_lowering=False, num_devices=1)
    arrays = {f"in_{n}": np.ascontiguousarray(v) for n, v in arrays.items()}
    args = [nc.dram_tensor(n, v.shape, my.dt.from_np(v.dtype), kind="ExternalInput").ap() for n, v in arrays.items()]
    args.append(nc.dram_tensor("out_0", (SEQ, D), F32, kind="ExternalOutput").ap())
    args.append(nc.dram_tensor("h2_rows", (SEQ, D), F32, kind="Internal").ap())
    args.append(nc.dram_tensor("y_rows", (TILES * P, D), F32, kind="Internal").ap())
    layer_kernel(nc, *args)
    r = run_bass_kernel_spmd(nc, [arrays], core_ids=[0])
    return np.asarray(r.results[0]["out_0"]).reshape(1, SEQ, D)
```

```python
from contextlib import ExitStack

import concourse.bass as bass
from concourse import mybir

ALU = mybir.AluOpType
ACT = mybir.ActivationFunctionType
AX = mybir.AxisListType
F32 = mybir.dt.float32
F32R = mybir.dt.float32r
I32 = mybir.dt.int32
U32 = mybir.dt.uint32

P = 128
D = 1024
SEQ = 1024
T = SEQ // P
KD = D // P
EPS = 1e-6
CHUNK = 64
LEFT = 8
HALF = 512
A_W, A_H, A_D = 512, 8, 64
A_PAIRS = A_H // 2
BAND_T = LEFT * CHUNK // P + 1
BANDW = BAND_T * P
B_V, B_QK, B_H, B_DK, B_DV, RANK = 512, 256, 4, 64, 128, 16
B_PAIRS = B_H // 2
GATE_TEMP = 16.0
LEVELS = 8
NG, EPG, NE = 4, 8, 32
DE = 256
MAX_OVER = 2 * SEQ // P
TILES = NE + MAX_OVER
NEG = -1e30


class Chain:

    def __init__(self, eng, sem, before=0):
        self.eng, self.sem, self.before, self.n = eng, sem, before, 0

    def __call__(self, ins):
        self.n += 1
        ins.then_inc(self.sem, 1)
        self.eng.wait_ge(self.sem, self.before + self.n)


def layer_kernel(nc, x, g1, wv, wqk, wlr, wd, wout, qg, kg, bog, gup, gbias, relx, g2p, wr, br,
                 w_gate, w_up, w_down, out, h2_dram, y_dram):
    x_t = x.rearrange("(t p) d -> t p d", p=P)
    out_t = out.rearrange("(t p) d -> t p d", p=P)
    h2_t = h2_dram.rearrange("(t p) d -> t p d", p=P)
    y_t = y_dram.rearrange("(t p) d -> t p d", p=P)
    wg_e = w_gate.rearrange("e (p k) f -> e p k f", p=P)
    wu_e = w_up.rearrange("e (p k) f -> e p k f", p=P)
    wn_e = w_down.rearrange("e (p c) n -> e p c n", p=P)

    with ExitStack() as top:
        def sem(name):
            return top.enter_context(nc.semaphore(name))

        def sb(name, shape, dt=F32, ctx=top):
            return ctx.enter_context(nc.sbuf_tensor(name, shape, dt))

        ps = top.enter_context(nc.psum_tensor("ps", [P, 8, HALF], F32))
        ticks = sem("ticks")

        def apart(eng):
            eng.sem_inc(ticks, 1)

        ident = sb("ident", [P, P])
        ones = sb("ones", [P, P])
        head_mean = sb("head_mean", [P, P])
        tri16 = sb("tri16", [P, P])
        before = sb("before", [P, P])
        load_small = sem("load_small")
        g1_sb = sb("g1_sb", [P, KD])
        qg_sb = sb("qg_sb", [P, A_PAIRS + 1])
        kg_sb = sb("kg_sb", [P, A_PAIRS + 1])
        bog_sb = sb("bog_sb", [P, B_H])
        lgt = sb("lgt", [P, T, NG + NE])
        eps_sb = sb("eps_sb", [P, 1])
        c_pool = sem("c_pool")
        c_dve = sem("c_dve")
        w_v_in = [sem(f"w_v_in{g}") for g in range(3)]

        yaT = sb("yaT", [P, A_W // P, SEQ])
        ybT = sb("ybT", [P, B_V // P, SEQ])
        hT = sb("hT", [P, KD, SEQ])

        mid = ExitStack()
        va = sb("va", [P, T, A_W], ctx=mid)
        vb = sb("vb", [P, T, B_V], ctx=mid)
        rs = sb("rs", [P, T, B_V], ctx=mid)

        with ExitStack() as st:
            wv_sb = sb("wv_sb", [P, KD, 3 * HALF], ctx=st)
            xin = [sb(f"xin{u}", [P, D], ctx=st) for u in range(2)]
            hn = [sb(f"hn{u}", [P, D], ctx=st) for u in range(2)]
            hst = [sb(f"hst{u}", [P, KD, P], ctx=st) for u in range(2)]
            junk = sb("junk_a", [P, D], ctx=st)
            msq = sb("msq", [P, 2], ctx=st)
            rstd = sb("rstd", [P, 2], ctx=st)
            sg = [sb(f"sg{u}", [P, HALF], ctx=st) for u in range(2)]
            x_in = [sem(f"x_in{u}") for u in range(2)]
            msq_ready = sem("msq_ready")
            rms_ready = sem("rms_ready")
            rstd_ready = sem("rstd_ready")
            hn_ready = sem("hn_ready")
            hT_psum = sem("hT_psum")
            hst_ready = sem("hst_ready")
            hT_copied = sem("hT_copied")
            v_psum = sem("v_psum")
            va_done = sem("va_done")
            vb_done = sem("vb_done")
            rs_done = sem("rs_done")
            sg_ready = sem("sg_ready")
            psT = [ps[:, 0:2, :].rearrange("p b c -> p (b c)"), ps[:, 2:4, :].rearrange("p b c -> p (b c)")]

            with nc.Block() as block:
                @block.sync
                def _(sp):
                    for dst, src in ((g1_sb[:], g1), (qg_sb[:, 0:A_PAIRS], qg), (kg_sb[:, 0:A_PAIRS], kg),
                                     (bog_sb[:], bog)):
                        sp.dma_start(dst, src).then_inc(load_small, 16)
                    for u in range(2):
                        sp.dma_start(xin[u][:], x_t[u]).then_inc(x_in[u], 16)
                    for g in range(3):
                        cols = slice(g * HALF, (g + 1) * HALF)
                        sp.dma_start(wv_sb[:, :, cols], wv[:, :, cols]).then_inc(w_v_in[g], 16)
                    with sp.Fori(1, T // 2) as i:
                        for u in range(2):
                            sp.wait_ge(hn_ready, i * 2 + u + 1)
                            sp.dma_start(xin[u][:], x_t[i * 2 + u]).then_inc(x_in[u], 16)

                @block.scalar
                def _(act):
                    act.sem_inc(va_done, 1)
                    act.sem_inc(vb_done, 1)
                    act.wait_ge(c_pool, 10)
                    with act.Fori(0, T // 2) as i:
                        for u in range(2):
                            act.wait_ge(x_in[u], i * 16 + 16)
                            act.wait_ge(hn_ready, i * 2 + u + 1)
                            nc.scalar.activation(junk[:], xin[u][:], ACT.Square, scale=D ** -0.5,
                                                 accum_out=msq[:, u:u + 1]).then_inc(msq_ready, 1)
                            act.wait_ge(msq_ready, i * 2 + u + 1)
                            nc.scalar.activation(msq[:, u:u + 1], msq[:, u:u + 1], ACT.Sqrt,
                                                 bias=eps_sb[:]).then_inc(rms_ready, 1)
                        for u in range(2):
                            t = i * 2 + u
                            act.wait_ge(v_psum, t * 3 + 1)
                            nc.scalar.copy(va[:, t, :], ps[:, 4, :]).then_inc(va_done, 1)
                            act.wait_ge(v_psum, t * 3 + 2)
                            nc.scalar.copy(vb[:, t, :], ps[:, 5, :]).then_inc(vb_done, 1)
                            act.wait_ge(v_psum, t * 3 + 3)
                            nc.scalar.activation(sg[u][:], ps[:, 6, :], ACT.Sigmoid).then_inc(sg_ready, 1)

                @block.gpsimd
                def _(pool):
                    pool.sem_inc(hT_copied, 2)
                    link = Chain(pool, c_pool)
                    link(nc.gpsimd.memset(ident[:], 0.0))
                    link(nc.gpsimd.affine_select(out=ident[:], in_=ident[:], compare_op=ALU.not_equal, fill=1.0,
                                                 base=0, pattern=[[-1, P]], channel_multiplier=1))
                    link(nc.gpsimd.memset(ones[:], 1.0))
                    link(nc.gpsimd.memset(eps_sb[:], EPS))
                    link(nc.gpsimd.memset(head_mean[:], 0.0))
                    for h in range(2):
                        link(nc.gpsimd.memset(head_mean[h * A_D:(h + 1) * A_D, h * A_D:(h + 1) * A_D], 1.0 / A_D))
                    link(nc.gpsimd.memset(tri16[:], 1.0 / GATE_TEMP))
                    link(nc.gpsimd.affine_select(out=tri16[:], in_=tri16[:], compare_op=ALU.is_ge, fill=0.0,
                                                 base=0, pattern=[[1, P]], channel_multiplier=-1))
                    link(nc.gpsimd.affine_select(out=before[:], in_=ones[:], compare_op=ALU.is_gt, fill=0.0,
                                                 base=0, pattern=[[1, P]], channel_multiplier=-1))
                    with pool.Fori(0, T // 2) as i:
                        for u in range(2):
                            t = i * 2 + u
                            pool.wait_ge(hst_ready, t + 3)
                            nc.gpsimd.tensor_copy(hT[:, :, bass.ds(t * P, P)], hst[u][:]).then_inc(hT_copied, 1)

                @block.vector
                def _(dve):
                    dve.sem_inc(hn_ready, 2)
                    dve.sem_inc(hst_ready, 2)
                    dve.sem_inc(rs_done, 1)
                    dve.wait_ge(load_small, 64)
                    with dve.Fori(0, T // 2) as i:
                        for u in range(2):
                            t = i * 2 + u
                            dve.wait_ge(rms_ready, t + 1)
                            nc.vector.reciprocal(rstd[:, u:u + 1], msq[:, u:u + 1]).then_inc(rstd_ready, 1)
                            dve.wait_ge(rstd_ready, t + 1)
                            dve.wait_ge(hst_ready, t + 1)
                            nc.vector.tensor_scalar(hn[u][:], xin[u][:], rstd[:, u:u + 1], None,
                                                    ALU.mult).then_inc(hn_ready, 1)
                        for u in range(2):
                            t = i * 2 + u
                            dve.wait_ge(hT_psum, t + 1)
                            dve.wait_ge(hT_copied, t + 1)
                            nc.vector.tensor_tensor(hst[u][:], psT[u].rearrange("p (k c) -> p k c", k=KD),
                                                    g1_sb[:].unsqueeze(2).broadcast_to([P, KD, P]),
                                                    ALU.mult).then_inc(hst_ready, 1)
                        for u in range(2):
                            t = i * 2 + u
                            dve.wait_ge(sg_ready, t + 1)
                            nc.vector.tensor_tensor(rs[:, t, :], ps[:, 6, :], sg[u][:], ALU.mult).then_inc(rs_done, 1)

                @block.tensor
                def _(pe):
                    pe.wait_ge(c_pool, 10)
                    with pe.Fori(0, T // 2) as i:
                        for u in range(2):
                            t = i * 2 + u
                            pe.wait_ge(hn_ready, t + 3)
                            for k in range(KD):
                                mm = pe.transpose(psT[u][:, k * P:(k + 1) * P], hn[u][:, k * P:(k + 1) * P], ident[:])
                            mm.then_inc(hT_psum, 1)
                        for u in range(2):
                            t = i * 2 + u
                            pe.wait_ge(hst_ready, t + 3)
                            for g, freed in enumerate((va_done, vb_done, rs_done)):
                                pe.wait_ge(w_v_in[g], 16)
                                pe.wait_ge(freed, t + 1)
                                for k in range(KD):
                                    mm = pe.matmul(ps[:, 4 + g, :], hst[u][:, k, :],
                                                   wv_sb[:, k, g * HALF:(g + 1) * HALF],
                                                   start=(k == 0), stop=(k == KD - 1))
                                mm.then_inc(v_psum, 1)

        UN = 2 * T
        BU = 2 * UN
        ahead = ExitStack()
        w_sb = [sb(f"w_sb{u}", [P, KD, 2 * P], ctx=ahead) for u in range(2)]
        raw = sb("raw", [P, 2, 2, SEQ], ctx=ahead)
        w_in = [sem(f"w_in{u}") for u in range(2)]
        with ExitStack() as st:
            qn = [sb(f"qn{u}", [P, SEQ], ctx=st) for u in range(2)]
            kn = [sb(f"kn{u}", [P, SEQ], ctx=st) for u in range(2)]
            sq = sb("sq", [P, 2, SEQ], ctx=st)
            bias = [sb(f"bias{u}", [P, 2, BANDW], ctx=st) for u in range(2)]
            ng = [sb(f"ng{u}", [P, BANDW], ctx=st) for u in range(2)]
            pr = [sb(f"pr{u}", [P, BANDW], ctx=st) for u in range(2)]
            prT = [sb(f"prT{u}", [P, BANDW], ctx=st) for u in range(2)]
            nmax = sb("nmax", [P, 2], ctx=st)
            rsum = sb("rsum", [P, 4], ctx=st)
            rinv = sb("rinv", [P, 2], ctx=st)
            ya = [sb(f"ya{u}", [P, P], ctx=st) for u in range(2)]
            bias_in = [sem(f"bias_in{u}") for u in range(2)]
            nx_psum = sem("nx_psum")
            nx_taken = sem("nx_taken")
            raw_sq = sem("raw_sq")
            masked = sem("masked")
            logs = sem("logs")
            roots = sem("roots")
            band_dve = sem("band_dve")
            norm_done = sem("norm_done")
            score_psum = sem("score_psum")
            neg_ready = sem("neg_ready")
            prob_ready = sem("prob_ready")
            probT_psum = sem("probT_psum")
            probT_ready = sem("probT_ready")
            pv_psum = sem("pv_psum")
            ya_ready = sem("ya_ready")
            last_psum = sem("last_psum")
            yaT_done = sem("yaT_done")

            def unit(m):
                t = m % UN // 2
                n = min(t + 1, BAND_T)
                return m // UN, t, m % 2, t + 1 - n, n

            s_ps = [ps[:, 0:2, :].rearrange("p b c -> p (b c)"), ps[:, 2:4, :].rearrange("p b c -> p (b c)")]
            tr_ps = ps[:, 4:6, :].rearrange("p b c -> p (b c)")
            yT_ps = ps[:, 5, P:2 * P]
            share = [4, 4, 3, 3, 2, 3, 3, 2]
            PROJ_U = len(share)
            mm_of = [range(KD + sum(share[:u]), KD + sum(share[:u + 1])) for u in range(PROJ_U)]
            group_end = {u: m[-1] // KD for u, m in enumerate(mm_of) if (m[-1] + 1) % KD == 0}
            ROOT_U = PROJ_U + 4

            with nc.Block() as block:
                @block.sync
                def _(sp):
                    for u in range(2):
                        sp.dma_start(w_sb[u][:], wqk[u]).then_inc(w_in[u], 16)

                    def load_bias(pair, u):
                        sp.dma_start(bias[u][0:CHUNK, :, 0:BANDW - CHUNK],
                                     relx[pair, 0:CHUNK, :, 0:BANDW - CHUNK]).then_inc(bias_in[u], 16)
                        sp.dma_start(bias[u][CHUNK:P, :, CHUNK:BANDW],
                                     relx[pair, CHUNK:P, :, CHUNK:BANDW]).then_inc(bias_in[u], 16)

                    for u in range(2):
                        load_bias(u, u)
                    for pair in range(2, A_PAIRS + 2):
                        u = pair % 2
                        sp.wait_ge(nx_psum, (pair - 2) * 8 + 4)
                        sp.dma_start(w_sb[u][:], wqk[pair]).then_inc(w_in[u], 16)
                        if pair < A_PAIRS:
                            sp.wait_ge(neg_ready, (pair - 1) * UN + 2)
                            load_bias(pair, u)

                @block.tensor
                def _(pe):
                    pe.sem_inc(probT_psum, 2)
                    pe.sem_inc(pv_psum, 2)

                    def project(par, uses, n):
                        g, k = n // KD, n % KD
                        if k == 0:
                            pe.wait_ge(nx_taken, uses + g + 1)
                        mm = pe.matmul(ps[:, 7, :], w_sb[par][:, k, (g // 2) * P:(g // 2 + 1) * P],
                                       hT[:, k, (g % 2) * HALF:(g % 2 + 1) * HALF],
                                       start=(k == 0), stop=(k == KD - 1))
                        if k == KD - 1:
                            mm.then_inc(nx_psum, 1)

                    def mean_square(uses, n0, j):
                        pe.wait_ge(raw_sq, n0 + j + 1)
                        pe.wait_ge(nx_taken, uses + 4 + j + 1)
                        pe.matmul(ps[:, 7, :], head_mean[:], sq[:, j // 2, (j % 2) * HALF:(j % 2 + 1) * HALF],
                                  start=True, stop=True).then_inc(nx_psum, 1)

                    pe.wait_ge(w_in[0], 16)
                    for n in range(4 * KD):
                        project(0, 0, n)
                    for j in range(4):
                        mean_square(0, 0, j)
                    pe.wait_ge(w_in[1], 16)
                    for n in range(KD):
                        project(1, 8, n)
                    with pe.Fori(0, A_PAIRS // 2) as i:
                        n0 = i * BU
                        for s in range(BU + 2):
                            if s < BU:
                                pp, t, h, k0, nk = unit(s)
                                nxt = i * 2 + pp + 1
                                su = s % UN
                                if su == 0:
                                    pe.wait_ge(norm_done, (i * 2 + pp) * 2 + 2)
                                hd = slice(h * A_D, (h + 1) * A_D)
                                pe.wait_ge(neg_ready, n0 + s + 1)
                                for c in range(0, nk * P, HALF):
                                    w = min(HALF, nk * P - c)
                                    mm = pe.matmul(s_ps[s % 2][:, c:c + w], qn[pp][hd, t * P:(t + 1) * P],
                                                   kn[pp][hd, k0 * P + c:k0 * P + c + w], start=True, stop=True)
                                mm.then_inc(score_psum, 1)
                                if su < PROJ_U:
                                    for n in mm_of[su]:
                                        project(1 - pp, nxt * 8, n)
                                elif su < PROJ_U + 4:
                                    mean_square(nxt * 8, nxt * 4, su - PROJ_U)
                                elif su == ROOT_U:
                                    pe.wait_ge(w_in[pp], i * 16 + 32)
                                    for n in range(KD):
                                        project(pp, nxt * 8 + 8, n)
                            if 0 <= s - 1 < BU:
                                m = s - 1
                                pp, t, h, k0, nk = unit(m)
                                pe.wait_ge(prob_ready, n0 + m + 3)
                                pe.wait_ge(probT_ready, n0 + m + 1)
                                for j in range(nk):
                                    mm = pe.transpose(tr_ps[:, j * P:(j + 1) * P], pr[m % 2][:, j * P:(j + 1) * P],
                                                      ident[:])
                                if m == 0:
                                    pe.wait_ge(yaT_done, i * 2 * T + 1)
                                if m >= 3 and m % 2 == 1:
                                    pe.wait_ge(ya_ready, n0 + m + 3)
                                    mm = pe.transpose(yT_ps, ya[(m - 3) // 2 % 2][:], ident[:])
                                mm.then_inc(probT_psum, 1)
                            if 0 <= s - 2 < BU:
                                m = s - 2
                                pp, t, h, k0, nk = unit(m)
                                pe.wait_ge(probT_ready, n0 + m + 2)
                                pe.wait_ge(ya_ready, n0 + m + 4)
                                for j in range(nk):
                                    mm = pe.matmul(ps[:, 6, h * A_D:(h + 1) * A_D], prT[m % 2][:, j * P:(j + 1) * P],
                                                   va[:, k0 + j, bass.ds((i * 2 + pp) * P + h * A_D, A_D)],
                                                   start=(j == 0), stop=(j == nk - 1))
                                mm.then_inc(pv_psum, 1)
                        pe.wait_ge(ya_ready, n0 + BU + 4)
                        pe.transpose(yT_ps, ya[1][:], ident[:]).then_inc(last_psum, 1)

                @block.scalar
                def _(act):
                    act.sem_inc(prob_ready, 2)
                    act.sem_inc(probT_ready, 1)
                    act.sem_inc(yaT_done, 1)
                    act.sem_inc(nx_taken, 1)

                    def take_projection(par, uses, g):
                        act.wait_ge(nx_psum, uses + g + 1)
                        cols = slice((g % 2) * HALF, (g % 2 + 1) * HALF)
                        nc.scalar.activation(sq[:, g // 2, cols], ps[:, 7, :], ACT.Square).then_inc(raw_sq, 1)
                        nc.scalar.copy(raw[:, par, g // 2, cols], ps[:, 7, :]).then_inc(nx_taken, 1)

                    def take_mean_square(uses, j):
                        act.wait_ge(nx_psum, uses + 4 + j + 1)
                        nc.scalar.copy(sq[:, j // 2, (j % 2) * HALF:(j % 2 + 1) * HALF],
                                       ps[:, 7, :]).then_inc(nx_taken, 1)

                    def take_roots(pair):
                        act.wait_ge(nx_taken, pair * 8 + 9)
                        nc.scalar.activation(sq[:], sq[:], ACT.Ln, bias=eps_sb[:]).then_inc(logs, 1)
                        act.wait_ge(logs, pair + 1)
                        nc.scalar.activation(sq[:], sq[:], ACT.Exp, scale=-0.5).then_inc(roots, 1)

                    def take_tile(i, tt):
                        nc.scalar.activation(yaT[:, i * 2 + tt // T, (tt % T) * P:(tt % T + 1) * P], yT_ps,
                                             ACT.Copy).then_inc(yaT_done, 1)

                    for g in range(4):
                        take_projection(0, 0, g)
                    for j in range(4):
                        take_mean_square(0, j)
                    take_roots(0)
                    act.wait_ge(norm_done, 2)
                    take_projection(1, 8, 0)
                    with act.Fori(0, A_PAIRS // 2) as i:
                        n0 = i * BU
                        for s in range(BU + 1):
                            if s < BU:
                                pp, t, h, k0, nk = unit(s)
                                w = nk * P
                                su, nxt = s % UN, i * 2 + pp + 1
                                if su - 1 in group_end:
                                    take_projection(1 - pp, nxt * 8, group_end[su - 1])
                                if su == ROOT_U + 1:
                                    act.wait_ge(norm_done, nxt * 2 + 2)
                                    take_projection(pp, nxt * 8 + 8, 0)
                                act.wait_ge(neg_ready, n0 + s + 3)
                                act.wait_ge(probT_psum, n0 + s + 1)
                                act.wait_ge(ya_ready, n0 + s + 1)
                                nc.scalar.activation(pr[s % 2][:, :w], ng[s % 2][:, :w], ACT.Exp,
                                                     bias=nmax[:, s % 2:s % 2 + 1], scale=-1.0,
                                                     accum_out=rsum[:, s % 4:s % 4 + 1]).then_inc(prob_ready, 1)
                                if 0 <= su - PROJ_U < 4:
                                    take_mean_square(nxt * 8, su - PROJ_U)
                            if 0 <= s - 1 < BU:
                                m = s - 1
                                w = unit(m)[4] * P
                                act.wait_ge(probT_psum, n0 + m + 3)
                                if m >= 3 and m % 2 == 1:
                                    take_tile(i, (m - 3) // 2)
                                act.wait_ge(pv_psum, n0 + m + 1)
                                nc.scalar.copy(prT[m % 2][:, :w], tr_ps[:, :w]).then_inc(probT_ready, 1)
                            if s < BU and s % UN == ROOT_U - 1:
                                take_roots(i * 2 + s // UN + 1)
                        act.wait_ge(last_psum, i + 1)
                        apart(act)
                        take_tile(i, 2 * T - 1)

                @block.vector
                def _(dve):
                    dve.sem_inc(neg_ready, 2)
                    dve.sem_inc(ya_ready, 4)
                    link0 = Chain(dve, c_dve)
                    link0(nc.vector.memset(qg_sb[:, A_PAIRS:], 1.0))
                    link0(nc.vector.memset(kg_sb[:, A_PAIRS:], 1.0))
                    link0(nc.vector.tensor_scalar(qg_sb[:], qg_sb[:], A_D ** -0.5, None, ALU.mult))
                    for u in range(2):
                        nc.vector.memset(bias[u][0:CHUNK, :, BANDW - CHUNK:BANDW], NEG).then_inc(masked, 1)
                        nc.vector.memset(bias[u][CHUNK:P, :, 0:CHUNK], NEG).then_inc(masked, 1)
                    dve.wait_ge(masked, 4)

                    def norm(pair, par, b):
                        gain, dst = ((qg_sb, qn), (kg_sb, kn))[b]
                        dve.wait_ge(roots, pair + 1)
                        nc.vector.scalar_tensor_tensor(out=dst[par][:], in0=raw[:, par, b, :],
                                                       scalar=gain[:, bass.ds(pair, 1)], in1=sq[:, b, :],
                                                       op0=ALU.mult, op1=ALU.mult).then_inc(norm_done, 1)

                    norm(0, 0, 0)
                    norm(0, 0, 1)
                    with dve.Fori(0, A_PAIRS // 2) as i:
                        n0 = i * BU
                        link = Chain(dve, band_dve, i * BU)
                        for s in range(BU + 2):
                            if s < BU:
                                pp, t, h, k0, nk = unit(s)
                                w = nk * P
                                dve.wait_ge(score_psum, n0 + s + 1)
                                if s % UN == 0:
                                    dve.wait_ge(bias_in[pp], i * 32 + 32)
                                dve.wait_ge(prob_ready, n0 + s + 1)
                                apart(dve)
                                nc.vector.tensor_tensor_reduce(
                                    out=ng[s % 2][:, :w], in0=s_ps[s % 2][:, :w], in1=bias[pp][:, s % 2, BANDW - w:BANDW],
                                    scale=-1.0, scalar=1e38, op0=ALU.add, op1=ALU.min,
                                    accum_out=nmax[:, s % 2:s % 2 + 1]).then_inc(neg_ready, 1)
                            if 0 <= s - 2:
                                m = s - 2
                                pp, t, h, k0, nk = unit(m)
                                dve.wait_ge(pv_psum, n0 + m + 3)
                                link(nc.vector.reciprocal(rinv[:, h:h + 1], rsum[:, m % 4:m % 4 + 1]))
                                dve.wait_ge(probT_psum, n0 + m // 2 * 2 + 2)
                                if m // 2 == 1:
                                    dve.wait_ge(yaT_done, i * 2 * T + 1)
                                nc.vector.tensor_scalar(ya[t % 2][:, h * A_D:(h + 1) * A_D],
                                                        ps[:, 6, h * A_D:(h + 1) * A_D], rinv[:, h:h + 1], None,
                                                        ALU.mult).then_inc(ya_ready, 1)
                            if s < BU and s % UN == ROOT_U:
                                for b in range(2):
                                    norm(i * 2 + s // UN + 1, 1 - s // UN, b)

        with ExitStack() as st:
            wlr_sb = sb("wlr_sb", [P, KD, RANK], ctx=st)
            gup_sb = sb("gup_sb", [RANK, B_QK], ctx=st)
            gbias_sb = sb("gbias_sb", [1, B_QK], ctx=st)
            lrT = sb("lrT", [RANK, SEQ], ctx=st)
            masks = sb("masks", [P, LEVELS, P], I32, ctx=st)
            ii = sb("ii", [P, P], I32, ctx=st)
            jj = sb("jj", [P, P], I32, ctx=st)
            vf = sb("vf", [P, P], ctx=st)
            tf = sb("tf", [P, P], ctx=st)
            bq = sb("bq", [P, SEQ], ctx=st)
            bk = sb("bk", [P, SEQ], ctx=st)
            gm = sb("gm", [P, SEQ], ctx=st)
            t1 = sb("t1", [P, SEQ], ctx=st)
            t2 = sb("t2", [P, SEQ], ctx=st)
            gl = sb("gl", [P, SEQ], ctx=st)
            cum = sb("cum", [P, SEQ], ctx=st)
            qe = sb("qe", [P, SEQ], ctx=st)
            kdT = w_sb[0][:, 4:8, :].rearrange("p k (a c) -> p (k a) c", c=P)
            df = [sb(f"df{u}", [P, SEQ], ctx=st) for u in range(2)]
            ef = [t1, t2]
            att = va[:, 0:4, :].rearrange("p t (a c) -> p (t a) c", c=P)
            ql = [gm, va[:, 4:6, :].rearrange("p t c -> p (t c)")]
            kl = [gl, va[:, 6:8, :].rearrange("p t c -> p (t c)")]
            state = [sb(f"state{u}", [P, P], ctx=st) for u in range(2)]
            elast = sb("elast", [P, T], ctx=st)
            junk = sb("junk_g", [P, 2, P], ctx=st)
            oms = sb("oms", [P, 2, 2], ctx=st)
            ors = sb("ors", [P, 2, 2], ctx=st)
            yb = [w_sb[0][:, u, :] for u in range(2)]
            g_small = sem("g_small")
            g_consts = sem("g_consts")
            iota_ready = sem("iota_ready")
            lr_psum = sem("lr_psum")
            lr_ready = sem("lr_ready")
            g_qk_psum = sem("g_qk_psum")
            g_raw_ready = sem("g_raw_ready")
            z_psum = sem("z_psum")
            g_qk_ready = sem("g_qk_ready")
            sp_act = sem("softplus_act")
            gla_dve = sem("gla_dve")
            decay_ready = sem("decay_ready")
            cum_psum = sem("cum_psum")
            cum_ready = sem("cum_ready")
            tail_diff = sem("tail_diff")
            head_exp = sem("head_exp")
            tail_exp = sem("tail_exp")
            kd_ready = sem("kd_ready")
            kd_psum = sem("kd_psum")
            kdT_ready = sem("kdT_ready")
            diff_ready = sem("diff_ready")
            exp_ready = sem("exp_ready")
            lev_ready = sem("lev_ready")
            lev_psum = sem("lev_psum")
            att_part = sem("att_part")
            o_psum = sem("o_psum")
            u_psum = sem("u_psum")
            st_ready = sem("st_ready")
            oms_ready = sem("oms_ready")
            orms_ready = sem("orms_ready")
            yb_ready = sem("yb_ready")
            ybT_psum = sem("ybT_psum")
            ybT_done = sem("ybT_done")
            two = lambda b: ps[:, b:b + 2, :].rearrange("p b c -> p (b c)")
            NL = LEVELS - 1

            with nc.Block() as block:
                @block.sync
                def _(sp):
                    sp.dma_start(wlr_sb[:], wlr).then_inc(g_small, 16)
                    sp.dma_start(gup_sb[:], gup).then_inc(g_small, 16)
                    sp.dma_start(gbias_sb[:], gbias).then_inc(g_small, 16)

                @block.gpsimd
                def _(pool):
                    nc.gpsimd.iota(ii[:], pattern=[[1, P]], base=0, channel_multiplier=0).then_inc(iota_ready, 1)
                    nc.gpsimd.iota(jj[:], pattern=[[0, P]], base=0, channel_multiplier=1).then_inc(iota_ready, 1)

                @block.tensor
                def _(pe):
                    pe.sem_inc(ybT_psum, 2)
                    pe.wait_ge(g_small, 48)
                    for half in range(2):
                        for k in range(KD):
                            mm = pe.matmul(ps[0:RANK, 6 + half, :], wlr_sb[:, k, :],
                                           hT[:, k, half * HALF:(half + 1) * HALF],
                                           start=(k == 0), stop=(k == KD - 1))
                    mm.then_inc(lr_psum, 1)
                    pe.wait_ge(w_in[1], 48)

                    def project_second(b):
                        for half in range(1 - b, 2):
                            for k in range(KD):
                                mm = pe.matmul(ps[:, 2 * b + half, :], w_sb[1][:, k, b * P:(b + 1) * P],
                                               hT[:, k, half * HALF:(half + 1) * HALF],
                                               start=(k == 0), stop=(k == KD - 1))
                        mm.then_inc(g_qk_psum, 1)

                    with pe.Fori(0, B_PAIRS) as p:
                        pe.wait_ge(ybT_done, p * T + 2)
                        pe.wait_ge(lr_ready, 1)
                        for t in range(T):
                            z = ps[:, 4 + t // 4, (t % 4) * P:(t % 4 + 1) * P]
                            pe.matmul(z, lrT[:, t * P:(t + 1) * P], gup_sb[:, bass.ds(p * P, P)],
                                      start=True, stop=False)
                            mm = pe.matmul(z, ones[0:1, :], gbias_sb[:, bass.ds(p * P, P)], start=False, stop=True)
                        mm.then_inc(z_psum, 1)
                        with pe.If(p < 1):
                            project_second(0)
                        pe.wait_ge(decay_ready, p + 1)
                        for t in range(T):
                            mm = pe.matmul(ps[:, 6 + t // 4, (t % 4) * P:(t % 4 + 1) * P], gl[:, t * P:(t + 1) * P],
                                           tri16[:], start=True, stop=True)
                        mm.then_inc(cum_psum, 1)
                        with pe.If(p < 1):
                            project_second(1)
                        pe.wait_ge(kd_ready, p + 1)
                        for t in range(T):
                            mm = pe.transpose(ps[:, 4 + t // 4, (t % 4) * P:(t % 4 + 1) * P],
                                              df[0][:, t * P:(t + 1) * P], ident[:])
                        mm.then_inc(kd_psum, 1)
                        pe.wait_ge(g_raw_ready, 2)
                        for l in range(LEVELS):
                            pe.wait_ge(lev_ready, p * LEVELS + l + 1)
                            if l == 1:
                                pe.wait_ge(kdT_ready, p + 1)
                            if l >= 2:
                                pe.wait_ge(att_part, p * LEVELS + l - 1)
                            kk, qq = (bk, bq) if l == 0 else (kl[l % 2], ql[l % 2])
                            for n in range(2 * T):
                                t, h = n % T, n // T
                                hd = slice(h * B_DK, (h + 1) * B_DK)
                                mm = pe.matmul(ps[:, (l % 2) * 4 + n // 4, (n % 4) * P:(n % 4 + 1) * P],
                                               kk[hd, t * P:(t + 1) * P], qq[hd, t * P:(t + 1) * P],
                                               start=True, stop=True)
                            mm.then_inc(lev_psum, 1)
                        pe.wait_ge(att_part, p * LEVELS + LEVELS)
                        for t in range(T + 1):
                            if t < T:
                                pe.wait_ge(yb_ready, p * T + t + 1)
                                if t >= 1:
                                    pe.wait_ge(st_ready, p * T + t)
                                for h in range(2):
                                    hd = slice(h * B_DK, (h + 1) * B_DK)
                                    o = ps[:, (t % 2) * 2 + h, 0:P]
                                    mm = pe.matmul(o, att[:, h * T + t, :], vb[:, t, bass.ds(p * 2 * P + h * P, P)],
                                                   start=True, stop=(t == 0))
                                    if t >= 1:
                                        mm = pe.matmul(o, qe[hd, t * P:(t + 1) * P], state[(t - 1) % 2][hd, :],
                                                       start=False, stop=True)
                                mm.then_inc(o_psum, 1)
                                pe.matmul(ps[:, 4 + t % 2, 0:2 * P], kdT[:, t, :], vb[:, t, bass.ds(p * 2 * P, 2 * P)],
                                          start=True, stop=True).then_inc(u_psum, 1)
                            if t >= 1:
                                m = t - 1
                                pe.wait_ge(yb_ready, p * T + m + 3)
                                pe.wait_ge(ybT_done, p * T + m + 1)
                                for h in range(2):
                                    mm = pe.transpose(ps[:, 6 + m % 2, h * P:(h + 1) * P],
                                                      yb[m % 2][:, h * P:(h + 1) * P], ident[:])
                                mm.then_inc(ybT_psum, 1)

                @block.scalar
                def _(act):
                    act.sem_inc(g_qk_ready, 1)
                    act.wait_ge(lr_psum, 1)
                    nc.scalar.copy(lrT[:], ps[0:RANK, 6:8, :].rearrange("p b c -> p (b c)")).then_inc(lr_ready, 1)
                    act.sem_inc(g_raw_ready, 1)
                    with act.Fori(0, B_PAIRS) as p:
                        act.wait_ge(g_raw_ready, p + 1)
                        act.wait_ge(yb_ready, p * T + 2)
                        rw = raw[:, bass.ds(p, 1), :, :].squeeze(1)
                        nc.scalar.activation(bq[:], rw[:, 0, :], ACT.Copy, scale=B_DK ** -0.5).then_inc(g_qk_ready, 1)
                        nc.scalar.activation(bk[:], rw[:, 1, :], ACT.Copy).then_inc(g_qk_ready, 1)
                        act.wait_ge(z_psum, p + 1)
                        link = Chain(act, sp_act, p * 3)
                        link(nc.scalar.activation(t1[:], two(4), ACT.Abs))
                        link(nc.scalar.activation(t2[:], t1[:], ACT.Exp, scale=-1.0))
                        link(nc.scalar.activation(gl[:], t2[:], ACT.Ln, bias=1.0))
                        act.wait_ge(cum_ready, p + 1)
                        nc.scalar.activation(qe[:], cum[:], ACT.Exp).then_inc(head_exp, 1)
                        act.wait_ge(tail_diff, p + 1)
                        nc.scalar.activation(t2[:], t1[:], ACT.Exp).then_inc(tail_exp, 1)
                        act.wait_ge(kd_psum, p + 1)
                        nc.scalar.copy(kdT, two(4).rearrange("p (t c) -> p t c", c=P)).then_inc(kdT_ready, 1)
                        with act.If(p < 1):
                            act.wait_ge(g_qk_psum, 1)
                            nc.scalar.copy(raw[:, 1, 0, HALF:], ps[:, 1, :])
                            act.wait_ge(g_qk_psum, 2)
                            nc.scalar.copy(raw[:, 1, 1, :], two(2)).then_inc(g_raw_ready, 1)
                        for l in range(1, LEVELS):
                            act.wait_ge(diff_ready, p * NL + l)
                            nc.scalar.activation(ef[l % 2][:], df[l % 2][:], ACT.Exp).then_inc(exp_ready, 1)
                        for t in range(T):
                            act.wait_ge(o_psum, p * T + t + 1)
                            act.wait_ge(yb_ready, p * T + t + 1)
                            for h in range(2):
                                nc.scalar.activation(junk[:, h, :], ps[:, (t % 2) * 2 + h, 0:P], ACT.Square,
                                                     scale=B_DV ** -0.5,
                                                     accum_out=oms[:, t % 2, h:h + 1]).then_inc(oms_ready, 1)
                            act.wait_ge(oms_ready, (p * T + t) * 2 + 2)
                            nc.scalar.activation(oms[:, t % 2, :], oms[:, t % 2, :], ACT.Sqrt,
                                                 bias=eps_sb[:]).then_inc(orms_ready, 1)

                @block.vector
                def _(dve):
                    dve.sem_inc(yb_ready, 2)
                    dve.sem_inc(ybT_done, 2)
                    link = Chain(dve, g_consts)
                    dve.wait_ge(iota_ready, 2)
                    link(nc.vector.tensor_tensor(masks[:, 0, :], ii[:], jj[:], ALU.bitwise_xor))
                    link(nc.vector.tensor_copy(vf[:], masks[:, 0, :]))
                    link(nc.vector.tensor_tensor(tf[:], ii[:], jj[:], ALU.is_ge))
                    link(nc.vector.scalar_tensor_tensor(out=vf[:], in0=vf[:], scalar=1.0, in1=tf[:],
                                                        op0=ALU.add, op1=ALU.mult))
                    link(nc.vector.tensor_scalar(masks[:, 0, :], vf[:], 1.0, None, ALU.is_equal))
                    for l in range(1, LEVELS):
                        c = 1 << (l - 1)
                        link(nc.vector.tensor_scalar(tf[:], vf[:], float(2 * c + 1), None, ALU.is_lt))
                        link(nc.vector.scalar_tensor_tensor(out=masks[:, l, :], in0=vf[:], scalar=float(c + 1),
                                                            in1=tf[:], op0=ALU.is_ge, op1=ALU.mult))
                    link(nc.vector.memset(att[:], 0.0))
                    link(nc.vector.memset(ql[1][:], 0.0))
                    link(nc.vector.memset(kl[1][:], 0.0))

                    def halves(a, c):
                        v = a[:].rearrange("p (n s c) -> p n s c", s=2, c=c)
                        return v[:, :, 0, :], v[:, :, 1, :]

                    with dve.Fori(0, B_PAIRS) as p:
                        link = Chain(dve, gla_dve, p * (3 + NL * 3 + 4 * T))
                        dve.wait_ge(sp_act, p * 3 + 1)
                        link(nc.vector.tensor_scalar(gm[:], two(4), 0.0, None, ALU.min))
                        dve.wait_ge(sp_act, p * 3 + 3)
                        nc.vector.tensor_tensor(gl[:], gm[:], gl[:], ALU.subtract).then_inc(decay_ready, 1)
                        dve.wait_ge(cum_psum, p + 1)
                        nc.vector.tensor_copy(cum[:], two(6)).then_inc(cum_ready, 1)
                        dve.wait_ge(cum_ready, p + 1)
                        c3 = cum[:].rearrange("p (t c) -> p t c", c=P)
                        nc.vector.tensor_tensor(t1[:].rearrange("p (t c) -> p t c", c=P),
                                                c3[:, :, P - 1:P].broadcast_to([P, T, P]), c3,
                                                ALU.subtract).then_inc(tail_diff, 1)
                        dve.wait_ge(head_exp, p + 1)
                        link(nc.vector.tensor_copy(elast[:], qe[:].rearrange("p (t c) -> p t c", c=P)[:, :, P - 1]))
                        dve.wait_ge(g_qk_ready, p * 2 + 3)
                        link(nc.vector.tensor_tensor(qe[:], qe[:], bq[:], ALU.mult))
                        dve.wait_ge(tail_exp, p + 1)
                        nc.vector.tensor_tensor(df[0][:], bk[:], t2[:], ALU.mult).then_inc(kd_ready, 1)
                        dve.wait_ge(kd_psum, p + 1)
                        dve.sem_inc(lev_ready, 1)

                        def diff(l):
                            c = 1 << (l - 1)
                            lo, hi = halves(cum, c)
                            dlo, dhi = halves(df[l % 2], c)
                            ref = lo[:, :, c - 1:c].broadcast_to([P, SEQ // (2 * c), c])
                            link(nc.vector.tensor_tensor(dlo, ref, lo, ALU.subtract))
                            nc.vector.tensor_tensor(dhi, hi, ref, ALU.subtract).then_inc(diff_ready, 1)

                        def take(l):
                            dve.wait_ge(lev_psum, p * LEVELS + l + 1)
                            apart(dve)
                            b = (l % 2) * 4
                            nc.vector.copy_predicated(
                                att[:], masks[:, l:l + 1, :].broadcast_to([P, 2 * T, P]),
                                ps[:, b:b + 4, :].rearrange("p b (n c) -> p (b n) c", c=P)).then_inc(att_part, 1)

                        diff(1)
                        for l in range(1, LEVELS):
                            if l + 1 < LEVELS:
                                diff(l + 1)
                            c = 1 << (l - 1)
                            dve.wait_ge(exp_ready, p * NL + l)
                            elo, ehi = halves(ef[l % 2], c)
                            link(nc.vector.tensor_tensor(halves(kl[l % 2], c)[0], halves(bk, c)[0], elo, ALU.mult))
                            link(nc.vector.tensor_tensor(halves(ql[l % 2], c)[1], halves(bq, c)[1], ehi, ALU.mult))
                            dve.sem_inc(lev_ready, 1)
                            take(l - 1)
                            dve.wait_ge(att_part, p * LEVELS + l)
                        take(LEVELS - 1)
                        for t in range(T + 1):
                            if t < T:
                                dve.wait_ge(u_psum, p * T + t + 1)
                                for h in range(2):
                                    hd = slice(h * B_DK, (h + 1) * B_DK)
                                    u = ps[hd, 4 + t % 2, h * P:(h + 1) * P]
                                    if t == 0:
                                        ins = nc.vector.tensor_copy(state[0][hd, :], u)
                                    else:
                                        ins = nc.vector.scalar_tensor_tensor(
                                            out=state[t % 2][hd, :], in0=state[(t - 1) % 2][hd, :],
                                            scalar=elast[hd, t:t + 1], in1=u, op0=ALU.mult, op1=ALU.add)
                                    if h == 0:
                                        link(ins)
                                ins.then_inc(st_ready, 1)
                                dve.wait_ge(st_ready, p * T + t + 1)
                                dve.wait_ge(orms_ready, p * T + t + 1)
                                link(nc.vector.reciprocal(ors[:, t % 2, :], oms[:, t % 2, :]))
                                dve.wait_ge(ybT_psum, p * T + t + 1)
                                for h in range(2):
                                    ins = nc.vector.scalar_tensor_tensor(
                                        out=yb[t % 2][:, h * P:(h + 1) * P], in0=ps[:, (t % 2) * 2 + h, 0:P],
                                        scalar=ors[:, t % 2, h:h + 1], in1=rs[:, t, bass.ds(p * 2 * P + h * P, P)],
                                        op0=ALU.mult, op1=ALU.mult)
                                    if h == 0:
                                        link(ins)
                                ins.then_inc(yb_ready, 1)
                            if t >= 1:
                                m = t - 1
                                dve.wait_ge(ybT_psum, p * T + m + 3)
                                for h in range(2):
                                    ins = nc.vector.tensor_scalar(
                                        ybT[:, p * 2 + h, m * P:(m + 1) * P], ps[:, 6 + m % 2, h * P:(h + 1) * P],
                                        bog_sb[:, bass.ds(p * 2 + h, 1)], None, ALU.mult)
                                    if h == 0:
                                        link(ins)
                                ins.then_inc(ybT_done, 1)
        ahead.close()
        mid.close()

        mT = hT
        with ExitStack() as st:
            GATES = 2 * KD * P
            PA, PB = GATES, GATES + (A_W // P) * P
            WD = PB + (B_V // P) * P
            wd_sb = [sb(f"wd{u}", [P, WD], ctx=st) for u in range(2)]
            wH = [sb(f"wH{u}", [P, GATES], F32R, ctx=st) for u in range(2)]
            wL = [sb(f"wL{u}", [P, GATES], F32R, ctx=st) for u in range(2)]
            hH = sb("hH", [P, KD, SEQ], F32R, ctx=st)
            hL = sb("hL", [P, KD, SEQ], F32R, ctx=st)
            gs = [sb(f"gs{u}", [P, 2, HALF], ctx=st) for u in range(2)]
            m1 = sb("m1", [P, HALF], ctx=st)
            m2 = sb("m2", [P, HALF], ctx=st)
            wd_in = [sem(f"wd_in{u}") for u in range(2)]
            wH_ready = sem("wH_ready")
            wL_ready = sem("wL_ready")
            hH_ready = sem("hH_ready")
            hL_ready = sem("hL_ready")
            d_psum = sem("d_psum")
            gs_ready = sem("gs_ready")
            m_dve = sem("m_dve")
            m_done = sem("m_done")
            with nc.Block() as block:
                @block.sync
                def _(sp):
                    with sp.Fori(0, KD // 2) as i:
                        for u in range(2):
                            sp.wait_ge(d_psum, (i * 2 + u) * 2 + 2)
                            sp.dma_start(wd_sb[u][:], wd[i * 2 + u]).then_inc(wd_in[u], 16)

                @block.tensor
                def _(pe):
                    pe.sem_inc(d_psum, 4)

                    def branches(u, half):
                        cols = slice(half * HALF, (half + 1) * HALF)
                        for b, base, src in ((2, PA, yaT), (3, PB, ybT)):
                            for k in range(A_W // P):
                                mm = pe.matmul(ps[:, half * 4 + b, :], wd_sb[u][:, base + k * P:base + (k + 1) * P],
                                               src[:, k, cols], start=(k == 0), stop=(k == A_W // P - 1))
                        return mm

                    def gates(u, half, split):
                        cols = slice(half * HALF, (half + 1) * HALF)
                        for b in range(2):
                            for k in range(KD):
                                if split and b == 0:
                                    pe.wait_ge(hL_ready, k + 1)
                                piece = slice((b * KD + k) * P, (b * KD + k + 1) * P)
                                for n, (w, h) in enumerate(((wH, hH), (wH, hL), (wL, hH))):
                                    mm = pe.matmul(ps[:, half * 4 + b, :], w[u][:, piece], h[:, k, cols],
                                                   start=(k == 0 and n == 0), stop=(k == KD - 1 and n == 2))
                        return mm

                    def blk(d, u, n, split):
                        pe.wait_ge(wd_in[u], n * 16)
                        pe.wait_ge(m_done, d * 2 + 1)
                        branches(u, 0)
                        pe.wait_ge(wL_ready, d + 1)
                        gates(u, 0, split).then_inc(d_psum, 1)
                        pe.wait_ge(m_done, d * 2 + 2)
                        branches(u, 1)
                        gates(u, 1, False).then_inc(d_psum, 1)

                    for d in range(2):
                        blk(d, d, 1, d == 0)
                    with pe.Fori(1, KD // 2) as i:
                        for u in range(2):
                            blk(i * 2 + u, u, i + 1, False)

                @block.scalar
                def _(act):
                    def split_weights(u, n):
                        act.wait_ge(wd_in[u], n * 16)
                        nc.scalar.copy(wH[u][:], wd_sb[u][:, 0:GATES]).then_inc(wH_ready, 1)

                    def sigmoids(n, half):
                        act.wait_ge(d_psum, n + 5)
                        act.wait_ge(m_done, n + 1)
                        nc.scalar.activation(gs[half][:], ps[:, half * 4:half * 4 + 2, :],
                                             ACT.Sigmoid).then_inc(gs_ready, 1)

                    nc.scalar.copy(hH[:, 0, :], hT[:, 0, :]).then_inc(hH_ready, 1)
                    split_weights(0, 1)
                    for k in range(1, KD):
                        nc.scalar.copy(hH[:, k, :], hT[:, k, :]).then_inc(hH_ready, 1)
                    split_weights(1, 1)
                    for n in range(2):
                        sigmoids(n, n)
                    with act.Fori(1, KD // 2) as i:
                        for u in range(2):
                            split_weights(u, i + 1)
                            for half in range(2):
                                sigmoids((i * 2 + u - 1) * 2 + half, half)
                    for half in range(2):
                        sigmoids((KD - 1) * 2 + half, half)

                @block.vector
                def _(dve):
                    dve.sem_inc(m_done, 2)

                    def rest_of_weights(d, u):
                        dve.wait_ge(wH_ready, d + 1)
                        nc.vector.tensor_tensor(wL[u][:], wd_sb[u][:, 0:GATES], wH[u][:].bitcast(F32),
                                                ALU.subtract).then_inc(wL_ready, 1)

                    def merged(d, half):
                        n = d * 2 + half
                        link = Chain(dve, m_dve, n * 2)
                        dve.wait_ge(gs_ready, n + 1)
                        dve.wait_ge(m_done, n + 2)
                        link(nc.vector.tensor_tensor(m1[:], gs[half][:, 0, :], ps[:, half * 4 + 2, :], ALU.mult))
                        link(nc.vector.tensor_tensor(m2[:], gs[half][:, 1, :], ps[:, half * 4 + 3, :], ALU.mult))
                        nc.vector.tensor_tensor(mT[:, d, half * HALF:(half + 1) * HALF], m1[:], m2[:],
                                                ALU.add).then_inc(m_done, 1)

                    for k in range(KD):
                        dve.wait_ge(hH_ready, k + 1)
                        nc.vector.tensor_tensor(hL[:, k, :], hT[:, k, :], hH[:, k, :].bitcast(F32),
                                                ALU.subtract).then_inc(hL_ready, 1)
                        if k == 0:
                            rest_of_weights(0, 0)
                    dve.wait_ge(hL_ready, KD)
                    rest_of_weights(1, 1)
                    for half in range(2):
                        merged(0, half)
                    with dve.Fori(1, KD // 2) as i:
                        for u in range(2):
                            rest_of_weights(i * 2 + u, u)
                            for half in range(2):
                                merged(i * 2 + u - 1, half)
                    for half in range(2):
                        merged(KD - 1, half)

        x2 = sb("x2", [P, T, D])
        WR = 4
        FIRST = 2
        wgu_first = [sb(f"wgu{e}", [P, KD, 2, DE]) for e in range(FIRST)]
        wdn_first = [a[:, 0:2, :] for a in (yaT, ybT)]
        wgu_in = [sem(f"wgu_in{w}") for w in range(WR)]
        wdn_in = [sem(f"wdn_in{w}") for w in range(WR)]

        def load_gate_up(sp, dst, e, landed):
            sp.dma_start(dst[:, :, 0, :], wg_e[e]).then_inc(landed, 16)
            sp.dma_start(dst[:, :, 1, :], wu_e[e]).then_inc(landed, 16)

        def load_down(sp, dst, e, landed):
            sp.dma_start(dst[:, :, :], wn_e[e]).then_inc(landed, 16)

        with ExitStack() as st:
            wo_sb = sb("wo_sb", [P, KD, D], ctx=st)
            xin = [sb(f"xin2{u}", [P, D], ctx=st) for u in range(2)]
            mst = [sb(f"mst{u}", [P, KD, P], ctx=st) for u in range(2)]
            h2 = [sb(f"h2{u}", [P, D], ctx=st) for u in range(2)]
            h2T = sb("h2T", [P, KD, P], ctx=st)
            junk = sb("junk_p", [P, D], ctx=st)
            g2_sb = sb("g2_sb", [P, D], ctx=st)
            wr_sb = sb("wr_sb", [P, KD, NG + NE], ctx=st)
            br_sb = sb("br_sb", [P, NG + NE], ctx=st)
            msq = sb("msq2", [P, 2], ctx=st)
            rstd = sb("rstd2", [P, 2], ctx=st)
            wo_in = [sem(f"wo_in{n}") for n in range(KD // 2)]
            r_small = sem("r_small")
            x_in = [sem(f"x2_in{u}") for u in range(2)]
            m_staged = sem("m_staged")
            o_psum2 = sem("out_psum")
            x2_ready = sem("x2_ready")
            msq_ready = sem("msq2_ready")
            rms_ready = sem("rms2_ready")
            rstd_ready = sem("rstd2_ready")
            h2_ready = sem("h2_ready")
            h2_stored = [sem(f"h2_stored{u}") for u in range(2)]
            h2T_psum = sem("h2T_psum")
            h2T_ready = sem("h2T_ready")
            lg_psum = sem("lg_psum")
            lg_ready = sem("lg_ready")
            with nc.Block() as block:
                @block.sync
                def _(sp):
                    for k in range(0, KD, 2):
                        sp.dma_start(wo_sb[:, k:k + 2, :], wout[:, k:k + 2, :]).then_inc(wo_in[k // 2], 16)
                        if k < 4:
                            sp.dma_start(xin[k // 2][:], x_t[k // 2]).then_inc(x_in[k // 2], 16)
                    sp.dma_start(wr_sb[:], wr).then_inc(r_small, 16)
                    sp.dma_start(br_sb[:], br.partition_broadcast(P)).then_inc(r_small, 16)
                    sp.dma_start(g2_sb[:], g2p.partition_broadcast(P)).then_inc(r_small, 16)
                    with sp.Fori(1, T // 2) as i:
                        for u in range(2):
                            sp.wait_ge(x2_ready, i * 2 + u + 1)
                            sp.dma_start(xin[u][:], x_t[i * 2 + u]).then_inc(x_in[u], 16)
                    for e in range(FIRST):
                        load_gate_up(sp, wgu_first[e], e, wgu_in[e])
                        load_down(sp, wdn_first[e], e, wdn_in[e])

                @block.gpsimd
                def _(pool):
                    with pool.Fori(0, T // 2) as i:
                        for u in range(2):
                            t = i * 2 + u
                            pool.wait_ge(o_psum2, t + 1)
                            nc.gpsimd.tensor_copy(mst[u][:], mT[:, :, bass.ds(t * P, P)]).then_inc(m_staged, 1)

                @block.tensor
                def _(pe):
                    pe.sem_inc(o_psum2, 2)
                    pe.sem_inc(h2T_psum, 2)

                    def project(t, u, first=False):
                        pe.wait_ge(m_staged, t + 1)
                        pe.wait_ge(x2_ready, t + 1)
                        for n in range(2):
                            for k in range(KD):
                                if first and n == 0 and k % 2 == 0:
                                    pe.wait_ge(wo_in[k // 2], 16)
                                mm = pe.matmul(ps[:, 2 * u + n, :], mst[u][:, k, :],
                                               wo_sb[:, k, n * HALF:(n + 1) * HALF],
                                               start=(k == 0), stop=(k == KD - 1))
                        mm.then_inc(o_psum2, 1)

                    def transposes_h2(t, u):
                        pe.wait_ge(h2_ready, t + 1)
                        for k in range(KD):
                            mm = pe.transpose(ps[:, 4 + k // 4, (k % 4) * P:(k % 4 + 1) * P],
                                              h2[u][:, k * P:(k + 1) * P], ident[:])
                        mm.then_inc(h2T_psum, 1)

                    def logits(t):
                        pe.wait_ge(h2T_ready, t + 1)
                        pe.wait_ge(lg_ready, t + 1)
                        for k in range(KD):
                            mm = pe.matmul(ps[:, 6, 0:NG + NE], h2T[:, k, :], wr_sb[:, k, :],
                                           start=(k == 0), stop=(k == KD - 1))
                        mm.then_inc(lg_psum, 1)

                    project(0, 0, first=True)
                    project(1, 1)
                    pe.wait_ge(r_small, 48)
                    transposes_h2(0, 0)
                    with pe.Fori(1, T // 2) as i:
                        for u in range(2):
                            project(i * 2 + u, u)
                            logits(i * 2 + u - 2)
                            transposes_h2(i * 2 + u - 1, 1 - u)
                    logits(T - 2)
                    transposes_h2(T - 1, 1)
                    logits(T - 1)

                @block.scalar
                def _(act):
                    with act.Fori(0, T // 2) as i:
                        for u in range(2):
                            t = i * 2 + u
                            act.wait_ge(x2_ready, t + 3)
                            nc.scalar.activation(junk[:], x2[:, t, :], ACT.Square, scale=D ** -0.5,
                                                 accum_out=msq[:, u:u + 1]).then_inc(msq_ready, 1)
                            act.wait_ge(msq_ready, t + 1)
                            nc.scalar.activation(msq[:, u:u + 1], msq[:, u:u + 1], ACT.Sqrt,
                                                 bias=eps_sb[:]).then_inc(rms_ready, 1)
                            act.wait_ge(h2_ready, t + 1)
                            act.dma_start(h2_t[t], h2[u][:]).then_inc(h2_stored[u], 16)
                            act.wait_ge(h2T_psum, t + 3)
                            nc.scalar.copy(h2T[:].rearrange("p k c -> p (k c)"), two(4)).then_inc(h2T_ready, 1)
                    for u in range(2):
                        act.wait_ge(h2_stored[u], 16 + 16 * (T // 2))

                @block.vector
                def _(dve):
                    dve.sem_inc(x2_ready, 2)
                    dve.sem_inc(lg_ready, 1)
                    for u in range(2):
                        dve.sem_inc(h2_stored[u], 16)
                    dve.wait_ge(r_small, 48)

                    def residual(t, u, n):
                        dve.wait_ge(o_psum2, t + 3)
                        dve.wait_ge(x_in[u], n * 16)
                        nc.vector.tensor_tensor(x2[:, t, :], two(2 * u), xin[u][:], ALU.add).then_inc(x2_ready, 1)

                    def normalise(t, u, n):
                        dve.wait_ge(rms_ready, t + 1)
                        nc.vector.reciprocal(rstd[:, u:u + 1], msq[:, u:u + 1]).then_inc(rstd_ready, 1)
                        dve.wait_ge(rstd_ready, t + 1)
                        dve.wait_ge(h2_stored[u], n * 16)
                        dve.wait_ge(h2T_psum, t + 1)
                        nc.vector.scalar_tensor_tensor(
                            out=h2[u][:].rearrange("q (k p) -> q k p", k=KD),
                            in0=x2[:, t, :].rearrange("q (p k) -> q k p", k=KD), scalar=rstd[:, u:u + 1],
                            in1=g2_sb[:].rearrange("q (k p) -> q k p", k=KD),
                            op0=ALU.mult, op1=ALU.mult).then_inc(h2_ready, 1)

                    def take_logits(t):
                        dve.wait_ge(lg_psum, t + 1)
                        nc.vector.tensor_tensor(lgt[:, t, :], ps[:, 6, 0:NG + NE], br_sb[:],
                                                ALU.add).then_inc(lg_ready, 1)

                    for u in range(2):
                        residual(u, u, 1)
                        normalise(u, u, 1)
                    with dve.Fori(1, T // 2) as i:
                        for u in range(2):
                            residual(i * 2 + u, u, i + 1)
                            normalise(i * 2 + u, u, i + 1)
                            take_logits(i * 2 + u - 2)
                    for t in range(T - 2, T):
                        take_logits(t)

        slot_id = sb("slot_id", [P, TILES], I32)
        row_id = sb("row_id", [P, TILES], I32)
        e_w = sb("e_w", [P, 2, T])
        over_e = sb("over_e", [P, MAX_OVER], I32)
        n_over = sb("n_over", [P, 1], I32)
        with ExitStack() as st:
            def f(name, shape, dt=F32):
                return sb("r_" + name, shape, dt, ctx=st)
            iot = f("iot", [P, P], I32)
            io = f("io", [P, P])
            row1_i = f("row1_i", [P, 2, T], I32)
            row1 = f("row1", [P, 2, T])
            rv4, rv8 = f("rv4", [P, NG]), f("rv8", [P, EPG])
            thr = f("thr", [P, T - 1])
            gmax, gex, gsum, gtop = f("gmax", [P, T]), f("gex", [P, T, NG]), f("gsum", [P, T]), f("gtop", [P, T])
            cand4, goh = f("cand4", [P, T, NG]), f("goh", [P, T, NG])
            r1 = f("r1", [P, T])
            prod = f("prod", [P, T, NG, EPG])
            es = [f("es0", [P, T, EPG]), f("es1", [P, T, EPG])]
            em = f("em", [P, 2, T])
            cand8 = f("cand8", [P, T, EPG])
            oh = [f("oh0", [P, T, EPG]), f("oh1", [P, T, EPG])]
            dif, ex, den = f("dif", [P, T]), f("ex", [P, T]), f("den", [P, T])
            M = [f("M0", [P, T, NE]), f("M1", [P, T, NE])]
            Ms, Mp = f("Ms", [P, T, NE]), f("Mp", [P, T, NE])
            tot, totT, novT = f("tot", [P, NE]), f("totT", [NE, 1]), f("novT", [NE, 1])
            cmp7 = f("cmp7", [NE, T - 1])
            novB = f("novB", [NE, P])
            incl = f("incl", [NE, 2, NE])
            off = f("off", [P, 2, NE])
            cmpo = f("cmpo", [P, MAX_OVER, NE])
            eid = f("eid", [P, MAX_OVER])
            pr32 = f("pr32", [P, T, NE])
            rank, ea, eb2 = f("rank", [P, 2, T]), f("ea", [P, 2, T]), f("eb", [P, 2, T])
            cmpr = f("cmpr", [P, 2, T, T - 1])
            mt, isov, tile_, slot = f("mt", [P, 2, T]), f("isov", [P, 2, T]), f("tile", [P, 2, T]), f("slot", [P, 2, T])
            R = f("R", [P, 2, T, P])
            O = f("O", [P, 2, T, TILES])
            lst, emp, row = f("lst", [P, TILES]), f("emp", [P, TILES]), f("row", [P, TILES])
            second = f("second", [P, TILES])
            r_iota = sem("r_iota")
            r_dve = sem("r_dve")
            r_act = sem("r_act")
            r_psum = sem("r_psum")
            need_exp = sem("need_exp")
            need_tot = sem("need_tot")
            need_off = sem("need_off")
            need_slots = sem("need_slots")

            def last(a, n):
                return a.unsqueeze(len(a.shape)).broadcast_to(list(a.shape) + [n])

            with nc.Block() as block:
                @block.gpsimd
                def _(pool):
                    nc.gpsimd.iota(iot[:], pattern=[[1, P]], base=0, channel_multiplier=0).then_inc(r_iota, 1)
                    nc.gpsimd.iota(row1_i[:], pattern=[[SEQ, 2], [P, T]], base=1, channel_multiplier=1).then_inc(r_iota, 1)

                @block.scalar
                def _(act):
                    act.wait_ge(need_exp, 1)
                    nc.scalar.activation(gex[:], cand4[:], ACT.Exp).then_inc(r_act, 1)
                    nc.scalar.activation(ex[:], dif[:], ACT.Exp).then_inc(r_act, 1)

                @block.tensor
                def _(pe):
                    pe.wait_ge(need_tot, 1)
                    rk = ps[:, 0, 0:T * NE]
                    pe.matmul(rk, before[:], Ms[:].rearrange("p t e -> p (t e)"), start=True, stop=False)
                    pe.matmul(rk, ones[:], Mp[:].rearrange("p t e -> p (t e)"), start=False, stop=True)
                    pe.matmul(ps[0:NE, 1, 0:1], tot[:], ones[:, 0:1], start=True, stop=True).then_inc(r_psum, 1)
                    pe.wait_ge(need_off, 1)
                    pe.matmul(ps[:, 2, 0:2 * NE], novB[:], incl[:].rearrange("p a e -> p (a e)"),
                              start=True, stop=True).then_inc(r_psum, 1)
                    for n in range(2 * T):
                        if n % T == 0:
                            pe.wait_ge(need_slots, 2 * (n // T) + 2)
                        mm = pe.matmul(ps[:, 3, 0:TILES], R[:, n // T, n % T, :], O[:, n // T, n % T, :],
                                       start=(n == 0), stop=(n == 2 * T - 1))
                    mm.then_inc(r_psum, 1)

                @block.vector
                def _(dve):
                    link = Chain(dve, r_dve)
                    v = nc.vector
                    dve.wait_ge(r_iota, 2)
                    link(v.tensor_copy(io[:], iot[:]))
                    link(v.tensor_copy(row1[:], row1_i[:]))
                    link(v.tensor_scalar(rv4[:], io[:, 0:NG], -1.0, float(NG), ALU.mult, ALU.add))
                    link(v.tensor_scalar(rv8[:], io[:, 0:EPG], -1.0, float(EPG), ALU.mult, ALU.add))
                    link(v.tensor_scalar(thr[:], io[:, 0:T - 1], 1.0, float(P), ALU.add, ALU.mult))
                    gl_ = lgt[:, :, 0:NG]
                    el_ = lgt[:, :, NG:].rearrange("p t (g e) -> p t g e", g=NG)
                    link(v.tensor_reduce(gmax[:], gl_, AX.X, ALU.max))
                    link(v.tensor_tensor(goh[:], gl_, last(gmax[:], NG), ALU.is_equal))
                    link(v.tensor_tensor(goh[:], goh[:], rv4[:].unsqueeze(1).broadcast_to([P, T, NG]), ALU.mult))
                    link(v.tensor_reduce(r1[:], goh[:], AX.X, ALU.max))
                    link(v.tensor_tensor(goh[:], goh[:], last(r1[:], NG), ALU.is_equal))
                    link(v.tensor_tensor(cand4[:], gl_, last(gmax[:], NG), ALU.subtract))
                    link(v.tensor_tensor(prod[:], el_, last(goh[:], EPG), ALU.mult))
                    link(v.tensor_reduce(es[0][:], prod[:].rearrange("p t g e -> p t e g"), AX.X, ALU.add))
                    for c in range(2):
                        link(v.tensor_reduce(em[:, c, :], es[c][:], AX.X, ALU.max))
                        link(v.tensor_tensor(cand8[:], es[c][:], last(em[:, c, :], EPG), ALU.is_equal))
                        link(v.tensor_tensor(cand8[:], cand8[:], rv8[:].unsqueeze(1).broadcast_to([P, T, EPG]),
                                             ALU.mult))
                        link(v.tensor_reduce(r1[:], cand8[:], AX.X, ALU.max))
                        link(v.tensor_tensor(oh[c][:], cand8[:], last(r1[:], EPG), ALU.is_equal))
                        if c == 0:
                            link(v.scalar_tensor_tensor(out=es[1][:], in0=oh[0][:], scalar=-3e38, in1=es[0][:],
                                                        op0=ALU.mult, op1=ALU.add))
                    v.tensor_tensor(dif[:], em[:, 1, :], em[:, 0, :], ALU.subtract).then_inc(need_exp, 1)
                    for c in range(2):
                        link(v.tensor_tensor(M[c][:].rearrange("p t (g e) -> p t g e", g=NG), last(goh[:], EPG),
                                             oh[c][:].unsqueeze(2).broadcast_to([P, T, NG, EPG]), ALU.mult))
                    link(v.tensor_tensor(Ms[:], M[0][:], M[1][:], ALU.add))
                    link(v.memset(Mp[:, 0, :], 0.0))
                    for t in range(1, T):
                        link(v.tensor_tensor(Mp[:, t, :], Mp[:, t - 1, :], Ms[:, t - 1, :], ALU.add))
                    v.tensor_tensor(tot[:], Mp[:, T - 1, :], Ms[:, T - 1, :], ALU.add).then_inc(need_tot, 1)
                    link(v.tensor_copy(incl[:, 0, :], before[0:NE, 0:NE]))
                    link(v.tensor_tensor(incl[:, 1, :], before[0:NE, 0:NE], ident[0:NE, 0:NE], ALU.add))
                    dve.wait_ge(r_act, 2)
                    link(v.tensor_reduce(gsum[:], gex[:], AX.X, ALU.add))
                    link(v.reciprocal(gtop[:], gsum[:]))
                    link(v.tensor_scalar(den[:], ex[:], 1.0, None, ALU.add))
                    link(v.reciprocal(den[:], den[:]))
                    link(v.tensor_tensor(e_w[:, 0, :], den[:], gtop[:], ALU.mult))
                    link(v.tensor_tensor(e_w[:, 1, :], e_w[:, 0, :], ex[:], ALU.mult))
                    dve.wait_ge(r_psum, 1)
                    link(v.tensor_copy(totT[:], ps[0:NE, 1, 0:1]))
                    link(v.tensor_scalar(cmp7[:], thr[0:NE, :], totT[:, 0:1], None, ALU.is_lt))
                    link(v.tensor_reduce(novT[:], cmp7[:], AX.X, ALU.add))
                    v.tensor_scalar(novB[:], ones[0:NE, :], novT[:, 0:1], None, ALU.mult).then_inc(need_off, 1)
                    rk = ps[:, 0, 0:T * NE].rearrange("p (t e) -> p t e", e=NE)
                    for c in range(2):
                        link(v.tensor_tensor(pr32[:], M[c][:], rk, ALU.mult))
                        link(v.tensor_reduce(rank[:, c, :], pr32[:], AX.X, ALU.add))
                        link(v.tensor_tensor(pr32[:], M[c][:], io[:, 0:NE].unsqueeze(1).broadcast_to([P, T, NE]),
                                             ALU.mult))
                        link(v.tensor_reduce(ea[:, c, :], pr32[:], AX.X, ALU.add))
                    dve.wait_ge(r_psum, 2)
                    link(v.tensor_copy(off[:].rearrange("p a e -> p (a e)"), ps[:, 2, 0:2 * NE]))
                    for c in range(2):
                        link(v.tensor_tensor(pr32[:], M[c][:], off[:, 0:1, :].broadcast_to([P, T, NE]), ALU.mult))
                        link(v.tensor_reduce(eb2[:, c, :], pr32[:], AX.X, ALU.add))
                    link(v.tensor_copy(n_over[:], off[:, 1, NE - 1:NE]))
                    link(v.tensor_tensor(cmpo[:], off[:, 1:2, :].broadcast_to([P, MAX_OVER, NE]),
                                         last(io[:, 0:MAX_OVER], NE), ALU.is_le))
                    link(v.tensor_reduce(eid[:], cmpo[:], AX.X, ALU.add))
                    link(v.tensor_scalar(over_e[:], eid[:], float(NE - 1), None, ALU.min))
                    link(v.tensor_tensor(cmpr[:], last(rank[:], T - 1),
                                         thr[:].unsqueeze(1).unsqueeze(1).broadcast_to([P, 2, T, T - 1]), ALU.is_ge))
                    link(v.tensor_reduce(mt[:], cmpr[:], AX.X, ALU.add))
                    link(v.tensor_scalar(isov[:], mt[:], 0.0, None, ALU.is_gt))
                    link(v.tensor_tensor(eb2[:], eb2[:], mt[:], ALU.add))
                    link(v.tensor_tensor(eb2[:], eb2[:], ea[:], ALU.subtract))
                    link(v.scalar_tensor_tensor(out=eb2[:], in0=eb2[:], scalar=float(NE - 1), in1=isov[:],
                                                op0=ALU.add, op1=ALU.mult))
                    link(v.tensor_tensor(tile_[:], ea[:], eb2[:], ALU.add))
                    link(v.scalar_tensor_tensor(out=slot[:], in0=mt[:], scalar=-float(P), in1=rank[:],
                                                op0=ALU.mult, op1=ALU.add))
                    for c in range(2):
                        v.tensor_tensor(R[:, c, :, :], io[:].unsqueeze(1).broadcast_to([P, T, P]),
                                        last(slot[:, c, :], P), ALU.is_equal).then_inc(need_slots, 1)
                        link(v.tensor_tensor(O[:, c, :, :], io[:, 0:TILES].unsqueeze(1).broadcast_to([P, T, TILES]),
                                             last(tile_[:, c, :], TILES), ALU.is_equal))
                        v.tensor_tensor(O[:, c, :, :], O[:, c, :, :], last(row1[:, c, :], TILES),
                                        ALU.mult).then_inc(need_slots, 1)
                    dve.wait_ge(r_psum, 3)
                    link(v.tensor_copy(lst[:], ps[:, 3, 0:TILES]))
                    link(v.tensor_scalar(emp[:], lst[:], 0.0, 8.0 * SEQ, ALU.is_equal, ALU.mult))
                    link(v.scalar_tensor_tensor(out=row[:], in0=lst[:], scalar=-1.0, in1=emp[:],
                                                op0=ALU.add, op1=ALU.add))
                    link(v.tensor_copy(row_id[:], row[:]))
                    link(v.tensor_scalar(second[:], row[:], float(SEQ), None, ALU.is_ge))
                    link(v.scalar_tensor_tensor(out=slot_id[:], in0=second[:], scalar=-float(SEQ), in1=row[:],
                                                op0=ALU.mult, op1=ALU.add))

        with ExitStack() as st:
            wgu = wgu_first + [hT[:, e * 4:(e + 1) * 4, :].rearrange("p a (b c f) -> p (a b) c f", b=2, c=2)
                               for e in range(2)]
            wdn = wdn_first + [sb(f"wdn{u}", [P, 2, D], ctx=st) for u in range(2)]
            idx = [sb(f"idx{w}", [P, 1], I32, ctx=st) for w in range(WR)]
            idy = [sb(f"idy{w}", [P, 1], I32, ctx=st) for w in range(WR)]
            hg = [yaT[:, 2 + w, :] for w in range(2)] + [sb(f"hg{w}", [P, D], ctx=st) for w in range(2)]
            hgT = [sb(f"hgT{u}", [P, KD, P], ctx=st) for u in range(2)]
            sg = [sb(f"esg{u}", [P, DE], ctx=st) for u in range(2)]
            sil = sb("sil", [P, DE], ctx=st)
            av = [sb(f"av{u}", [P, 2, P], ctx=st) for u in range(2)]
            avT = [sb(f"avT{u}", [P, 2, P], ctx=st) for u in range(2)]
            ys = [ybT[:, 2 + w, :] for w in range(2)] + [sb(f"ys{w}", [P, D], ctx=st) for w in range(2)]
            hg_clear = sem("hg_clear")
            idx_ready = sem("idx_ready")
            idy_ready = sem("idy_ready")
            hg_in = [sem(f"hg_in{w}") for w in range(WR)]
            hgT_psum = sem("hgT_psum")
            hgT_ready = sem("hgT_ready")
            gu_psum = sem("gu_psum")
            esg_ready = sem("esg_ready")
            sil_ready = sem("sil_ready")
            av_ready = sem("av_ready")
            avT_psum = sem("avT_psum")
            avT_ready = sem("avT_ready")
            y_psum = sem("y_psum")
            ys_ready = sem("ys_ready")
            ys_stored = [sem(f"ys_stored{w}") for w in range(WR)]
            ys_free = sem("ys_free")
            o_w_in = sem("o_w_in")
            o_idx = sem("o_idx")
            o_idy = sem("o_idy")
            o_hg_in = sem("o_hg_in")
            o_pe = sem("o_pe")
            o_act = sem("o_act")
            o_dve = sem("o_dve")
            o_stored = sem("o_stored")
            o_free = sem("o_free")

            def transposes(pe, src, pieces, dst):
                for k in range(pieces):
                    mm = pe.transpose(dst[:, k * P:(k + 1) * P], src[:, k * P:(k + 1) * P], ident[:])
                return mm

            def gate_up(pe, u, w, bank):
                for k in range(KD):
                    mm = pe.matmul(ps[:, bank, :], hgT[u][:, k, :], wgu[w][:, k, :, :].rearrange("p a f -> p (a f)"),
                                   start=(k == 0), stop=(k == KD - 1))
                return mm

            def down(pe, u, w):
                for n in range(2):
                    for c in range(2):
                        mm = pe.matmul(ps[:, 5 + n, :], avT[u][:, c, :], wdn[w][:, c, n * HALF:(n + 1) * HALF],
                                       start=(c == 0), stop=(c == 1))
                return mm

            def act_order(a):
                return a.rearrange("q (p c) -> q c p", c=2)

            av2 = [a[:].rearrange("p c f -> p (c f)") for a in av]
            avT2 = [a[:].rearrange("p c f -> p (c f)") for a in avT]
            with nc.Block() as block:
                @block.sync
                def _(sp):
                    for w in range(WR):
                        sp.wait_ge(hg_in[w], 16)
                    for e in range(FIRST, WR):
                        load_gate_up(sp, wgu[e], e, wgu_in[e])
                        load_down(sp, wdn[e], e, wdn_in[e])
                    with sp.Fori(1, NE // WR) as i:
                        for u in range(WR):
                            e = i * WR + u
                            sp.wait_ge(gu_psum, e + 1)
                            load_gate_up(sp, wgu[u], e, wgu_in[u])
                            sp.wait_ge(y_psum, e + 1)
                            load_down(sp, wdn[u], e, wdn_in[u])
                    over = sp.value_load(n_over[0:1, 0:1], min_val=0, max_val=MAX_OVER)
                    sp.wait_ge(y_psum, NE + 1)
                    with sp.Fori(0, MAX_OVER) as o:
                        with sp.If(o < over):
                            sp.wait_ge(o_pe, o * 4 + 4)
                            apart(sp)
                            e = sp.value_load(over_e[0:1, bass.ds(o, 1)], min_val=0, max_val=NE - 1)
                            load_gate_up(sp, wgu[0], e, o_w_in)
                            load_down(sp, wdn[0], e, o_w_in)
                            sp.nop()

                @block.gpsimd
                def _(pool):
                    pool.wait_ge(hg_clear, WR)

                    def gather(t, w, n):
                        nc.gpsimd.tensor_copy(idx[w][:], slot_id[:, bass.ds(t, 1)]).then_inc(idx_ready, 1)
                        pool.wait_ge(idx_ready, n)
                        apart(pool)
                        nc.gpsimd.indirect_dma_start(
                            hg[w][:], None, h2_dram, bass.IndirectOffsetOnAxis(ap=idx[w][:, 0:1].bitcast(U32), axis=0),
                            bounds_check=SEQ - 1, oob_is_err=False).then_inc(hg_in[w], 16)

                    def scatter(t, w, ready, n, stored):
                        nc.gpsimd.tensor_copy(idy[w][:], row_id[:, bass.ds(t, 1)]).then_inc(ready, 1)
                        pool.wait_ge(ready, n)
                        apart(pool)
                        nc.gpsimd.indirect_dma_start(
                            y_dram, bass.IndirectOffsetOnAxis(ap=idy[w][:, 0:1].bitcast(U32), axis=0), ys[w][:], None,
                            bounds_check=2 * SEQ - 1, oob_is_err=False).then_inc(stored, 16)

                    def stored(w, n):
                        pool.wait_ge(ys_stored[w], n * 16)
                        pool.sem_inc(ys_free, 1)

                    def step(i, w):
                        t = i * WR + w
                        pool.wait_ge(hgT_psum, t + 3)
                        gather(t + WR, w, t + WR + 1)
                        pool.wait_ge(ys_ready, t + 2)
                        scatter(t, w, idy_ready, t + 1, ys_stored[w])

                    for w in range(WR):
                        gather(w, w, w + 1)
                    step(0, 0)
                    for w in range(1, WR):
                        step(0, w)
                        stored(w - 1, 1)
                    with pool.Fori(1, NE // WR) as i:
                        step(i, 0)
                        stored(WR - 1, i)
                        for w in range(1, WR):
                            step(i, w)
                            stored(w - 1, i + 1)
                    stored(WR - 1, NE // WR)
                    over = pool.value_load(n_over[0:1, 0:1], min_val=0, max_val=MAX_OVER)
                    for w in range(WR):
                        pool.wait_ge(hg_in[w], (NE // WR + 1) * 16)
                    pool.wait_ge(hgT_psum, NE + 3)
                    with pool.Fori(0, MAX_OVER) as o:
                        with pool.If(o < over):
                            pool.wait_ge(o_pe, o * 4 + 4)
                            nc.gpsimd.tensor_copy(idx[0][:], slot_id[:, bass.ds(o + NE, 1)]).then_inc(o_idx, 1)
                            pool.wait_ge(o_idx, o + 1)
                            apart(pool)
                            nc.gpsimd.indirect_dma_start(
                                hg[0][:], None, h2_dram,
                                bass.IndirectOffsetOnAxis(ap=idx[0][:, 0:1].bitcast(U32), axis=0),
                                bounds_check=SEQ - 1, oob_is_err=False).then_inc(o_hg_in, 16)
                            pool.wait_ge(o_dve, o * 5 + 5)
                            scatter(o + NE, 0, o_idy, o + 1, o_stored)
                            pool.wait_ge(o_stored, o * 16 + 16)
                            pool.sem_inc(o_free, 1)

                @block.tensor
                def _(pe):
                    pe.sem_inc(hgT_psum, 2)
                    pe.sem_inc(gu_psum, WR)
                    pe.sem_inc(y_psum, WR)
                    pe.sem_inc(o_pe, 4)

                    def gathered_transposes(t, w, n):
                        pe.wait_ge(hg_in[w], n * 16)
                        pe.wait_ge(hgT_ready, t + 1)
                        transposes(pe, hg[w], KD, two(0)).then_inc(hgT_psum, 1)

                    def first_half(t, w, n):
                        u = w % 2
                        pe.wait_ge(wgu_in[w], n * 32)
                        pe.wait_ge(hgT_ready, t + 2)
                        pe.wait_ge(av_ready, t + 1)
                        gate_up(pe, u, w, 2 + u).then_inc(gu_psum, 1)

                    def hidden_transposes(t, u):
                        pe.wait_ge(av_ready, t + 3)
                        pe.wait_ge(avT_ready, t + 1)
                        transposes(pe, av2[u], 2, ps[:, 4 + 3 * u, 0:2 * P]).then_inc(avT_psum, 1)

                    def second_half(t, w, n):
                        u = w % 2
                        pe.wait_ge(avT_ready, t + 3)
                        pe.wait_ge(wdn_in[w], n * 16)
                        pe.wait_ge(ys_ready, t + 1)
                        down(pe, u, w).then_inc(y_psum, 1)

                    def step(i, w):
                        t, u = i * WR + w, w % 2
                        first_half(t, w, i + 1)
                        if w > 0:
                            before_w, before_n = w - 1, i + 1
                        else:
                            before_w, before_n = WR - 1, i
                        hidden_transposes(t - 1, 1 - u)
                        gathered_transposes(t + 1, (w + 1) % WR, i + 1 + (w + 1) // WR)
                        second_half(t - 1, before_w, before_n)

                    gathered_transposes(0, 0, 1)
                    first_half(0, 0, 1)
                    gathered_transposes(1, 1, 1)
                    for w in range(1, WR):
                        step(0, w)
                    with pe.Fori(1, NE // WR) as i:
                        for w in range(WR):
                            step(i, w)
                    hidden_transposes(NE - 1, 1)
                    second_half(NE - 1, WR - 1, NE // WR)
                    over = pe.value_load(n_over[0:1, 0:1], min_val=0, max_val=MAX_OVER)
                    pe.wait_ge(ys_ready, NE + 1)
                    pe.wait_ge(hgT_ready, NE + 2)
                    with pe.Fori(0, MAX_OVER) as o:
                        with pe.If(o < over):
                            pe.wait_ge(o_hg_in, o * 16 + 16)
                            transposes(pe, hg[0], KD, two(0)).then_inc(o_pe, 1)
                            pe.wait_ge(o_w_in, o * 48 + 48)
                            pe.wait_ge(o_dve, o * 5 + 1)
                            gate_up(pe, 0, 0, 2).then_inc(o_pe, 1)
                            pe.wait_ge(o_dve, o * 5 + 3)
                            transposes(pe, av2[0], 2, ps[:, 4, 0:2 * P]).then_inc(o_pe, 1)
                            pe.wait_ge(o_dve, o * 5 + 4)
                            down(pe, 0, 0).then_inc(o_pe, 1)
                            pe.nop()

                @block.scalar
                def _(act):
                    act.sem_inc(hgT_ready, 1)
                    act.wait_ge(hgT_psum, 3)
                    nc.scalar.copy(hgT[0][:].rearrange("p k c -> p (k c)"), two(0)).then_inc(hgT_ready, 1)
                    with act.Fori(0, NE // 2) as i:
                        for u in range(2):
                            t = i * 2 + u
                            act.wait_ge(gu_psum, t + 1 + WR)
                            act.wait_ge(av_ready, t + 1)
                            nc.scalar.activation(sg[u][:], ps[:, 2 + u, 0:DE], ACT.Sigmoid).then_inc(esg_ready, 1)
                            act.wait_ge(hgT_psum, t + 4)
                            nc.scalar.copy(hgT[1 - u][:].rearrange("p k c -> p (k c)"), two(0)).then_inc(hgT_ready, 1)
                    over = act.value_load(n_over[0:1, 0:1], min_val=0, max_val=MAX_OVER)
                    with act.Fori(0, MAX_OVER) as o:
                        with act.If(o < over):
                            act.wait_ge(o_pe, o * 4 + 6)
                            nc.scalar.activation(sg[0][:], ps[:, 2, 0:DE], ACT.Sigmoid).then_inc(o_act, 1)
                            act.nop()

                @block.vector
                def _(dve):
                    dve.sem_inc(av_ready, 2)
                    dve.sem_inc(avT_ready, 2)
                    dve.sem_inc(ys_ready, 1)
                    dve.sem_inc(ys_free, WR)
                    for w in range(WR):
                        nc.vector.memset(hg[w][:], 0.0).then_inc(hg_clear, 1)
                    dve.sem_inc(o_free, 1)
                    with dve.Fori(0, NE // WR) as i:
                        for w in range(WR):
                            t, u = i * WR + w, w % 2
                            dve.wait_ge(esg_ready, t + 1)
                            nc.vector.tensor_tensor(sil[:], ps[:, 2 + u, 0:DE], sg[u][:],
                                                    ALU.mult).then_inc(sil_ready, 1)
                            dve.wait_ge(sil_ready, t + 1)
                            nc.vector.tensor_tensor(av[u][:], act_order(sil[:]), act_order(ps[:, 2 + u, DE:2 * DE]),
                                                    ALU.mult).then_inc(av_ready, 1)
                            dve.wait_ge(avT_psum, t + 1)
                            nc.vector.tensor_copy(avT2[u], ps[:, 4 + 3 * u, 0:2 * P]).then_inc(avT_ready, 1)
                            dve.wait_ge(y_psum, t + 1 + WR)
                            dve.wait_ge(ys_free, t + 1)
                            nc.vector.tensor_copy(ys[w][:], two(5)).then_inc(ys_ready, 1)
                    over = dve.value_load(n_over[0:1, 0:1], min_val=0, max_val=MAX_OVER)
                    dve.wait_ge(ys_free, NE + WR)
                    with dve.Fori(0, MAX_OVER) as o:
                        with dve.If(o < over):
                            link = Chain(dve, o_dve, o * 5)
                            dve.wait_ge(o_pe, o * 4 + 5)
                            link(nc.vector.tensor_copy(hgT[0][:].rearrange("p k c -> p (k c)"), two(0)))
                            dve.wait_ge(o_act, o + 1)
                            link(nc.vector.tensor_tensor(sil[:], ps[:, 2, 0:DE], sg[0][:], ALU.mult))
                            link(nc.vector.tensor_tensor(av[0][:], act_order(sil[:]), act_order(ps[:, 2, DE:2 * DE]),
                                                         ALU.mult))
                            dve.wait_ge(o_pe, o * 4 + 7)
                            link(nc.vector.tensor_copy(avT2[0], ps[:, 4, 0:2 * P]))
                            dve.wait_ge(o_pe, o * 4 + 8)
                            dve.wait_ge(o_free, o + 1)
                            link(nc.vector.tensor_copy(ys[0][:], two(5)))
                            apart(dve)

        with ExitStack() as st:
            yc = [[sb(f"yc{c}{u}", [P, D], ctx=st) for u in range(2)] for c in range(2)]
            yc_in = [sem(f"yc_in{u}") for u in range(2)]
            first_added = sem("first_added")
            both_added = sem("both_added")
            out_stored = sem("out_stored")
            with nc.Block() as block:
                @block.scalar
                def _(act):
                    with act.Fori(0, T // 2) as i:
                        for u in range(2):
                            act.wait_ge(both_added, i * 2 + u + 1)
                            for c in range(2):
                                act.dma_start(yc[c][u][:], y_t[i * 2 + u + c * T]).then_inc(yc_in[u], 16)

                @block.vector
                def _(dve):
                    dve.sem_inc(both_added, 2)
                    with dve.Fori(0, T // 2) as i:
                        for u in range(2):
                            t = i * 2 + u
                            dve.wait_ge(yc_in[u], i * 32 + 32)
                            nc.vector.scalar_tensor_tensor(out=x2[:, t, :], in0=yc[0][u][:],
                                                           scalar=e_w[:, 0, bass.ds(t, 1)], in1=x2[:, t, :],
                                                           op0=ALU.mult, op1=ALU.add).then_inc(first_added, 1)
                            dve.wait_ge(first_added, t + 1)
                            nc.vector.scalar_tensor_tensor(out=x2[:, t, :], in0=yc[1][u][:],
                                                           scalar=e_w[:, 1, bass.ds(t, 1)], in1=x2[:, t, :],
                                                           op0=ALU.mult, op1=ALU.add).then_inc(both_added, 1)

                @block.sync
                def _(sp):
                    with sp.Fori(0, T) as t:
                        sp.wait_ge(both_added, t + 3)
                        sp.dma_start(out_t[t], x2[:, t, :]).then_inc(out_stored, 16)
                    sp.wait_ge(out_stored, 16 * T)


def kernel(**inputs):
    import numpy as np
    import concourse.bacc as bacc
    from concourse import mybir as my
    from concourse.bass_utils import run_bass_kernel_spmd

    a = {k: np.asarray(v) for k, v in inputs.items()}
    w_in = a["w_in"][0]

    def rows(w):
        return w.reshape(-1, P, w.shape[1]).transpose(1, 0, 2)

    def cols(v):
        return v.reshape(-1, P).T

    o = [0, 512, 1024, 1536, 1792, 2048, 2560, 3072, 3088, 5136]
    part = [w_in[:, o[n]:o[n + 1]] for n in range(9)]
    aq, ak, av, bq, bk, bv, brr, lr, gates = part
    pairs = [(aq, ak, n) for n in range(A_PAIRS)] + [(bq, bk, n) for n in range(B_PAIRS)]
    blk = lambda w, n: w[:, n * P:(n + 1) * P]
    wqk = np.stack([rows(np.concatenate([blk(q, n), blk(k, n)], 1)) for q, k, n in pairs])
    flat = lambda w: rows(w).reshape(P, -1)
    wd = np.stack([np.concatenate([flat(blk(gates, n)), flat(blk(gates, KD + n)), flat(blk(a["proj_a"][0], n)),
                                   flat(blk(a["proj_b"][0], n))], 1) for n in range(KD)])
    rel = a["rel_bias"]
    at = np.clip(5 * P + np.arange(P)[:, None] - np.arange(BANDW)[None, :], 0, 2 * P)
    relx = rel[at].transpose(2, 0, 1).reshape(A_PAIRS, 2, P, BANDW).transpose(0, 2, 1, 3)
    turned = lambda w: w.reshape(P, KD, -1)
    arrays = {
        "x": a["x"][0], "g1": cols(a["norm_mix_gain"][0]), "wv": rows(np.concatenate([av, bv, brr], 1)),
        "wqk": wqk, "wlr": rows(lr), "wd": wd, "wout": rows(a["w_out"][0]),
        "qg": cols(a["a_q_gain"][0].reshape(-1)), "kg": cols(a["a_k_gain"][0].reshape(-1)),
        "bog": cols(a["b_out_gain"][0].reshape(-1)), "gup": a["b_gate_up"][0], "gbias": a["b_gate_bias"],
        "relx": relx, "g2p": a["norm_ffn_gain"][0].reshape(P, KD).T.reshape(-1),
        "wr": turned(np.concatenate([a["w_group"][0], a["w_router"][0]], 1)),
        "br": np.concatenate([a["b_group"][0], a["b_router"][0]]),
        "w_gate": a["w_gate"][0], "w_up": a["w_up"][0], "w_down": a["w_down"][0],
    }
    nc = bacc.Bacc("TRN2", target_bir_lowering=False, num_devices=1)
    arrays = {f"in_{n}": np.ascontiguousarray(v) for n, v in arrays.items()}
    args = [nc.dram_tensor(n, v.shape, my.dt.from_np(v.dtype), kind="ExternalInput").ap() for n, v in arrays.items()]
    args.append(nc.dram_tensor("out_0", (SEQ, D), F32, kind="ExternalOutput").ap())
    args.append(nc.dram_tensor("h2_rows", (SEQ, D), F32, kind="Internal").ap())
    args.append(nc.dram_tensor("y_rows", (2 * SEQ, D), F32, kind="Internal").ap())
    layer_kernel(nc, *args)
    r = run_bass_kernel_spmd(nc, [arrays], core_ids=[0])
    return np.asarray(r.results[0]["out_0"]).reshape(1, SEQ, D)
```

```python
from contextlib import ExitStack

import concourse.bass as bass
from concourse import mybir

ALU = mybir.AluOpType
ACT = mybir.ActivationFunctionType
AX = mybir.AxisListType
F32 = mybir.dt.float32
F32R = mybir.dt.float32r
I32 = mybir.dt.int32
U32 = mybir.dt.uint32

P = 128
D = 1024
SEQ = 1024
T = SEQ // P
KD = D // P
EPS = 1e-6
CHUNK = 64
LEFT = 8
HALF = 512
A_W, A_H, A_D = 512, 8, 64
A_PAIRS = A_H // 2
BAND_T = LEFT * CHUNK // P + 1
BANDW = BAND_T * P
B_V, B_QK, B_H, B_DK, B_DV, RANK = 512, 256, 4, 64, 128, 16
B_PAIRS = B_H // 2
GATE_TEMP = 16.0
LEVELS = 8
NG, EPG, NE = 4, 8, 32
DE = 256
MAX_OVER = 2 * SEQ // P
TILES = NE + MAX_OVER
NEG = -1e30


class Chain:

    def __init__(self, eng, sem, before=0):
        self.eng, self.sem, self.before, self.n = eng, sem, before, 0

    def __call__(self, ins):
        self.n += 1
        ins.then_inc(self.sem, 1)
        self.eng.wait_ge(self.sem, self.before + self.n)


def layer_kernel(nc, x, g1, wv, wqk, wlr, wd, wout, qg, kg, bog, gup, gbias, relx, g2p, wr, br,
                 w_gate, w_up, w_down, out, h2_dram, y_dram):
    x_t = x.rearrange("(t p) d -> t p d", p=P)
    out_t = out.rearrange("(t p) d -> t p d", p=P)
    h2_t = h2_dram.rearrange("(t p) d -> t p d", p=P)
    y_t = y_dram.rearrange("(t p) d -> t p d", p=P)
    wg_e = w_gate.rearrange("e (p k) f -> e p k f", p=P)
    wu_e = w_up.rearrange("e (p k) f -> e p k f", p=P)
    wn_e = w_down.rearrange("e (p c) n -> e p c n", p=P)

    with ExitStack() as top:
        def sem(name):
            return top.enter_context(nc.semaphore(name))

        def sb(name, shape, dt=F32, ctx=top):
            return ctx.enter_context(nc.sbuf_tensor(name, shape, dt))

        ps = top.enter_context(nc.psum_tensor("ps", [P, 8, HALF], F32))
        ticks = sem("ticks")

        def apart(eng):
            eng.sem_inc(ticks, 1)

        ident = sb("ident", [P, P])
        ones = sb("ones", [P, P])
        head_mean = sb("head_mean", [P, P])
        tri16 = sb("tri16", [P, P])
        before = sb("before", [P, P])
        load_small = sem("load_small")
        g1_sb = sb("g1_sb", [P, KD])
        qg_sb = sb("qg_sb", [P, A_PAIRS + 1])
        kg_sb = sb("kg_sb", [P, A_PAIRS + 1])
        bog_sb = sb("bog_sb", [P, B_H])
        lgt = sb("lgt", [P, T, NG + NE])
        eps_sb = sb("eps_sb", [P, 1])
        c_pool = sem("c_pool")
        c_dve = sem("c_dve")

        yaT = sb("yaT", [P, A_W // P, SEQ])
        ybT = sb("ybT", [P, B_V // P, SEQ])
        hT = sb("hT", [P, KD, SEQ])

        mid = ExitStack()
        va = sb("va", [P, T, A_W], ctx=mid)
        vb = sb("vb", [P, T, B_V], ctx=mid)
        rs = sb("rs", [P, T, B_V], ctx=mid)

        w_in = [sem(f"w_in{u}") for u in range(2)]
        w_first = ybT[:, 0:2, :].rearrange("p a (b c) -> p (a b) c", c=2 * P)
        with ExitStack() as st:
            wraw = [a[:].rearrange("p a (b c) -> p (a b) c", c=HALF) for a in (yaT, ybT)]
            wvH = [sb(f"wvH{u}", [P, KD, HALF], F32R, ctx=st) for u in range(2)]
            wvL = [sb(f"wvL{u}", [P, KD, HALF], F32R, ctx=st) for u in range(2)]
            hsH = [sb(f"hsH{u}", [P, KD, P], F32R, ctx=st) for u in range(2)]
            hsL = [sb(f"hsL{u}", [P, KD, P], F32R, ctx=st) for u in range(2)]
            xin = [rs[:, 2 * u:2 * u + 2, :].rearrange("p a b -> p (a b)") for u in range(2)]
            hn = [rs[:, 4 + 2 * u:6 + 2 * u, :].rearrange("p a b -> p (a b)") for u in range(2)]
            msq = sb("msq", [P, 2], ctx=st)
            rstd = sb("rstd", [P, 2], ctx=st)
            sg = [sb(f"sg{u}", [P, HALF], ctx=st) for u in range(2)]
            x_in = [sem(f"x_in{u}") for u in range(2)]
            wraw_in = [sem(f"wraw_in{n}") for n in range(4)]
            msq_ready = sem("msq_ready")
            rms_ready = sem("rms_ready")
            rstd_ready = sem("rstd_ready")
            hn_ready = sem("hn_ready")
            hT_psum = sem("hT_psum")
            hT_ready = sem("hT_ready")
            hsH_ready = sem("hsH_ready")
            hsL_ready = sem("hsL_ready")
            wvH_ready = sem("wvH_ready")
            wvL_ready = sem("wvL_ready")
            v_psum = sem("v_psum")
            v_taken = sem("v_taken")
            sg_ready = sem("sg_ready")
            psT = [ps[:, 0:2, :].rearrange("p b c -> p (b c)"), ps[:, 2:4, :].rearrange("p b c -> p (b c)")]

            def over_tiles(eng, step):
                step(0, 0)
                with eng.Fori(0, (T - 2) // 2) as i:
                    for u in range(2):
                        step(i * 2 + u + 1, (u + 1) % 2)
                step(T - 1, (T - 1) % 2)

            with nc.Block() as block:
                @block.sync
                def _(sp):
                    for dst, src in ((g1_sb[:], g1), (qg_sb[:, 0:A_PAIRS], qg), (kg_sb[:, 0:A_PAIRS], kg),
                                     (bog_sb[:], bog)):
                        sp.dma_start(dst, src).then_inc(load_small, 16)
                    for t in range(2):
                        sp.dma_start(xin[t], x_t[t]).then_inc(x_in[t], 16)
                    for n in range(2):
                        ks = slice(n * KD // 2, (n + 1) * KD // 2)
                        sp.dma_start(wraw[0][:, ks, :], wv[:, ks, 0:HALF]).then_inc(wraw_in[n], 16)
                    for t in range(2, 4):
                        sp.wait_ge(hn_ready, t - 1)
                        sp.dma_start(xin[t % 2], x_t[t]).then_inc(x_in[t % 2], 16)
                    sp.dma_start(wraw[1][:], wv[:, :, HALF:2 * HALF]).then_inc(wraw_in[2], 16)
                    with sp.Fori(2, T // 2) as i:
                        for u in range(2):
                            sp.wait_ge(hn_ready, i * 2 + u - 1)
                            sp.dma_start(xin[u], x_t[i * 2 + u]).then_inc(x_in[u], 16)
                    sp.wait_ge(wvL_ready, KD)
                    sp.dma_start(wraw[0][:], wv[:, :, 2 * HALF:3 * HALF]).then_inc(wraw_in[3], 16)
                    sp.wait_ge(wvL_ready, 2 * KD)
                    sp.dma_start(w_first, wqk[0]).then_inc(w_in[0], 16)

                @block.scalar
                def _(act):
                    act.wait_ge(c_pool, 10)

                    def mean_square(t, u, n):
                        act.wait_ge(x_in[u], n * 16)
                        nc.scalar.activation(hn[u], xin[u], ACT.Square, scale=D ** -0.5,
                                             accum_out=msq[:, u:u + 1]).then_inc(msq_ready, 1)
                        act.wait_ge(msq_ready, t + 1)
                        nc.scalar.activation(msq[:, u:u + 1], msq[:, u:u + 1], ACT.Sqrt,
                                             bias=eps_sb[:]).then_inc(rms_ready, 1)

                    def load_of(t, u):
                        return (t - u) // 2 + 1

                    def high_weights(g, k):
                        nc.scalar.copy(wvH[g % 2][:, bass.ds(k, 1), :],
                                       wraw[g % 2][:, bass.ds(k, 1), :]).then_inc(wvH_ready, 1)

                    def take(g, t, u):
                        q = t + g * T
                        act.wait_ge(v_psum, q + 3)
                        if g < 2:
                            nc.scalar.copy((va, vb)[g][:, bass.ds(t, 1), :],
                                           ps[:, 4 + u:5 + u, :]).then_inc(v_taken, 1)
                        else:
                            act.wait_ge(v_taken, q + 1)
                            nc.scalar.activation(sg[u][:], ps[:, 4 + u, :], ACT.Sigmoid).then_inc(sg_ready, 1)

                    def step_of(g):
                        def step(t, u):
                            q = t + g * T
                            peeled = isinstance(t, int)
                            if g == 0:
                                act.wait_ge(hT_ready, t + 3)
                            act.wait_ge(v_psum, q + 1)
                            nc.scalar.copy(hsH[u][:], hT[:, :, bass.ds(t * P, P)]).then_inc(hsH_ready, 1)
                            if g == 0 and not (peeled and t == T - 1):
                                mean_square(t + 1, 1 - u, load_of(t + 1, 1 - u))
                            if peeled and t == 0:
                                if g == 0:
                                    for k in range(KD):
                                        act.wait_ge(wraw_in[k * 2 // KD], 16)
                                        high_weights(0, k)
                                else:
                                    take(g - 1, T - 1, 1)
                            else:
                                take(g, t - 1, 1 - u)
                                if g < 2:
                                    act.wait_ge(wraw_in[2 + g], 16)
                                    high_weights(g + 1, t - 1)
                                    if peeled:
                                        high_weights(g + 1, KD - 1)
                        return step

                    mean_square(0, 0, 1)
                    for g in range(3):
                        over_tiles(act, step_of(g))
                    take(2, T - 1, 1)

                @block.gpsimd
                def _(pool):
                    link = Chain(pool, c_pool)
                    link(nc.gpsimd.memset(ident[:], 0.0))
                    link(nc.gpsimd.affine_select(out=ident[:], in_=ident[:], compare_op=ALU.not_equal, fill=1.0,
                                                 base=0, pattern=[[-1, P]], channel_multiplier=1))
                    link(nc.gpsimd.memset(ones[:], 1.0))
                    link(nc.gpsimd.memset(eps_sb[:], EPS))
                    link(nc.gpsimd.memset(head_mean[:], 0.0))
                    for h in range(2):
                        link(nc.gpsimd.memset(head_mean[h * A_D:(h + 1) * A_D, h * A_D:(h + 1) * A_D], 1.0 / A_D))
                    link(nc.gpsimd.memset(tri16[:], 1.0 / GATE_TEMP))
                    link(nc.gpsimd.affine_select(out=tri16[:], in_=tri16[:], compare_op=ALU.is_ge, fill=0.0,
                                                 base=0, pattern=[[1, P]], channel_multiplier=-1))
                    link(nc.gpsimd.affine_select(out=before[:], in_=ones[:], compare_op=ALU.is_gt, fill=0.0,
                                                 base=0, pattern=[[1, P]], channel_multiplier=-1))

                @block.vector
                def _(dve):
                    dve.sem_inc(hT_ready, 2)
                    dve.wait_ge(load_small, 64)

                    def normalise(t, u):
                        dve.wait_ge(rms_ready, t + 1)
                        nc.vector.reciprocal(rstd[:, u:u + 1], msq[:, u:u + 1]).then_inc(rstd_ready, 1)
                        dve.wait_ge(rstd_ready, t + 1)
                        nc.vector.tensor_scalar(hn[u], xin[u], rstd[:, u:u + 1], None, ALU.mult).then_inc(hn_ready, 1)

                    def rest_of_weights(g, k):
                        dve.wait_ge(wvH_ready, k + g * KD + 1)
                        nc.vector.tensor_tensor(wvL[g % 2][:, bass.ds(k, 1), :], wraw[g % 2][:, bass.ds(k, 1), :],
                                                wvH[g % 2][:, bass.ds(k, 1), :].bitcast(F32),
                                                ALU.subtract).then_inc(wvL_ready, 1)

                    def swish(t, u):
                        dve.wait_ge(sg_ready, t + 1)
                        nc.vector.tensor_tensor(rs[:, bass.ds(t, 1), :], ps[:, 4 + u:5 + u, :],
                                                sg[u][:].unsqueeze(1), ALU.mult).then_inc(v_taken, 1)

                    def step_of(g):
                        def step(t, u):
                            peeled = isinstance(t, int)
                            tile = hT[:, :, bass.ds(t * P, P)]
                            if g == 0:
                                dve.wait_ge(hT_psum, t + 1)
                                nc.vector.tensor_tensor(tile, psT[u].rearrange("p (k c) -> p k c", k=KD),
                                                        g1_sb[:].unsqueeze(2).broadcast_to([P, KD, P]),
                                                        ALU.mult).then_inc(hT_ready, 1)
                            dve.wait_ge(hsH_ready, t + g * T + 1)
                            nc.vector.tensor_tensor(hsL[u][:], tile, hsH[u][:].bitcast(F32),
                                                    ALU.subtract).then_inc(hsL_ready, 1)
                            if g == 0 and not (peeled and t == T - 1):
                                normalise(t + 1, 1 - u)
                            if peeled and t == 0:
                                for k in range(KD if g == 0 else 0):
                                    rest_of_weights(0, k)
                            else:
                                if g < 2:
                                    rest_of_weights(g + 1, t - 1)
                                    if peeled:
                                        rest_of_weights(g + 1, KD - 1)
                                else:
                                    swish(t - 1, 1 - u)
                        return step

                    normalise(0, 0)
                    for g in range(3):
                        over_tiles(dve, step_of(g))
                    swish(T - 1, 1)

                @block.tensor
                def _(pe):
                    pe.sem_inc(v_psum, 2)
                    pe.sem_inc(v_taken, 2)
                    pe.wait_ge(c_pool, 10)

                    def transposes(t, u):
                        pe.wait_ge(hn_ready, t + 1)
                        pe.wait_ge(hT_ready, t + 1)
                        for k in range(KD):
                            mm = pe.transpose(psT[u][:, k * P:(k + 1) * P], hn[u][:, k * P:(k + 1) * P], ident[:])
                        mm.then_inc(hT_psum, 1)

                    def step_of(g):
                        def step(t, u):
                            q = t + g * T
                            peeled = isinstance(t, int)
                            if g == 0 and not (peeled and t == T - 1):
                                transposes(t + 1, 1 - u)
                            pe.wait_ge(hsL_ready, q + 1)
                            pe.wait_ge(v_taken, q + 1)
                            for k in range(KD):
                                if peeled and t == 0:
                                    pe.wait_ge(wvL_ready, g * KD + k + 1)
                                for n, (h, w) in enumerate(((hsH, wvH), (hsL, wvH), (hsH, wvL))):
                                    mm = pe.matmul(ps[:, 4 + u, :], h[u][:, k, :], w[g % 2][:, k, :],
                                                   start=(k == 0 and n == 0), stop=(k == KD - 1 and n == 2))
                            mm.then_inc(v_psum, 1)
                        return step

                    transposes(0, 0)
                    for g in range(3):
                        over_tiles(pe, step_of(g))

        UN = 2 * T
        BU = 2 * UN
        ahead = ExitStack()
        w_sb = [sb(f"w_sb{u}", [P, KD, 2 * P], ctx=ahead) for u in range(2)]
        raw = sb("raw", [P, 2, 2, SEQ], ctx=ahead)
        wlr_sb = sb("wlr_sb", [P, KD, RANK], ctx=ahead)
        gup_sb = sb("gup_sb", [RANK, B_QK], ctx=ahead)
        gbias_sb = sb("gbias_sb", [1, B_QK], ctx=ahead)
        with ExitStack() as st:
            qn = [sb(f"qn{u}", [P, SEQ], ctx=st) for u in range(2)]
            kn = [sb(f"kn{u}", [P, SEQ], ctx=st) for u in range(2)]
            sq = sb("sq", [P, 2, SEQ], ctx=st)
            bias = [sb(f"bias{u}", [P, 2, BANDW], ctx=st) for u in range(2)]
            ng = [sb(f"ng{u}", [P, BANDW], ctx=st) for u in range(2)]
            pr = [sb(f"pr{u}", [P, BANDW], ctx=st) for u in range(2)]
            prT = [sb(f"prT{u}", [P, BANDW], ctx=st) for u in range(2)]
            nmax = sb("nmax", [P, 2], ctx=st)
            rsum = sb("rsum", [P, 4], ctx=st)
            rinv = sb("rinv", [P, 2], ctx=st)
            ya = [sb(f"ya{u}", [P, P], ctx=st) for u in range(2)]
            bias_in = [sem(f"bias_in{u}") for u in range(2)]
            nx_psum = sem("nx_psum")
            nx_taken = sem("nx_taken")
            raw_sq = sem("raw_sq")
            logs = sem("logs")
            roots = sem("roots")
            band_dve = sem("band_dve")
            norm_done = sem("norm_done")
            score_psum = sem("score_psum")
            neg_ready = sem("neg_ready")
            prob_ready = sem("prob_ready")
            probT_psum = sem("probT_psum")
            probT_ready = sem("probT_ready")
            pv_psum = sem("pv_psum")
            ya_ready = sem("ya_ready")
            last_psum = sem("last_psum")
            yaT_done = sem("yaT_done")

            def unit(m):
                t = m % UN // 2
                n = min(t + 1, BAND_T)
                return m // UN, t, m % 2, t + 1 - n, n

            s_ps = [ps[:, 0:2, :].rearrange("p b c -> p (b c)"), ps[:, 2:4, :].rearrange("p b c -> p (b c)")]
            tr_ps = ps[:, 4:6, :].rearrange("p b c -> p (b c)")
            yT_ps = ps[:, 5, P:2 * P]
            share = [4, 4, 3, 3, 2, 3, 3, 2]
            PROJ_U = len(share)
            mm_of = [range(KD + sum(share[:u]), KD + sum(share[:u + 1])) for u in range(PROJ_U)]
            group_end = {u: m[-1] // KD for u, m in enumerate(mm_of) if (m[-1] + 1) % KD == 0}
            ROOT_U = PROJ_U + 4

            with nc.Block() as block:
                @block.sync
                def _(sp):
                    sp.dma_start(w_sb[1][:], wqk[1]).then_inc(w_in[1], 16)

                    def load_bias(pair, u):
                        sp.dma_start(bias[u][0:CHUNK, :, 0:BANDW - CHUNK],
                                     relx[pair, 0:CHUNK, :, 0:BANDW - CHUNK]).then_inc(bias_in[u], 16)
                        sp.dma_start(bias[u][CHUNK:P, :, CHUNK:BANDW],
                                     relx[pair, CHUNK:P, :, CHUNK:BANDW]).then_inc(bias_in[u], 16)

                    for u in range(2):
                        load_bias(u, u)
                    sp.dma_start(wlr_sb[:], wlr).then_inc(load_small, 16)
                    sp.dma_start(gup_sb[:], gup).then_inc(load_small, 16)
                    sp.dma_start(gbias_sb[:], gbias).then_inc(load_small, 16)
                    for pair in range(2, A_PAIRS + 2):
                        u = pair % 2
                        sp.wait_ge(nx_psum, (pair - 2) * 8 + 4)
                        sp.dma_start(w_sb[u][:], wqk[pair]).then_inc(w_in[u], 16)
                        if pair < A_PAIRS:
                            sp.wait_ge(neg_ready, (pair - 1) * UN + 2)
                            load_bias(pair, u)

                @block.tensor
                def _(pe):
                    pe.sem_inc(probT_psum, 2)
                    pe.sem_inc(pv_psum, 2)

                    def project(par, uses, n):
                        g, k = n // KD, n % KD
                        first = isinstance(uses, int) and uses == 0
                        if k == 0 and not first:
                            pe.wait_ge(nx_taken, uses + g + 1)
                        mm = pe.matmul(ps[:, g if first else 7, :], (w_first if first else w_sb[par])[:, k, (g // 2) * P:(g // 2 + 1) * P],
                                       hT[:, k, (g % 2) * HALF:(g % 2 + 1) * HALF],
                                       start=(k == 0), stop=(k == KD - 1))
                        if k == KD - 1:
                            mm.then_inc(nx_psum, 1)

                    def mean_square(uses, n0, j):
                        pe.wait_ge(raw_sq, n0 + j + 1)
                        first = isinstance(uses, int) and uses == 0
                        if not first:
                            pe.wait_ge(nx_taken, uses + 4 + j + 1)
                        pe.matmul(ps[:, 4 + j if first else 7, :], head_mean[:], sq[:, j // 2, (j % 2) * HALF:(j % 2 + 1) * HALF],
                                  start=True, stop=True).then_inc(nx_psum, 1)

                    pe.wait_ge(w_in[0], 16)
                    for n in range(4 * KD):
                        project(0, 0, n)
                    for j in range(4):
                        mean_square(0, 0, j)
                    pe.wait_ge(w_in[1], 16)
                    for n in range(KD):
                        project(1, 8, n)
                    with pe.Fori(0, A_PAIRS // 2) as i:
                        n0 = i * BU
                        for s in range(BU + 2):
                            if s < BU:
                                pp, t, h, k0, nk = unit(s)
                                nxt = i * 2 + pp + 1
                                su = s % UN
                                if su == 0:
                                    pe.wait_ge(norm_done, (i * 2 + pp) * 2 + 2)
                                hd = slice(h * A_D, (h + 1) * A_D)
                                pe.wait_ge(neg_ready, n0 + s + 1)
                                for c in range(0, nk * P, HALF):
                                    w = min(HALF, nk * P - c)
                                    mm = pe.matmul(s_ps[s % 2][:, c:c + w], qn[pp][hd, t * P:(t + 1) * P],
                                                   kn[pp][hd, k0 * P + c:k0 * P + c + w], start=True, stop=True)
                                mm.then_inc(score_psum, 1)
                                if su < PROJ_U:
                                    for n in mm_of[su]:
                                        project(1 - pp, nxt * 8, n)
                                elif su < PROJ_U + 4:
                                    mean_square(nxt * 8, nxt * 4, su - PROJ_U)
                                elif su == ROOT_U:
                                    pe.wait_ge(w_in[pp], i * 16 + 32)
                                    for n in range(KD):
                                        project(pp, nxt * 8 + 8, n)
                            if 0 <= s - 1 < BU:
                                m = s - 1
                                pp, t, h, k0, nk = unit(m)
                                pe.wait_ge(prob_ready, n0 + m + 3)
                                pe.wait_ge(probT_ready, n0 + m + 1)
                                for j in range(nk):
                                    mm = pe.transpose(tr_ps[:, j * P:(j + 1) * P], pr[m % 2][:, j * P:(j + 1) * P],
                                                      ident[:])
                                if m == 0:
                                    pe.wait_ge(yaT_done, i * 2 * T + 1)
                                if m >= 3 and m % 2 == 1:
                                    pe.wait_ge(ya_ready, n0 + m + 3)
                                    mm = pe.transpose(yT_ps, ya[(m - 3) // 2 % 2][:], ident[:])
                                mm.then_inc(probT_psum, 1)
                            if 0 <= s - 2 < BU:
                                m = s - 2
                                pp, t, h, k0, nk = unit(m)
                                pe.wait_ge(probT_ready, n0 + m + 2)
                                pe.wait_ge(ya_ready, n0 + m + 4)
                                for j in range(nk):
                                    mm = pe.matmul(ps[:, 6, h * A_D:(h + 1) * A_D], prT[m % 2][:, j * P:(j + 1) * P],
                                                   va[:, k0 + j, bass.ds((i * 2 + pp) * P + h * A_D, A_D)],
                                                   start=(j == 0), stop=(j == nk - 1))
                                mm.then_inc(pv_psum, 1)
                        pe.wait_ge(ya_ready, n0 + BU + 4)
                        pe.transpose(yT_ps, ya[1][:], ident[:]).then_inc(last_psum, 1)

                @block.scalar
                def _(act):
                    act.sem_inc(prob_ready, 2)
                    act.sem_inc(probT_ready, 1)
                    act.sem_inc(yaT_done, 1)
                    act.sem_inc(nx_taken, 1)

                    def take_projection(par, uses, g, bank=7):
                        act.wait_ge(nx_psum, uses + g + 1)
                        cols = slice((g % 2) * HALF, (g % 2 + 1) * HALF)
                        nc.scalar.activation(sq[:, g // 2, cols], ps[:, bank, :], ACT.Square).then_inc(raw_sq, 1)
                        nc.scalar.copy(raw[:, par, g // 2, cols], ps[:, bank, :]).then_inc(nx_taken, 1)

                    def take_mean_square(uses, j, bank=7):
                        act.wait_ge(nx_psum, uses + 4 + j + 1)
                        nc.scalar.copy(sq[:, j // 2, (j % 2) * HALF:(j % 2 + 1) * HALF],
                                       ps[:, bank, :]).then_inc(nx_taken, 1)

                    def take_roots(pair):
                        act.wait_ge(nx_taken, pair * 8 + 9)
                        nc.scalar.activation(sq[:], sq[:], ACT.Ln, bias=eps_sb[:]).then_inc(logs, 1)
                        act.wait_ge(logs, pair + 1)
                        nc.scalar.activation(sq[:], sq[:], ACT.Exp, scale=-0.5).then_inc(roots, 1)

                    def take_tile(i, tt):
                        nc.scalar.activation(yaT[:, i * 2 + tt // T, (tt % T) * P:(tt % T + 1) * P], yT_ps,
                                             ACT.Copy).then_inc(yaT_done, 1)

                    for g in range(4):
                        take_projection(0, 0, g, bank=g)
                    for j in range(4):
                        take_mean_square(0, j, bank=4 + j)
                    take_roots(0)
                    act.wait_ge(norm_done, 2)
                    take_projection(1, 8, 0)
                    with act.Fori(0, A_PAIRS // 2) as i:
                        n0 = i * BU
                        for s in range(BU + 1):
                            if s < BU:
                                pp, t, h, k0, nk = unit(s)
                                w = nk * P
                                su, nxt = s % UN, i * 2 + pp + 1
                                if su - 1 in group_end:
                                    take_projection(1 - pp, nxt * 8, group_end[su - 1])
                                if su == ROOT_U + 1:
                                    act.wait_ge(norm_done, nxt * 2 + 2)
                                    take_projection(pp, nxt * 8 + 8, 0)
                                act.wait_ge(neg_ready, n0 + s + 3)
                                act.wait_ge(probT_psum, n0 + s + 1)
                                act.wait_ge(ya_ready, n0 + s + 1)
                                nc.scalar.activation(pr[s % 2][:, :w], ng[s % 2][:, :w], ACT.Exp,
                                                     bias=nmax[:, s % 2:s % 2 + 1], scale=-1.0,
                                                     accum_out=rsum[:, s % 4:s % 4 + 1]).then_inc(prob_ready, 1)
                                if 0 <= su - PROJ_U < 4:
                                    take_mean_square(nxt * 8, su - PROJ_U)
                            if 0 <= s - 1 < BU:
                                m = s - 1
                                w = unit(m)[4] * P
                                act.wait_ge(probT_psum, n0 + m + 3)
                                if m >= 3 and m % 2 == 1:
                                    take_tile(i, (m - 3) // 2)
                                act.wait_ge(pv_psum, n0 + m + 1)
                                nc.scalar.copy(prT[m % 2][:, :w], tr_ps[:, :w]).then_inc(probT_ready, 1)
                            if s < BU and s % UN == ROOT_U - 1:
                                take_roots(i * 2 + s // UN + 1)
                        act.wait_ge(last_psum, i + 1)
                        apart(act)
                        take_tile(i, 2 * T - 1)

                @block.vector
                def _(dve):
                    dve.sem_inc(neg_ready, 2)
                    dve.sem_inc(ya_ready, 4)
                    link0 = Chain(dve, c_dve)
                    link0(nc.vector.memset(qg_sb[:, A_PAIRS:], 1.0))
                    link0(nc.vector.memset(kg_sb[:, A_PAIRS:], 1.0))
                    link0(nc.vector.tensor_scalar(qg_sb[:], qg_sb[:], A_D ** -0.5, None, ALU.mult))
                    for u in range(2):
                        link0(nc.vector.memset(bias[u][0:CHUNK, :, BANDW - CHUNK:BANDW], NEG))
                        link0(nc.vector.memset(bias[u][CHUNK:P, :, 0:CHUNK], NEG))

                    def norm(pair, par, b):
                        gain, dst = ((qg_sb, qn), (kg_sb, kn))[b]
                        dve.wait_ge(roots, pair + 1)
                        nc.vector.scalar_tensor_tensor(out=dst[par][:], in0=raw[:, par, b, :],
                                                       scalar=gain[:, bass.ds(pair, 1)], in1=sq[:, b, :],
                                                       op0=ALU.mult, op1=ALU.mult).then_inc(norm_done, 1)

                    norm(0, 0, 0)
                    norm(0, 0, 1)
                    with dve.Fori(0, A_PAIRS // 2) as i:
                        n0 = i * BU
                        link = Chain(dve, band_dve, i * BU)
                        for s in range(BU + 2):
                            if s < BU:
                                pp, t, h, k0, nk = unit(s)
                                w = nk * P
                                dve.wait_ge(score_psum, n0 + s + 1)
                                if s % UN == 0:
                                    dve.wait_ge(bias_in[pp], i * 32 + 32)
                                dve.wait_ge(prob_ready, n0 + s + 1)
                                apart(dve)
                                nc.vector.tensor_tensor_reduce(
                                    out=ng[s % 2][:, :w], in0=s_ps[s % 2][:, :w], in1=bias[pp][:, s % 2, BANDW - w:BANDW],
                                    scale=-1.0, scalar=1e38, op0=ALU.add, op1=ALU.min,
                                    accum_out=nmax[:, s % 2:s % 2 + 1]).then_inc(neg_ready, 1)
                            if 0 <= s - 2:
                                m = s - 2
                                pp, t, h, k0, nk = unit(m)
                                dve.wait_ge(pv_psum, n0 + m + 3)
                                link(nc.vector.reciprocal(rinv[:, h:h + 1], rsum[:, m % 4:m % 4 + 1]))
                                dve.wait_ge(probT_psum, n0 + m // 2 * 2 + 2)
                                if m // 2 == 1:
                                    dve.wait_ge(yaT_done, i * 2 * T + 1)
                                nc.vector.tensor_scalar(ya[t % 2][:, h * A_D:(h + 1) * A_D],
                                                        ps[:, 6, h * A_D:(h + 1) * A_D], rinv[:, h:h + 1], None,
                                                        ALU.mult).then_inc(ya_ready, 1)
                            if s < BU and s % UN == ROOT_U:
                                for b in range(2):
                                    norm(i * 2 + s // UN + 1, 1 - s // UN, b)

        with ExitStack() as st:
            lrT = sb("lrT", [RANK, SEQ], ctx=st)
            masks = sb("masks", [P, LEVELS, P], I32, ctx=st)
            ii = sb("ii", [P, P], I32, ctx=st)
            jj = sb("jj", [P, P], I32, ctx=st)
            vf = sb("vf", [P, P], ctx=st)
            tf = sb("tf", [P, P], ctx=st)
            bq = sb("bq", [P, SEQ], ctx=st)
            bk = sb("bk", [P, SEQ], ctx=st)
            gm = sb("gm", [P, SEQ], ctx=st)
            t1 = sb("t1", [P, SEQ], ctx=st)
            t2 = sb("t2", [P, SEQ], ctx=st)
            gl = sb("gl", [P, SEQ], ctx=st)
            cum = sb("cum", [P, SEQ], ctx=st)
            qe = sb("qe", [P, SEQ], ctx=st)
            kdT = w_sb[0][:, 4:8, :].rearrange("p k (a c) -> p (k a) c", c=P)
            df = [sb(f"df{u}", [P, SEQ], ctx=st) for u in range(2)]
            ef = [t1, t2]
            att = va[:, 0:4, :].rearrange("p t (a c) -> p (t a) c", c=P)
            ql = [gm, va[:, 4:6, :].rearrange("p t c -> p (t c)")]
            kl = [gl, va[:, 6:8, :].rearrange("p t c -> p (t c)")]
            state = [sb(f"state{u}", [P, P], ctx=st) for u in range(2)]
            elast = sb("elast", [P, T], ctx=st)
            junk = sb("junk_g", [P, 2, P], ctx=st)
            oms = sb("oms", [P, 2, 2], ctx=st)
            ors = sb("ors", [P, 2, 2], ctx=st)
            yb = [w_sb[0][:, u, :] for u in range(2)]
            g_consts = sem("g_consts")
            iota_ready = sem("iota_ready")
            lr_psum = sem("lr_psum")
            lr_ready = sem("lr_ready")
            g_qk_psum = sem("g_qk_psum")
            g_raw_ready = sem("g_raw_ready")
            z_psum = sem("z_psum")
            g_qk_ready = sem("g_qk_ready")
            sp_act = sem("softplus_act")
            gla_dve = sem("gla_dve")
            decay_ready = sem("decay_ready")
            cum_psum = sem("cum_psum")
            cum_ready = sem("cum_ready")
            tail_diff = sem("tail_diff")
            head_exp = sem("head_exp")
            tail_exp = sem("tail_exp")
            kd_ready = sem("kd_ready")
            kd_psum = sem("kd_psum")
            kdT_ready = sem("kdT_ready")
            diff_ready = sem("diff_ready")
            exp_ready = sem("exp_ready")
            lev_ready = sem("lev_ready")
            lev_psum = sem("lev_psum")
            att_part = sem("att_part")
            o_psum = sem("o_psum")
            u_psum = sem("u_psum")
            st_ready = sem("st_ready")
            oms_ready = sem("oms_ready")
            orms_ready = sem("orms_ready")
            yb_ready = sem("yb_ready")
            ybT_psum = sem("ybT_psum")
            ybT_done = sem("ybT_done")
            two = lambda b: ps[:, b:b + 2, :].rearrange("p b c -> p (b c)")
            NL = LEVELS - 1

            with nc.Block() as block:
                @block.gpsimd
                def _(pool):
                    nc.gpsimd.iota(ii[:], pattern=[[1, P]], base=0, channel_multiplier=0).then_inc(iota_ready, 1)
                    nc.gpsimd.iota(jj[:], pattern=[[0, P]], base=0, channel_multiplier=1).then_inc(iota_ready, 1)

                @block.tensor
                def _(pe):
                    pe.sem_inc(ybT_psum, 2)
                    pe.wait_ge(load_small, 64 + 48)
                    for half in range(2):
                        for k in range(KD):
                            mm = pe.matmul(ps[0:RANK, 6 + half, :], wlr_sb[:, k, :],
                                           hT[:, k, half * HALF:(half + 1) * HALF],
                                           start=(k == 0), stop=(k == KD - 1))
                    mm.then_inc(lr_psum, 1)
                    pe.wait_ge(w_in[1], 48)

                    def project_second(b):
                        for half in range(1 - b, 2):
                            for k in range(KD):
                                mm = pe.matmul(ps[:, 2 * b + half, :], w_sb[1][:, k, b * P:(b + 1) * P],
                                               hT[:, k, half * HALF:(half + 1) * HALF],
                                               start=(k == 0), stop=(k == KD - 1))
                        mm.then_inc(g_qk_psum, 1)

                    with pe.Fori(0, B_PAIRS) as p:
                        pe.wait_ge(ybT_done, p * T + 2)
                        pe.wait_ge(lr_ready, 1)
                        for t in range(T):
                            z = ps[:, 4 + t // 4, (t % 4) * P:(t % 4 + 1) * P]
                            pe.matmul(z, lrT[:, t * P:(t + 1) * P], gup_sb[:, bass.ds(p * P, P)],
                                      start=True, stop=False)
                            mm = pe.matmul(z, ones[0:1, :], gbias_sb[:, bass.ds(p * P, P)], start=False, stop=True)
                        mm.then_inc(z_psum, 1)
                        with pe.If(p < 1):
                            project_second(0)
                        pe.wait_ge(decay_ready, p + 1)
                        for t in range(T):
                            mm = pe.matmul(ps[:, 6 + t // 4, (t % 4) * P:(t % 4 + 1) * P], gl[:, t * P:(t + 1) * P],
                                           tri16[:], start=True, stop=True)
                        mm.then_inc(cum_psum, 1)
                        with pe.If(p < 1):
                            project_second(1)
                        pe.wait_ge(kd_ready, p + 1)
                        for t in range(T):
                            mm = pe.transpose(ps[:, 4 + t // 4, (t % 4) * P:(t % 4 + 1) * P],
                                              df[0][:, t * P:(t + 1) * P], ident[:])
                        mm.then_inc(kd_psum, 1)
                        pe.wait_ge(g_raw_ready, 2)
                        for l in range(LEVELS):
                            pe.wait_ge(lev_ready, p * LEVELS + l + 1)
                            if l == 1:
                                pe.wait_ge(kdT_ready, p + 1)
                            if l >= 2:
                                pe.wait_ge(att_part, p * LEVELS + l - 1)
                            kk, qq = (bk, bq) if l == 0 else (kl[l % 2], ql[l % 2])
                            for n in range(2 * T):
                                t, h = n % T, n // T
                                hd = slice(h * B_DK, (h + 1) * B_DK)
                                mm = pe.matmul(ps[:, (l % 2) * 4 + n // 4, (n % 4) * P:(n % 4 + 1) * P],
                                               kk[hd, t * P:(t + 1) * P], qq[hd, t * P:(t + 1) * P],
                                               start=True, stop=True)
                            mm.then_inc(lev_psum, 1)
                        pe.wait_ge(att_part, p * LEVELS + LEVELS)
                        for t in range(T + 1):
                            if t < T:
                                pe.wait_ge(yb_ready, p * T + t + 1)
                                if t >= 1:
                                    pe.wait_ge(st_ready, p * T + t)
                                for h in range(2):
                                    hd = slice(h * B_DK, (h + 1) * B_DK)
                                    o = ps[:, (t % 2) * 2 + h, 0:P]
                                    mm = pe.matmul(o, att[:, h * T + t, :], vb[:, t, bass.ds(p * 2 * P + h * P, P)],
                                                   start=True, stop=(t == 0))
                                    if t >= 1:
                                        mm = pe.matmul(o, qe[hd, t * P:(t + 1) * P], state[(t - 1) % 2][hd, :],
                                                       start=False, stop=True)
                                mm.then_inc(o_psum, 1)
                                pe.matmul(ps[:, 4 + t % 2, 0:2 * P], kdT[:, t, :], vb[:, t, bass.ds(p * 2 * P, 2 * P)],
                                          start=True, stop=True).then_inc(u_psum, 1)
                            if t >= 1:
                                m = t - 1
                                pe.wait_ge(yb_ready, p * T + m + 3)
                                pe.wait_ge(ybT_done, p * T + m + 1)
                                for h in range(2):
                                    mm = pe.transpose(ps[:, 6 + m % 2, h * P:(h + 1) * P],
                                                      yb[m % 2][:, h * P:(h + 1) * P], ident[:])
                                mm.then_inc(ybT_psum, 1)

                @block.scalar
                def _(act):
                    act.sem_inc(g_qk_ready, 1)
                    act.wait_ge(lr_psum, 1)
                    nc.scalar.copy(lrT[:], ps[0:RANK, 6:8, :].rearrange("p b c -> p (b c)")).then_inc(lr_ready, 1)
                    act.sem_inc(g_raw_ready, 1)
                    with act.Fori(0, B_PAIRS) as p:
                        act.wait_ge(g_raw_ready, p + 1)
                        act.wait_ge(yb_ready, p * T + 2)
                        rw = raw[:, bass.ds(p, 1), :, :].squeeze(1)
                        nc.scalar.activation(bq[:], rw[:, 0, :], ACT.Copy, scale=B_DK ** -0.5).then_inc(g_qk_ready, 1)
                        nc.scalar.activation(bk[:], rw[:, 1, :], ACT.Copy).then_inc(g_qk_ready, 1)
                        act.wait_ge(z_psum, p + 1)
                        link = Chain(act, sp_act, p * 3)
                        link(nc.scalar.activation(t1[:], two(4), ACT.Abs))
                        link(nc.scalar.activation(t2[:], t1[:], ACT.Exp, scale=-1.0))
                        link(nc.scalar.activation(gl[:], t2[:], ACT.Ln, bias=1.0))
                        act.wait_ge(cum_ready, p + 1)
                        nc.scalar.activation(qe[:], cum[:], ACT.Exp).then_inc(head_exp, 1)
                        act.wait_ge(tail_diff, p + 1)
                        nc.scalar.activation(t2[:], t1[:], ACT.Exp).then_inc(tail_exp, 1)
                        act.wait_ge(kd_psum, p + 1)
                        nc.scalar.copy(kdT, two(4).rearrange("p (t c) -> p t c", c=P)).then_inc(kdT_ready, 1)
                        with act.If(p < 1):
                            act.wait_ge(g_qk_psum, 1)
                            nc.scalar.copy(raw[:, 1, 0, HALF:], ps[:, 1, :])
                            act.wait_ge(g_qk_psum, 2)
                            nc.scalar.copy(raw[:, 1, 1, :], two(2)).then_inc(g_raw_ready, 1)
                        for l in range(1, LEVELS):
                            act.wait_ge(diff_ready, p * NL + l)
                            nc.scalar.activation(ef[l % 2][:], df[l % 2][:], ACT.Exp).then_inc(exp_ready, 1)
                        for t in range(T):
                            act.wait_ge(o_psum, p * T + t + 1)
                            act.wait_ge(yb_ready, p * T + t + 1)
                            for h in range(2):
                                nc.scalar.activation(junk[:, h, :], ps[:, (t % 2) * 2 + h, 0:P], ACT.Square,
                                                     scale=B_DV ** -0.5,
                                                     accum_out=oms[:, t % 2, h:h + 1]).then_inc(oms_ready, 1)
                            act.wait_ge(oms_ready, (p * T + t) * 2 + 2)
                            nc.scalar.activation(oms[:, t % 2, :], oms[:, t % 2, :], ACT.Sqrt,
                                                 bias=eps_sb[:]).then_inc(orms_ready, 1)

                @block.vector
                def _(dve):
                    dve.sem_inc(yb_ready, 2)
                    dve.sem_inc(ybT_done, 2)
                    link = Chain(dve, g_consts)
                    dve.wait_ge(iota_ready, 2)
                    link(nc.vector.tensor_tensor(masks[:, 0, :], ii[:], jj[:], ALU.bitwise_xor))
                    link(nc.vector.tensor_copy(vf[:], masks[:, 0, :]))
                    link(nc.vector.tensor_tensor(tf[:], ii[:], jj[:], ALU.is_ge))
                    link(nc.vector.scalar_tensor_tensor(out=vf[:], in0=vf[:], scalar=1.0, in1=tf[:],
                                                        op0=ALU.add, op1=ALU.mult))
                    link(nc.vector.tensor_scalar(masks[:, 0, :], vf[:], 1.0, None, ALU.is_equal))
                    for l in range(1, LEVELS):
                        c = 1 << (l - 1)
                        link(nc.vector.tensor_scalar(tf[:], vf[:], float(2 * c + 1), None, ALU.is_lt))
                        link(nc.vector.scalar_tensor_tensor(out=masks[:, l, :], in0=vf[:], scalar=float(c + 1),
                                                            in1=tf[:], op0=ALU.is_ge, op1=ALU.mult))
                    link(nc.vector.memset(att[:], 0.0))
                    link(nc.vector.memset(ql[1][:], 0.0))
                    link(nc.vector.memset(kl[1][:], 0.0))

                    def halves(a, c):
                        v = a[:].rearrange("p (n s c) -> p n s c", s=2, c=c)
                        return v[:, :, 0, :], v[:, :, 1, :]

                    with dve.Fori(0, B_PAIRS) as p:
                        link = Chain(dve, gla_dve, p * (3 + NL * 3 + 4 * T))
                        dve.wait_ge(sp_act, p * 3 + 1)
                        link(nc.vector.tensor_scalar(gm[:], two(4), 0.0, None, ALU.min))
                        dve.wait_ge(sp_act, p * 3 + 3)
                        nc.vector.tensor_tensor(gl[:], gm[:], gl[:], ALU.subtract).then_inc(decay_ready, 1)
                        dve.wait_ge(cum_psum, p + 1)
                        nc.vector.tensor_copy(cum[:], two(6)).then_inc(cum_ready, 1)
                        dve.wait_ge(cum_ready, p + 1)
                        c3 = cum[:].rearrange("p (t c) -> p t c", c=P)
                        nc.vector.tensor_tensor(t1[:].rearrange("p (t c) -> p t c", c=P),
                                                c3[:, :, P - 1:P].broadcast_to([P, T, P]), c3,
                                                ALU.subtract).then_inc(tail_diff, 1)
                        dve.wait_ge(head_exp, p + 1)
                        link(nc.vector.tensor_copy(elast[:], qe[:].rearrange("p (t c) -> p t c", c=P)[:, :, P - 1]))
                        dve.wait_ge(g_qk_ready, p * 2 + 3)
                        link(nc.vector.tensor_tensor(qe[:], qe[:], bq[:], ALU.mult))
                        dve.wait_ge(tail_exp, p + 1)
                        nc.vector.tensor_tensor(df[0][:], bk[:], t2[:], ALU.mult).then_inc(kd_ready, 1)
                        dve.wait_ge(kd_psum, p + 1)
                        dve.sem_inc(lev_ready, 1)

                        def diff(l):
                            c = 1 << (l - 1)
                            lo, hi = halves(cum, c)
                            dlo, dhi = halves(df[l % 2], c)
                            ref = lo[:, :, c - 1:c].broadcast_to([P, SEQ // (2 * c), c])
                            link(nc.vector.tensor_tensor(dlo, ref, lo, ALU.subtract))
                            nc.vector.tensor_tensor(dhi, hi, ref, ALU.subtract).then_inc(diff_ready, 1)

                        def take(l):
                            dve.wait_ge(lev_psum, p * LEVELS + l + 1)
                            apart(dve)
                            b = (l % 2) * 4
                            nc.vector.copy_predicated(
                                att[:], masks[:, l:l + 1, :].broadcast_to([P, 2 * T, P]),
                                ps[:, b:b + 4, :].rearrange("p b (n c) -> p (b n) c", c=P)).then_inc(att_part, 1)

                        diff(1)
                        for l in range(1, LEVELS):
                            if l + 1 < LEVELS:
                                diff(l + 1)
                            c = 1 << (l - 1)
                            dve.wait_ge(exp_ready, p * NL + l)
                            elo, ehi = halves(ef[l % 2], c)
                            link(nc.vector.tensor_tensor(halves(kl[l % 2], c)[0], halves(bk, c)[0], elo, ALU.mult))
                            link(nc.vector.tensor_tensor(halves(ql[l % 2], c)[1], halves(bq, c)[1], ehi, ALU.mult))
                            dve.sem_inc(lev_ready, 1)
                            take(l - 1)
                            dve.wait_ge(att_part, p * LEVELS + l)
                        take(LEVELS - 1)
                        for t in range(T + 1):
                            if t < T:
                                dve.wait_ge(u_psum, p * T + t + 1)
                                for h in range(2):
                                    hd = slice(h * B_DK, (h + 1) * B_DK)
                                    u = ps[hd, 4 + t % 2, h * P:(h + 1) * P]
                                    if t == 0:
                                        ins = nc.vector.tensor_copy(state[0][hd, :], u)
                                    else:
                                        ins = nc.vector.scalar_tensor_tensor(
                                            out=state[t % 2][hd, :], in0=state[(t - 1) % 2][hd, :],
                                            scalar=elast[hd, t:t + 1], in1=u, op0=ALU.mult, op1=ALU.add)
                                    if h == 0:
                                        link(ins)
                                ins.then_inc(st_ready, 1)
                                dve.wait_ge(st_ready, p * T + t + 1)
                                dve.wait_ge(orms_ready, p * T + t + 1)
                                link(nc.vector.reciprocal(ors[:, t % 2, :], oms[:, t % 2, :]))
                                dve.wait_ge(ybT_psum, p * T + t + 1)
                                for h in range(2):
                                    ins = nc.vector.scalar_tensor_tensor(
                                        out=yb[t % 2][:, h * P:(h + 1) * P], in0=ps[:, (t % 2) * 2 + h, 0:P],
                                        scalar=ors[:, t % 2, h:h + 1], in1=rs[:, t, bass.ds(p * 2 * P + h * P, P)],
                                        op0=ALU.mult, op1=ALU.mult)
                                    if h == 0:
                                        link(ins)
                                ins.then_inc(yb_ready, 1)
                            if t >= 1:
                                m = t - 1
                                dve.wait_ge(ybT_psum, p * T + m + 3)
                                for h in range(2):
                                    ins = nc.vector.tensor_scalar(
                                        ybT[:, p * 2 + h, m * P:(m + 1) * P], ps[:, 6 + m % 2, h * P:(h + 1) * P],
                                        bog_sb[:, bass.ds(p * 2 + h, 1)], None, ALU.mult)
                                    if h == 0:
                                        link(ins)
                                ins.then_inc(ybT_done, 1)
        ahead.close()
        mid.close()

        mT = hT
        with ExitStack() as st:
            GATES = 2 * KD * P
            PA, PB = GATES, GATES + (A_W // P) * P
            WD = PB + (B_V // P) * P
            wd_sb = [sb(f"wd{u}", [P, WD], ctx=st) for u in range(2)]
            wH = [sb(f"wH{u}", [P, GATES], F32R, ctx=st) for u in range(2)]
            wL = [sb(f"wL{u}", [P, GATES], F32R, ctx=st) for u in range(2)]
            hH = sb("hH", [P, KD, SEQ], F32R, ctx=st)
            hL = sb("hL", [P, KD, SEQ], F32R, ctx=st)
            gs = [sb(f"gs{u}", [P, 2, HALF], ctx=st) for u in range(2)]
            m1 = sb("m1", [P, HALF], ctx=st)
            m2 = sb("m2", [P, HALF], ctx=st)
            wd_in = [sem(f"wd_in{u}") for u in range(2)]
            wH_ready = sem("wH_ready")
            wL_ready = sem("wL_ready")
            hH_ready = sem("hH_ready")
            hL_ready = sem("hL_ready")
            d_psum = sem("d_psum")
            gs_ready = sem("gs_ready")
            m_dve = sem("m_dve")
            m_done = sem("m_done")
            with nc.Block() as block:
                @block.sync
                def _(sp):
                    with sp.Fori(0, KD // 2) as i:
                        for u in range(2):
                            sp.wait_ge(d_psum, (i * 2 + u) * 2 + 2)
                            sp.dma_start(wd_sb[u][:], wd[i * 2 + u]).then_inc(wd_in[u], 16)

                @block.tensor
                def _(pe):
                    pe.sem_inc(d_psum, 4)

                    def branches(u, half):
                        cols = slice(half * HALF, (half + 1) * HALF)
                        for b, base, src in ((2, PA, yaT), (3, PB, ybT)):
                            for k in range(A_W // P):
                                mm = pe.matmul(ps[:, half * 4 + b, :], wd_sb[u][:, base + k * P:base + (k + 1) * P],
                                               src[:, k, cols], start=(k == 0), stop=(k == A_W // P - 1))
                        return mm

                    def gates(u, half, split):
                        cols = slice(half * HALF, (half + 1) * HALF)
                        for b in range(2):
                            for k in range(KD):
                                if split and b == 0:
                                    pe.wait_ge(hL_ready, k + 1)
                                piece = slice((b * KD + k) * P, (b * KD + k + 1) * P)
                                for n, (w, h) in enumerate(((wH, hH), (wH, hL), (wL, hH))):
                                    mm = pe.matmul(ps[:, half * 4 + b, :], w[u][:, piece], h[:, k, cols],
                                                   start=(k == 0 and n == 0), stop=(k == KD - 1 and n == 2))
                        return mm

                    def blk(d, u, n, split):
                        pe.wait_ge(wd_in[u], n * 16)
                        pe.wait_ge(m_done, d * 2 + 1)
                        branches(u, 0)
                        pe.wait_ge(wL_ready, d + 1)
                        gates(u, 0, split).then_inc(d_psum, 1)
                        pe.wait_ge(m_done, d * 2 + 2)
                        branches(u, 1)
                        gates(u, 1, False).then_inc(d_psum, 1)

                    for d in range(2):
                        blk(d, d, 1, d == 0)
                    with pe.Fori(1, KD // 2) as i:
                        for u in range(2):
                            blk(i * 2 + u, u, i + 1, False)

                @block.scalar
                def _(act):
                    def split_weights(u, n):
                        act.wait_ge(wd_in[u], n * 16)
                        nc.scalar.copy(wH[u][:], wd_sb[u][:, 0:GATES]).then_inc(wH_ready, 1)

                    def sigmoids(n, half):
                        act.wait_ge(d_psum, n + 5)
                        act.wait_ge(m_done, n + 1)
                        nc.scalar.activation(gs[half][:], ps[:, half * 4:half * 4 + 2, :],
                                             ACT.Sigmoid).then_inc(gs_ready, 1)

                    nc.scalar.copy(hH[:, 0, :], hT[:, 0, :]).then_inc(hH_ready, 1)
                    split_weights(0, 1)
                    for k in range(1, KD):
                        nc.scalar.copy(hH[:, k, :], hT[:, k, :]).then_inc(hH_ready, 1)
                    split_weights(1, 1)
                    for n in range(2):
                        sigmoids(n, n)
                    with act.Fori(1, KD // 2) as i:
                        for u in range(2):
                            split_weights(u, i + 1)
                            for half in range(2):
                                sigmoids((i * 2 + u - 1) * 2 + half, half)
                    for half in range(2):
                        sigmoids((KD - 1) * 2 + half, half)

                @block.vector
                def _(dve):
                    dve.sem_inc(m_done, 2)

                    def rest_of_weights(d, u):
                        dve.wait_ge(wH_ready, d + 1)
                        nc.vector.tensor_tensor(wL[u][:], wd_sb[u][:, 0:GATES], wH[u][:].bitcast(F32),
                                                ALU.subtract).then_inc(wL_ready, 1)

                    def merged(d, half):
                        n = d * 2 + half
                        link = Chain(dve, m_dve, n * 2)
                        dve.wait_ge(gs_ready, n + 1)
                        dve.wait_ge(m_done, n + 2)
                        link(nc.vector.tensor_tensor(m1[:], gs[half][:, 0, :], ps[:, half * 4 + 2, :], ALU.mult))
                        link(nc.vector.tensor_tensor(m2[:], gs[half][:, 1, :], ps[:, half * 4 + 3, :], ALU.mult))
                        nc.vector.tensor_tensor(mT[:, d, half * HALF:(half + 1) * HALF], m1[:], m2[:],
                                                ALU.add).then_inc(m_done, 1)

                    for k in range(KD):
                        dve.wait_ge(hH_ready, k + 1)
                        nc.vector.tensor_tensor(hL[:, k, :], hT[:, k, :], hH[:, k, :].bitcast(F32),
                                                ALU.subtract).then_inc(hL_ready, 1)
                        if k == 0:
                            rest_of_weights(0, 0)
                    dve.wait_ge(hL_ready, KD)
                    rest_of_weights(1, 1)
                    for half in range(2):
                        merged(0, half)
                    with dve.Fori(1, KD // 2) as i:
                        for u in range(2):
                            rest_of_weights(i * 2 + u, u)
                            for half in range(2):
                                merged(i * 2 + u - 1, half)
                    for half in range(2):
                        merged(KD - 1, half)

        x2 = sb("x2", [P, T, D])
        WR = 4
        FIRST = 2
        wdn_first = [a[:, 0:2, :] for a in (yaT, ybT)]
        wgu_in = [sem(f"wgu_in{w}") for w in range(WR)]
        wdn_in = [sem(f"wdn_in{w}") for w in range(WR)]

        def load_gate_up(sp, dst, e, landed):
            sp.dma_start(dst[:, :, 0, :], wg_e[e]).then_inc(landed, 16)
            sp.dma_start(dst[:, :, 1, :], wu_e[e]).then_inc(landed, 16)

        def load_down(sp, dst, e, landed):
            sp.dma_start(dst[:, :, :], wn_e[e]).then_inc(landed, 16)

        with ExitStack() as st:
            woraw = [yaT, ybT]
            woH = sb("woH", [P, KD, D], F32R, ctx=st)
            woL = sb("woL", [P, KD, D], F32R, ctx=st)
            xin = [sb(f"xin2{u}", [P, D], ctx=st) for u in range(2)]
            mH = [sb(f"mH{u}", [P, KD, P], F32R, ctx=st) for u in range(2)]
            mL = [sb(f"mL{u}", [P, KD, P], F32R, ctx=st) for u in range(2)]
            h2 = [sb(f"h2{u}", [P, D], ctx=st) for u in range(2)]
            h2T = sb("h2T", [P, KD, P], ctx=st)
            g2_sb = sb("g2_sb", [P, D], ctx=st)
            wr_sb = sb("wr_sb", [P, KD, NG + NE], ctx=st)
            br_sb = sb("br_sb", [P, NG + NE], ctx=st)
            msq = sb("msq2", [P, 2], ctx=st)
            rstd = sb("rstd2", [P, 2], ctx=st)
            wo_in = [sem(f"wo_in{n}") for n in range(KD // 2)]
            x_in = [sem(f"x2_in{u}") for u in range(2)]
            high_ready = sem("high_ready")
            low_ready = sem("low_ready")
            o_psum2 = sem("out_psum")
            x2_ready = sem("x2_ready")
            msq_ready = sem("msq2_ready")
            rms_ready = sem("rms2_ready")
            rstd_ready = sem("rstd2_ready")
            h2_ready = sem("h2_ready")
            h2_stored = [sem(f"h2_stored{u}") for u in range(2)]
            h2T_psum = sem("h2T_psum")
            h2T_ready = sem("h2T_ready")
            lg_psum = sem("lg_psum")
            lg_ready = sem("lg_ready")
            with nc.Block() as block:
                @block.sync
                def _(sp):
                    for k in range(0, KD, 2):
                        sp.dma_start(woraw[k // 4][:, k % 4:k % 4 + 2, :],
                                     wout[:, k:k + 2, :]).then_inc(wo_in[k // 2], 16)
                        if k < 4:
                            sp.dma_start(xin[k // 2][:], x_t[k // 2]).then_inc(x_in[k // 2], 16)
                    sp.dma_start(wr_sb[:], wr).then_inc(load_small, 16)
                    sp.dma_start(br_sb[:], br.partition_broadcast(P)).then_inc(load_small, 16)
                    sp.dma_start(g2_sb[:], g2p.partition_broadcast(P)).then_inc(load_small, 16)
                    with sp.Fori(1, T // 2) as i:
                        for u in range(2):
                            sp.wait_ge(x2_ready, i * 2 + u + 1)
                            sp.dma_start(xin[u][:], x_t[i * 2 + u]).then_inc(x_in[u], 16)

                @block.tensor
                def _(pe):
                    pe.sem_inc(o_psum2, 2)
                    pe.sem_inc(h2T_psum, 2)

                    def project(t, u, first=False):
                        pe.wait_ge(low_ready, 1 if first else t + KD + 1)
                        pe.wait_ge(x2_ready, t + 1)
                        for n in range(2):
                            for k in range(KD):
                                if first and n == 0:
                                    pe.wait_ge(low_ready, k + 2)
                                for j, (m, w) in enumerate(((mH, woH), (mL, woH), (mH, woL))):
                                    mm = pe.matmul(ps[:, 2 * u + n, :], m[u][:, k, :], w[:, k, n * HALF:(n + 1) * HALF],
                                                   start=(k == 0 and j == 0), stop=(k == KD - 1 and j == 2))
                        mm.then_inc(o_psum2, 1)

                    def transposes_h2(t, u):
                        pe.wait_ge(h2_ready, t + 1)
                        for k in range(KD):
                            mm = pe.transpose(ps[:, 4 + k // 4, (k % 4) * P:(k % 4 + 1) * P],
                                              h2[u][:, k * P:(k + 1) * P], ident[:])
                        mm.then_inc(h2T_psum, 1)

                    def logits(t):
                        pe.wait_ge(h2T_ready, t + 1)
                        pe.wait_ge(lg_ready, t + 1)
                        for k in range(KD):
                            mm = pe.matmul(ps[:, 6, 0:NG + NE], h2T[:, k, :], wr_sb[:, k, :],
                                           start=(k == 0), stop=(k == KD - 1))
                        mm.then_inc(lg_psum, 1)

                    project(0, 0, first=True)
                    project(1, 1)
                    pe.wait_ge(load_small, 64 + 48 + 48)
                    transposes_h2(0, 0)
                    with pe.Fori(1, T // 2) as i:
                        for u in range(2):
                            project(i * 2 + u, u)
                            logits(i * 2 + u - 2)
                            transposes_h2(i * 2 + u - 1, 1 - u)
                    logits(T - 2)
                    transposes_h2(T - 1, 1)
                    logits(T - 1)

                @block.scalar
                def _(act):
                    def high_tile(t, u):
                        act.wait_ge(o_psum2, t + 1)
                        nc.scalar.copy(mH[u][:], mT[:, :, bass.ds(t * P, P)]).then_inc(high_ready, 1)

                    def tile(i, u, ahead):
                        t = i * 2 + u
                        act.wait_ge(x2_ready, t + 3)
                        act.wait_ge(h2_stored[u], i * 16 + 16)
                        act.wait_ge(h2T_psum, t + 1)
                        nc.scalar.activation(h2[u][:], x2[:, bass.ds(t, 1), :].squeeze(1), ACT.Square,
                                             scale=D ** -0.5, accum_out=msq[:, u:u + 1]).then_inc(msq_ready, 1)
                        act.wait_ge(msq_ready, t + 1)
                        nc.scalar.activation(msq[:, u:u + 1], msq[:, u:u + 1], ACT.Sqrt,
                                             bias=eps_sb[:]).then_inc(rms_ready, 1)
                        if ahead:
                            high_tile(t + 2, u)
                        act.wait_ge(h2_ready, t + 1)
                        act.dma_start(h2_t[t], h2[u][:]).then_inc(h2_stored[u], 16)
                        act.wait_ge(h2T_psum, t + 3)
                        nc.scalar.copy(h2T[:].rearrange("p k c -> p (k c)"), two(4)).then_inc(h2T_ready, 1)

                    high_tile(0, 0)
                    for k in range(KD):
                        act.wait_ge(wo_in[k // 2], 16)
                        nc.scalar.copy(woH[:, k, :], woraw[k // 4][:, k % 4, :]).then_inc(high_ready, 1)
                    high_tile(1, 1)
                    with act.Fori(0, T // 2 - 1) as i:
                        for u in range(2):
                            tile(i, u, True)
                    for u in range(2):
                        tile(T // 2 - 1, u, False)
                    for u in range(2):
                        act.wait_ge(h2_stored[u], 16 + 16 * (T // 2))

                @block.vector
                def _(dve):
                    dve.sem_inc(x2_ready, 2)
                    dve.sem_inc(lg_ready, 1)
                    for u in range(2):
                        dve.sem_inc(h2_stored[u], 16)

                    def residual(t, u, n):
                        dve.wait_ge(o_psum2, t + 3)
                        dve.wait_ge(x_in[u], n * 16)
                        nc.vector.tensor_tensor(x2[:, t, :], two(2 * u), xin[u][:], ALU.add).then_inc(x2_ready, 1)

                    def normalise(t, u, n):
                        dve.wait_ge(rms_ready, t + 1)
                        nc.vector.reciprocal(rstd[:, u:u + 1], msq[:, u:u + 1]).then_inc(rstd_ready, 1)
                        dve.wait_ge(rstd_ready, t + 1)
                        dve.wait_ge(h2_stored[u], n * 16)
                        dve.wait_ge(h2T_psum, t + 1)
                        nc.vector.scalar_tensor_tensor(
                            out=h2[u][:].rearrange("q (k p) -> q k p", k=KD),
                            in0=x2[:, t, :].rearrange("q (p k) -> q k p", k=KD), scalar=rstd[:, u:u + 1],
                            in1=g2_sb[:].rearrange("q (k p) -> q k p", k=KD),
                            op0=ALU.mult, op1=ALU.mult).then_inc(h2_ready, 1)

                    def take_logits(t):
                        dve.wait_ge(lg_psum, t + 1)
                        nc.vector.tensor_tensor(lgt[:, t, :], ps[:, 6, 0:NG + NE], br_sb[:],
                                                ALU.add).then_inc(lg_ready, 1)

                    def low_tile(t, u, n):
                        dve.wait_ge(high_ready, n)
                        nc.vector.tensor_tensor(mL[u][:], mT[:, :, bass.ds(t * P, P)], mH[u][:].bitcast(F32),
                                                ALU.subtract).then_inc(low_ready, 1)

                    def tile(i, u):
                        residual(i * 2 + u, u, i + 1)
                        normalise(i * 2 + u, u, i + 1)

                    low_tile(0, 0, 1)
                    for k in range(KD):
                        dve.wait_ge(high_ready, k + 2)
                        nc.vector.tensor_tensor(woL[:, k, :], woraw[k // 4][:, k % 4, :], woH[:, k, :].bitcast(F32),
                                                ALU.subtract).then_inc(low_ready, 1)
                    low_tile(1, 1, KD + 2)
                    dve.wait_ge(load_small, 64 + 48 + 48)
                    for u in range(2):
                        tile(0, u)
                        low_tile(u + 2, u, u + KD + 3)
                    with dve.Fori(1, T // 2 - 1) as i:
                        for u in range(2):
                            t = i * 2 + u
                            tile(i, u)
                            low_tile(t + 2, u, t + KD + 3)
                            take_logits(t - 2)
                    for u in range(2):
                        tile(T // 2 - 1, u)
                        take_logits(T - 4 + u)
                    for t in range(T - 2, T):
                        take_logits(t)

        wgu_first = [sb(f"wgu{e}", [P, KD, 2, DE]) for e in range(FIRST)]
        slot_id = sb("slot_id", [P, TILES], I32)
        row_id = sb("row_id", [P, TILES], I32)
        e_w = sb("e_w", [P, 2, T])
        over_e = sb("over_e", [P, MAX_OVER], I32)
        n_over = sb("n_over", [P, 1], I32)
        with ExitStack() as st:
            def f(name, shape, dt=F32):
                return sb("r_" + name, shape, dt, ctx=st)
            iot = f("iot", [P, P], I32)
            io = f("io", [P, P])
            row1_i = f("row1_i", [P, 2, T], I32)
            row1 = f("row1", [P, 2, T])
            rv4, rv8 = f("rv4", [P, NG]), f("rv8", [P, EPG])
            thr = f("thr", [P, T - 1])
            gmax, gex, gsum, gtop = f("gmax", [P, T]), f("gex", [P, T, NG]), f("gsum", [P, T]), f("gtop", [P, T])
            cand4, goh = f("cand4", [P, T, NG]), f("goh", [P, T, NG])
            r1 = f("r1", [P, T])
            prod = f("prod", [P, T, NG, EPG])
            es = [f("es0", [P, T, EPG]), f("es1", [P, T, EPG])]
            em = f("em", [P, 2, T])
            cand8 = f("cand8", [P, T, EPG])
            oh = [f("oh0", [P, T, EPG]), f("oh1", [P, T, EPG])]
            dif, ex, den = f("dif", [P, T]), f("ex", [P, T]), f("den", [P, T])
            M = [f("M0", [P, T, NE]), f("M1", [P, T, NE])]
            Ms, Mp = f("Ms", [P, T, NE]), f("Mp", [P, T, NE])
            tot, totT, novT = f("tot", [P, NE]), f("totT", [NE, 1]), f("novT", [NE, 1])
            cmp7 = f("cmp7", [NE, T - 1])
            novB = f("novB", [NE, P])
            incl = f("incl", [NE, 2, NE])
            off = f("off", [P, 2, NE])
            cmpo = f("cmpo", [P, MAX_OVER, NE])
            eid = f("eid", [P, MAX_OVER])
            pr32 = f("pr32", [P, T, NE])
            rank, ea, eb2 = f("rank", [P, 2, T]), f("ea", [P, 2, T]), f("eb", [P, 2, T])
            cmpr = f("cmpr", [P, 2, T, T - 1])
            mt, isov, tile_, slot = f("mt", [P, 2, T]), f("isov", [P, 2, T]), f("tile", [P, 2, T]), f("slot", [P, 2, T])
            R = f("R", [P, 2, T, P])
            O = f("O", [P, 2, T, TILES])
            lst, emp, row = f("lst", [P, TILES]), f("emp", [P, TILES]), f("row", [P, TILES])
            second = f("second", [P, TILES])
            r_iota = sem("r_iota")
            r_dve = sem("r_dve")
            r_act = sem("r_act")
            r_psum = sem("r_psum")
            need_exp = sem("need_exp")
            need_tot = sem("need_tot")
            need_off = sem("need_off")
            need_slots = sem("need_slots")

            def last(a, n):
                return a.unsqueeze(len(a.shape)).broadcast_to(list(a.shape) + [n])

            with nc.Block() as block:
                @block.sync
                def _(sp):
                    for e in range(FIRST):
                        load_gate_up(sp, wgu_first[e], e, wgu_in[e])
                        load_down(sp, wdn_first[e], e, wdn_in[e])

                @block.gpsimd
                def _(pool):
                    nc.gpsimd.iota(iot[:], pattern=[[1, P]], base=0, channel_multiplier=0).then_inc(r_iota, 1)
                    nc.gpsimd.iota(row1_i[:], pattern=[[SEQ, 2], [P, T]], base=1, channel_multiplier=1).then_inc(r_iota, 1)

                @block.scalar
                def _(act):
                    act.wait_ge(need_exp, 1)
                    nc.scalar.activation(gex[:], cand4[:], ACT.Exp).then_inc(r_act, 1)
                    nc.scalar.activation(ex[:], dif[:], ACT.Exp).then_inc(r_act, 1)

                @block.tensor
                def _(pe):
                    pe.wait_ge(need_tot, 1)
                    rk = ps[:, 0, 0:T * NE]
                    pe.matmul(rk, before[:], Ms[:].rearrange("p t e -> p (t e)"), start=True, stop=False)
                    pe.matmul(rk, ones[:], Mp[:].rearrange("p t e -> p (t e)"), start=False, stop=True)
                    pe.matmul(ps[0:NE, 1, 0:1], tot[:], ones[:, 0:1], start=True, stop=True).then_inc(r_psum, 1)
                    pe.wait_ge(need_off, 1)
                    pe.matmul(ps[:, 2, 0:2 * NE], novB[:], incl[:].rearrange("p a e -> p (a e)"),
                              start=True, stop=True).then_inc(r_psum, 1)
                    for n in range(2 * T):
                        if n % T == 0:
                            pe.wait_ge(need_slots, 2 * (n // T) + 2)
                        mm = pe.matmul(ps[:, 3, 0:TILES], R[:, n // T, n % T, :], O[:, n // T, n % T, :],
                                       start=(n == 0), stop=(n == 2 * T - 1))
                    mm.then_inc(r_psum, 1)

                @block.vector
                def _(dve):
                    link = Chain(dve, r_dve)
                    v = nc.vector
                    dve.wait_ge(r_iota, 2)
                    link(v.tensor_copy(io[:], iot[:]))
                    link(v.tensor_copy(row1[:], row1_i[:]))
                    link(v.tensor_scalar(rv4[:], io[:, 0:NG], -1.0, float(NG), ALU.mult, ALU.add))
                    link(v.tensor_scalar(rv8[:], io[:, 0:EPG], -1.0, float(EPG), ALU.mult, ALU.add))
                    link(v.tensor_scalar(thr[:], io[:, 0:T - 1], 1.0, float(P), ALU.add, ALU.mult))
                    gl_ = lgt[:, :, 0:NG]
                    el_ = lgt[:, :, NG:].rearrange("p t (g e) -> p t g e", g=NG)
                    link(v.tensor_reduce(gmax[:], gl_, AX.X, ALU.max))
                    link(v.tensor_tensor(goh[:], gl_, last(gmax[:], NG), ALU.is_equal))
                    link(v.tensor_tensor(goh[:], goh[:], rv4[:].unsqueeze(1).broadcast_to([P, T, NG]), ALU.mult))
                    link(v.tensor_reduce(r1[:], goh[:], AX.X, ALU.max))
                    link(v.tensor_tensor(goh[:], goh[:], last(r1[:], NG), ALU.is_equal))
                    link(v.tensor_tensor(cand4[:], gl_, last(gmax[:], NG), ALU.subtract))
                    link(v.tensor_tensor(prod[:], el_, last(goh[:], EPG), ALU.mult))
                    link(v.tensor_reduce(es[0][:], prod[:].rearrange("p t g e -> p t e g"), AX.X, ALU.add))
                    for c in range(2):
                        link(v.tensor_reduce(em[:, c, :], es[c][:], AX.X, ALU.max))
                        link(v.tensor_tensor(cand8[:], es[c][:], last(em[:, c, :], EPG), ALU.is_equal))
                        link(v.tensor_tensor(cand8[:], cand8[:], rv8[:].unsqueeze(1).broadcast_to([P, T, EPG]),
                                             ALU.mult))
                        link(v.tensor_reduce(r1[:], cand8[:], AX.X, ALU.max))
                        link(v.tensor_tensor(oh[c][:], cand8[:], last(r1[:], EPG), ALU.is_equal))
                        if c == 0:
                            link(v.scalar_tensor_tensor(out=es[1][:], in0=oh[0][:], scalar=-3e38, in1=es[0][:],
                                                        op0=ALU.mult, op1=ALU.add))
                    v.tensor_tensor(dif[:], em[:, 1, :], em[:, 0, :], ALU.subtract).then_inc(need_exp, 1)
                    for c in range(2):
                        link(v.tensor_tensor(M[c][:].rearrange("p t (g e) -> p t g e", g=NG), last(goh[:], EPG),
                                             oh[c][:].unsqueeze(2).broadcast_to([P, T, NG, EPG]), ALU.mult))
                    link(v.tensor_tensor(Ms[:], M[0][:], M[1][:], ALU.add))
                    link(v.memset(Mp[:, 0, :], 0.0))
                    for t in range(1, T):
                        link(v.tensor_tensor(Mp[:, t, :], Mp[:, t - 1, :], Ms[:, t - 1, :], ALU.add))
                    v.tensor_tensor(tot[:], Mp[:, T - 1, :], Ms[:, T - 1, :], ALU.add).then_inc(need_tot, 1)
                    link(v.tensor_copy(incl[:, 0, :], before[0:NE, 0:NE]))
                    link(v.tensor_tensor(incl[:, 1, :], before[0:NE, 0:NE], ident[0:NE, 0:NE], ALU.add))
                    dve.wait_ge(r_act, 2)
                    link(v.tensor_reduce(gsum[:], gex[:], AX.X, ALU.add))
                    link(v.reciprocal(gtop[:], gsum[:]))
                    link(v.tensor_scalar(den[:], ex[:], 1.0, None, ALU.add))
                    link(v.reciprocal(den[:], den[:]))
                    link(v.tensor_tensor(e_w[:, 0, :], den[:], gtop[:], ALU.mult))
                    link(v.tensor_tensor(e_w[:, 1, :], e_w[:, 0, :], ex[:], ALU.mult))
                    dve.wait_ge(r_psum, 1)
                    link(v.tensor_copy(totT[:], ps[0:NE, 1, 0:1]))
                    link(v.tensor_scalar(cmp7[:], thr[0:NE, :], totT[:, 0:1], None, ALU.is_lt))
                    link(v.tensor_reduce(novT[:], cmp7[:], AX.X, ALU.add))
                    v.tensor_scalar(novB[:], ones[0:NE, :], novT[:, 0:1], None, ALU.mult).then_inc(need_off, 1)
                    rk = ps[:, 0, 0:T * NE].rearrange("p (t e) -> p t e", e=NE)
                    for c in range(2):
                        link(v.tensor_tensor(pr32[:], M[c][:], rk, ALU.mult))
                        link(v.tensor_reduce(rank[:, c, :], pr32[:], AX.X, ALU.add))
                        link(v.tensor_tensor(pr32[:], M[c][:], io[:, 0:NE].unsqueeze(1).broadcast_to([P, T, NE]),
                                             ALU.mult))
                        link(v.tensor_reduce(ea[:, c, :], pr32[:], AX.X, ALU.add))
                    dve.wait_ge(r_psum, 2)
                    link(v.tensor_copy(off[:].rearrange("p a e -> p (a e)"), ps[:, 2, 0:2 * NE]))
                    for c in range(2):
                        link(v.tensor_tensor(pr32[:], M[c][:], off[:, 0:1, :].broadcast_to([P, T, NE]), ALU.mult))
                        link(v.tensor_reduce(eb2[:, c, :], pr32[:], AX.X, ALU.add))
                    link(v.tensor_copy(n_over[:], off[:, 1, NE - 1:NE]))
                    link(v.tensor_tensor(cmpo[:], off[:, 1:2, :].broadcast_to([P, MAX_OVER, NE]),
                                         last(io[:, 0:MAX_OVER], NE), ALU.is_le))
                    link(v.tensor_reduce(eid[:], cmpo[:], AX.X, ALU.add))
                    link(v.tensor_scalar(over_e[:], eid[:], float(NE - 1), None, ALU.min))
                    link(v.tensor_tensor(cmpr[:], last(rank[:], T - 1),
                                         thr[:].unsqueeze(1).unsqueeze(1).broadcast_to([P, 2, T, T - 1]), ALU.is_ge))
                    link(v.tensor_reduce(mt[:], cmpr[:], AX.X, ALU.add))
                    link(v.tensor_scalar(isov[:], mt[:], 0.0, None, ALU.is_gt))
                    link(v.tensor_tensor(eb2[:], eb2[:], mt[:], ALU.add))
                    link(v.tensor_tensor(eb2[:], eb2[:], ea[:], ALU.subtract))
                    link(v.scalar_tensor_tensor(out=eb2[:], in0=eb2[:], scalar=float(NE - 1), in1=isov[:],
                                                op0=ALU.add, op1=ALU.mult))
                    link(v.tensor_tensor(tile_[:], ea[:], eb2[:], ALU.add))
                    link(v.scalar_tensor_tensor(out=slot[:], in0=mt[:], scalar=-float(P), in1=rank[:],
                                                op0=ALU.mult, op1=ALU.add))
                    for c in range(2):
                        v.tensor_tensor(R[:, c, :, :], io[:].unsqueeze(1).broadcast_to([P, T, P]),
                                        last(slot[:, c, :], P), ALU.is_equal).then_inc(need_slots, 1)
                        link(v.tensor_tensor(O[:, c, :, :], io[:, 0:TILES].unsqueeze(1).broadcast_to([P, T, TILES]),
                                             last(tile_[:, c, :], TILES), ALU.is_equal))
                        v.tensor_tensor(O[:, c, :, :], O[:, c, :, :], last(row1[:, c, :], TILES),
                                        ALU.mult).then_inc(need_slots, 1)
                    dve.wait_ge(r_psum, 3)
                    link(v.tensor_copy(lst[:], ps[:, 3, 0:TILES]))
                    link(v.tensor_scalar(emp[:], lst[:], 0.0, 8.0 * SEQ, ALU.is_equal, ALU.mult))
                    link(v.scalar_tensor_tensor(out=row[:], in0=lst[:], scalar=-1.0, in1=emp[:],
                                                op0=ALU.add, op1=ALU.add))
                    link(v.tensor_copy(row_id[:], row[:]))
                    link(v.tensor_scalar(second[:], row[:], float(SEQ), None, ALU.is_ge))
                    link(v.scalar_tensor_tensor(out=slot_id[:], in0=second[:], scalar=-float(SEQ), in1=row[:],
                                                op0=ALU.mult, op1=ALU.add))

        with ExitStack() as st:
            wgu = wgu_first + [hT[:, e * 4:(e + 1) * 4, :].rearrange("p a (b c f) -> p (a b) c f", b=2, c=2)
                               for e in range(2)]
            wdn = wdn_first + [sb(f"wdn{u}", [P, 2, D], ctx=st) for u in range(2)]
            idx = [sb(f"idx{w}", [P, 1], I32, ctx=st) for w in range(WR)]
            idy = [sb(f"idy{w}", [P, 1], I32, ctx=st) for w in range(WR)]
            hg = [yaT[:, 2 + w, :] for w in range(2)] + [sb(f"hg{w}", [P, D], ctx=st) for w in range(2)]
            hgT = [sb(f"hgT{u}", [P, KD, P], ctx=st) for u in range(2)]
            sg = [sb(f"esg{u}", [P, DE], ctx=st) for u in range(2)]
            sil = sb("sil", [P, DE], ctx=st)
            av = [sb(f"av{u}", [P, 2, P], ctx=st) for u in range(2)]
            avT = [sb(f"avT{u}", [P, 2, P], ctx=st) for u in range(2)]
            ys = [ybT[:, 2 + w, :] for w in range(2)] + [sb(f"ys{w}", [P, D], ctx=st) for w in range(2)]
            hg_clear = sem("hg_clear")
            idx_ready = sem("idx_ready")
            idy_ready = sem("idy_ready")
            hg_in = [sem(f"hg_in{w}") for w in range(WR)]
            hgT_psum = sem("hgT_psum")
            hgT_ready = sem("hgT_ready")
            gu_psum = sem("gu_psum")
            esg_ready = sem("esg_ready")
            sil_ready = sem("sil_ready")
            av_ready = sem("av_ready")
            avT_psum = sem("avT_psum")
            avT_ready = sem("avT_ready")
            y_psum = sem("y_psum")
            ys_ready = sem("ys_ready")
            ys_stored = [sem(f"ys_stored{w}") for w in range(WR)]
            ys_free = sem("ys_free")
            o_w_in = sem("o_w_in")
            o_idx = sem("o_idx")
            o_idy = sem("o_idy")
            o_hg_in = sem("o_hg_in")
            o_pe = sem("o_pe")
            o_act = sem("o_act")
            o_dve = sem("o_dve")
            o_stored = sem("o_stored")
            o_free = sem("o_free")

            def transposes(pe, src, pieces, dst):
                for k in range(pieces):
                    mm = pe.transpose(dst[:, k * P:(k + 1) * P], src[:, k * P:(k + 1) * P], ident[:])
                return mm

            def gate_up(pe, u, w, bank):
                for k in range(KD):
                    mm = pe.matmul(ps[:, bank, :], hgT[u][:, k, :], wgu[w][:, k, :, :].rearrange("p a f -> p (a f)"),
                                   start=(k == 0), stop=(k == KD - 1))
                return mm

            def down(pe, u, w):
                for n in range(2):
                    for c in range(2):
                        mm = pe.matmul(ps[:, 5 + n, :], avT[u][:, c, :], wdn[w][:, c, n * HALF:(n + 1) * HALF],
                                       start=(c == 0), stop=(c == 1))
                return mm

            def act_order(a):
                return a.rearrange("q (p c) -> q c p", c=2)

            av2 = [a[:].rearrange("p c f -> p (c f)") for a in av]
            avT2 = [a[:].rearrange("p c f -> p (c f)") for a in avT]
            with nc.Block() as block:
                @block.sync
                def _(sp):
                    for w in range(WR):
                        sp.wait_ge(hg_in[w], 16)
                    for e in range(FIRST, WR):
                        load_gate_up(sp, wgu[e], e, wgu_in[e])
                        load_down(sp, wdn[e], e, wdn_in[e])
                    with sp.Fori(1, NE // WR) as i:
                        for u in range(WR):
                            e = i * WR + u
                            sp.wait_ge(gu_psum, e + 1)
                            load_gate_up(sp, wgu[u], e, wgu_in[u])
                            sp.wait_ge(y_psum, e + 1)
                            load_down(sp, wdn[u], e, wdn_in[u])
                    over = sp.value_load(n_over[0:1, 0:1], min_val=0, max_val=MAX_OVER)
                    sp.wait_ge(y_psum, NE + 1)
                    with sp.Fori(0, MAX_OVER) as o:
                        with sp.If(o < over):
                            sp.wait_ge(o_pe, o * 4 + 4)
                            apart(sp)
                            e = sp.value_load(over_e[0:1, bass.ds(o, 1)], min_val=0, max_val=NE - 1)
                            load_gate_up(sp, wgu[0], e, o_w_in)
                            load_down(sp, wdn[0], e, o_w_in)
                            sp.nop()

                @block.gpsimd
                def _(pool):
                    pool.wait_ge(hg_clear, WR)

                    def gather(t, w, n):
                        nc.gpsimd.tensor_copy(idx[w][:], slot_id[:, bass.ds(t, 1)]).then_inc(idx_ready, 1)
                        pool.wait_ge(idx_ready, n)
                        apart(pool)
                        nc.gpsimd.indirect_dma_start(
                            hg[w][:], None, h2_dram, bass.IndirectOffsetOnAxis(ap=idx[w][:, 0:1].bitcast(U32), axis=0),
                            bounds_check=SEQ - 1, oob_is_err=False).then_inc(hg_in[w], 16)

                    def scatter(t, w, ready, n, stored):
                        nc.gpsimd.tensor_copy(idy[w][:], row_id[:, bass.ds(t, 1)]).then_inc(ready, 1)
                        pool.wait_ge(ready, n)
                        apart(pool)
                        nc.gpsimd.indirect_dma_start(
                            y_dram, bass.IndirectOffsetOnAxis(ap=idy[w][:, 0:1].bitcast(U32), axis=0), ys[w][:], None,
                            bounds_check=2 * SEQ - 1, oob_is_err=False).then_inc(stored, 16)

                    def stored(w, n):
                        pool.wait_ge(ys_stored[w], n * 16)
                        pool.sem_inc(ys_free, 1)

                    def step(i, w):
                        t = i * WR + w
                        pool.wait_ge(hgT_psum, t + 3)
                        gather(t + WR, w, t + WR + 1)
                        pool.wait_ge(ys_ready, t + 2)
                        scatter(t, w, idy_ready, t + 1, ys_stored[w])

                    for w in range(WR):
                        gather(w, w, w + 1)
                    step(0, 0)
                    for w in range(1, WR):
                        step(0, w)
                        stored(w - 1, 1)
                    with pool.Fori(1, NE // WR) as i:
                        step(i, 0)
                        stored(WR - 1, i)
                        for w in range(1, WR):
                            step(i, w)
                            stored(w - 1, i + 1)
                    stored(WR - 1, NE // WR)
                    over = pool.value_load(n_over[0:1, 0:1], min_val=0, max_val=MAX_OVER)
                    for w in range(WR):
                        pool.wait_ge(hg_in[w], (NE // WR + 1) * 16)
                    pool.wait_ge(hgT_psum, NE + 3)
                    with pool.Fori(0, MAX_OVER) as o:
                        with pool.If(o < over):
                            pool.wait_ge(o_pe, o * 4 + 4)
                            nc.gpsimd.tensor_copy(idx[0][:], slot_id[:, bass.ds(o + NE, 1)]).then_inc(o_idx, 1)
                            pool.wait_ge(o_idx, o + 1)
                            apart(pool)
                            nc.gpsimd.indirect_dma_start(
                                hg[0][:], None, h2_dram,
                                bass.IndirectOffsetOnAxis(ap=idx[0][:, 0:1].bitcast(U32), axis=0),
                                bounds_check=SEQ - 1, oob_is_err=False).then_inc(o_hg_in, 16)
                            pool.wait_ge(o_dve, o * 5 + 5)
                            scatter(o + NE, 0, o_idy, o + 1, o_stored)
                            pool.wait_ge(o_stored, o * 16 + 16)
                            pool.sem_inc(o_free, 1)

                @block.tensor
                def _(pe):
                    pe.sem_inc(hgT_psum, 2)
                    pe.sem_inc(gu_psum, WR)
                    pe.sem_inc(y_psum, WR)
                    pe.sem_inc(o_pe, 4)

                    def gathered_transposes(t, w, n):
                        pe.wait_ge(hg_in[w], n * 16)
                        pe.wait_ge(hgT_ready, t + 1)
                        transposes(pe, hg[w], KD, two(0)).then_inc(hgT_psum, 1)

                    def first_half(t, w, n):
                        u = w % 2
                        pe.wait_ge(wgu_in[w], n * 32)
                        pe.wait_ge(hgT_ready, t + 2)
                        pe.wait_ge(av_ready, t + 1)
                        gate_up(pe, u, w, 2 + u).then_inc(gu_psum, 1)

                    def hidden_transposes(t, u):
                        pe.wait_ge(av_ready, t + 3)
                        pe.wait_ge(avT_ready, t + 1)
                        transposes(pe, av2[u], 2, ps[:, 4 + 3 * u, 0:2 * P]).then_inc(avT_psum, 1)

                    def second_half(t, w, n):
                        u = w % 2
                        pe.wait_ge(avT_ready, t + 3)
                        pe.wait_ge(wdn_in[w], n * 16)
                        pe.wait_ge(ys_ready, t + 1)
                        down(pe, u, w).then_inc(y_psum, 1)

                    def step(i, w):
                        t, u = i * WR + w, w % 2
                        first_half(t, w, i + 1)
                        if w > 0:
                            before_w, before_n = w - 1, i + 1
                        else:
                            before_w, before_n = WR - 1, i
                        hidden_transposes(t - 1, 1 - u)
                        gathered_transposes(t + 1, (w + 1) % WR, i + 1 + (w + 1) // WR)
                        second_half(t - 1, before_w, before_n)

                    gathered_transposes(0, 0, 1)
                    first_half(0, 0, 1)
                    gathered_transposes(1, 1, 1)
                    for w in range(1, WR):
                        step(0, w)
                    with pe.Fori(1, NE // WR) as i:
                        for w in range(WR):
                            step(i, w)
                    hidden_transposes(NE - 1, 1)
                    second_half(NE - 1, WR - 1, NE // WR)
                    over = pe.value_load(n_over[0:1, 0:1], min_val=0, max_val=MAX_OVER)
                    pe.wait_ge(ys_ready, NE + 1)
                    pe.wait_ge(hgT_ready, NE + 2)
                    with pe.Fori(0, MAX_OVER) as o:
                        with pe.If(o < over):
                            pe.wait_ge(o_hg_in, o * 16 + 16)
                            transposes(pe, hg[0], KD, two(0)).then_inc(o_pe, 1)
                            pe.wait_ge(o_w_in, o * 48 + 48)
                            pe.wait_ge(o_dve, o * 5 + 1)
                            gate_up(pe, 0, 0, 2).then_inc(o_pe, 1)
                            pe.wait_ge(o_dve, o * 5 + 3)
                            transposes(pe, av2[0], 2, ps[:, 4, 0:2 * P]).then_inc(o_pe, 1)
                            pe.wait_ge(o_dve, o * 5 + 4)
                            down(pe, 0, 0).then_inc(o_pe, 1)
                            pe.nop()

                @block.scalar
                def _(act):
                    act.sem_inc(hgT_ready, 1)
                    act.wait_ge(hgT_psum, 3)
                    nc.scalar.copy(hgT[0][:].rearrange("p k c -> p (k c)"), two(0)).then_inc(hgT_ready, 1)
                    with act.Fori(0, NE // 2) as i:
                        for u in range(2):
                            t = i * 2 + u
                            act.wait_ge(gu_psum, t + 1 + WR)
                            act.wait_ge(av_ready, t + 1)
                            nc.scalar.activation(sg[u][:], ps[:, 2 + u, 0:DE], ACT.Sigmoid).then_inc(esg_ready, 1)
                            act.wait_ge(hgT_psum, t + 4)
                            nc.scalar.copy(hgT[1 - u][:].rearrange("p k c -> p (k c)"), two(0)).then_inc(hgT_ready, 1)
                    over = act.value_load(n_over[0:1, 0:1], min_val=0, max_val=MAX_OVER)
                    with act.Fori(0, MAX_OVER) as o:
                        with act.If(o < over):
                            act.wait_ge(o_pe, o * 4 + 6)
                            nc.scalar.activation(sg[0][:], ps[:, 2, 0:DE], ACT.Sigmoid).then_inc(o_act, 1)
                            act.nop()

                @block.vector
                def _(dve):
                    dve.sem_inc(av_ready, 2)
                    dve.sem_inc(avT_ready, 2)
                    dve.sem_inc(ys_ready, 1)
                    dve.sem_inc(ys_free, WR)
                    for w in range(WR):
                        nc.vector.memset(hg[w][:], 0.0).then_inc(hg_clear, 1)
                    dve.sem_inc(o_free, 1)
                    with dve.Fori(0, NE // WR) as i:
                        for w in range(WR):
                            t, u = i * WR + w, w % 2
                            dve.wait_ge(esg_ready, t + 1)
                            nc.vector.tensor_tensor(sil[:], ps[:, 2 + u, 0:DE], sg[u][:],
                                                    ALU.mult).then_inc(sil_ready, 1)
                            dve.wait_ge(sil_ready, t + 1)
                            nc.vector.tensor_tensor(av[u][:], act_order(sil[:]), act_order(ps[:, 2 + u, DE:2 * DE]),
                                                    ALU.mult).then_inc(av_ready, 1)
                            dve.wait_ge(avT_psum, t + 1)
                            nc.vector.tensor_copy(avT2[u], ps[:, 4 + 3 * u, 0:2 * P]).then_inc(avT_ready, 1)
                            dve.wait_ge(y_psum, t + 1 + WR)
                            dve.wait_ge(ys_free, t + 1)
                            nc.vector.tensor_copy(ys[w][:], two(5)).then_inc(ys_ready, 1)
                    over = dve.value_load(n_over[0:1, 0:1], min_val=0, max_val=MAX_OVER)
                    dve.wait_ge(ys_free, NE + WR)
                    with dve.Fori(0, MAX_OVER) as o:
                        with dve.If(o < over):
                            link = Chain(dve, o_dve, o * 5)
                            dve.wait_ge(o_pe, o * 4 + 5)
                            link(nc.vector.tensor_copy(hgT[0][:].rearrange("p k c -> p (k c)"), two(0)))
                            dve.wait_ge(o_act, o + 1)
                            link(nc.vector.tensor_tensor(sil[:], ps[:, 2, 0:DE], sg[0][:], ALU.mult))
                            link(nc.vector.tensor_tensor(av[0][:], act_order(sil[:]), act_order(ps[:, 2, DE:2 * DE]),
                                                         ALU.mult))
                            dve.wait_ge(o_pe, o * 4 + 7)
                            link(nc.vector.tensor_copy(avT2[0], ps[:, 4, 0:2 * P]))
                            dve.wait_ge(o_pe, o * 4 + 8)
                            dve.wait_ge(o_free, o + 1)
                            link(nc.vector.tensor_copy(ys[0][:], two(5)))
                            apart(dve)

        with ExitStack() as st:
            yc = [[sb(f"yc{c}{u}", [P, D], ctx=st) for u in range(2)] for c in range(2)]
            yc_in = [sem(f"yc_in{u}") for u in range(2)]
            first_added = sem("first_added")
            both_added = sem("both_added")
            out_stored = sem("out_stored")
            with nc.Block() as block:
                @block.scalar
                def _(act):
                    with act.Fori(0, T // 2) as i:
                        for u in range(2):
                            act.wait_ge(both_added, i * 2 + u + 1)
                            for c in range(2):
                                act.dma_start(yc[c][u][:], y_t[i * 2 + u + c * T]).then_inc(yc_in[u], 16)

                @block.vector
                def _(dve):
                    dve.sem_inc(both_added, 2)
                    with dve.Fori(0, T // 2) as i:
                        for u in range(2):
                            t = i * 2 + u
                            dve.wait_ge(yc_in[u], i * 32 + 32)
                            nc.vector.scalar_tensor_tensor(out=x2[:, t, :], in0=yc[0][u][:],
                                                           scalar=e_w[:, 0, bass.ds(t, 1)], in1=x2[:, t, :],
                                                           op0=ALU.mult, op1=ALU.add).then_inc(first_added, 1)
                            dve.wait_ge(first_added, t + 1)
                            nc.vector.scalar_tensor_tensor(out=x2[:, t, :], in0=yc[1][u][:],
                                                           scalar=e_w[:, 1, bass.ds(t, 1)], in1=x2[:, t, :],
                                                           op0=ALU.mult, op1=ALU.add).then_inc(both_added, 1)

                @block.sync
                def _(sp):
                    with sp.Fori(0, T) as t:
                        sp.wait_ge(both_added, t + 3)
                        sp.dma_start(out_t[t], x2[:, t, :]).then_inc(out_stored, 16)
                    sp.wait_ge(out_stored, 16 * T)


def kernel(**inputs):
    import numpy as np
    import concourse.bacc as bacc
    from concourse import mybir as my
    from concourse.bass_utils import run_bass_kernel_spmd

    a = {k: np.asarray(v) for k, v in inputs.items()}
    w_in = a["w_in"][0]

    def rows(w):
        return w.reshape(-1, P, w.shape[1]).transpose(1, 0, 2)

    def cols(v):
        return v.reshape(-1, P).T

    o = [0, 512, 1024, 1536, 1792, 2048, 2560, 3072, 3088, 5136]
    part = [w_in[:, o[n]:o[n + 1]] for n in range(9)]
    aq, ak, av, bq, bk, bv, brr, lr, gates = part
    pairs = [(aq, ak, n) for n in range(A_PAIRS)] + [(bq, bk, n) for n in range(B_PAIRS)]
    blk = lambda w, n: w[:, n * P:(n + 1) * P]
    wqk = np.stack([rows(np.concatenate([blk(q, n), blk(k, n)], 1)) for q, k, n in pairs])
    flat = lambda w: rows(w).reshape(P, -1)
    wd = np.stack([np.concatenate([flat(blk(gates, n)), flat(blk(gates, KD + n)), flat(blk(a["proj_a"][0], n)),
                                   flat(blk(a["proj_b"][0], n))], 1) for n in range(KD)])
    rel = a["rel_bias"]
    at = np.clip(5 * P + np.arange(P)[:, None] - np.arange(BANDW)[None, :], 0, 2 * P)
    relx = rel[at].transpose(2, 0, 1).reshape(A_PAIRS, 2, P, BANDW).transpose(0, 2, 1, 3)
    turned = lambda w: w.reshape(P, KD, -1)
    arrays = {
        "x": a["x"][0], "g1": cols(a["norm_mix_gain"][0]), "wv": rows(np.concatenate([av, bv, brr], 1)),
        "wqk": wqk, "wlr": rows(lr), "wd": wd, "wout": rows(a["w_out"][0]),
        "qg": cols(a["a_q_gain"][0].reshape(-1)), "kg": cols(a["a_k_gain"][0].reshape(-1)),
        "bog": cols(a["b_out_gain"][0].reshape(-1)), "gup": a["b_gate_up"][0], "gbias": a["b_gate_bias"],
        "relx": relx, "g2p": a["norm_ffn_gain"][0].reshape(P, KD).T.reshape(-1),
        "wr": turned(np.concatenate([a["w_group"][0], a["w_router"][0]], 1)),
        "br": np.concatenate([a["b_group"][0], a["b_router"][0]]),
        "w_gate": a["w_gate"][0], "w_up": a["w_up"][0], "w_down": a["w_down"][0],
    }
    nc = bacc.Bacc("TRN2", target_bir_lowering=False, num_devices=1)
    arrays = {f"in_{n}": np.ascontiguousarray(v) for n, v in arrays.items()}
    args = [nc.dram_tensor(n, v.shape, my.dt.from_np(v.dtype), kind="ExternalInput").ap() for n, v in arrays.items()]
    args.append(nc.dram_tensor("out_0", (SEQ, D), F32, kind="ExternalOutput").ap())
    args.append(nc.dram_tensor("h2_rows", (SEQ, D), F32, kind="Internal").ap())
    args.append(nc.dram_tensor("y_rows", (2 * SEQ, D), F32, kind="Internal").ap())
    layer_kernel(nc, *args)
    r = run_bass_kernel_spmd(nc, [arrays], core_ids=[0])
    return np.asarray(r.results[0]["out_0"]).reshape(1, SEQ, D)
```
